# Optimizing a Trainium2 kernel written in Bass

```python
import math
import jax, jax.numpy as jnp
from jax import lax
import numpy as np

D_MODEL = 1024
BATCH = 1
SEQ = 256
DEPTH = 1

D_SSM = D_MODEL // 2
SSM_GROUP = 16
N_SSM_GROUPS = D_SSM // SSM_GROUP
SSM_STATE = 64
DT_MIN = 1e-3
DT_MAX = 1e-1
N_HEADS = 8
N_KV_HEADS = 2
HEAD_DIM = 64
D_ATTN = N_HEADS * HEAD_DIM
D_KV = N_KV_HEADS * HEAD_DIM
IDX_HEADS = 16
IDX_DIM = 64
TOPK = 256
Q_BLOCK = 128
ROPE_THETA = 10000.0
N_EXPERTS = 32
TOP_K_EXPERTS = 4
D_EXPERT = D_MODEL
SWIGLU_LIMIT = 7.0
SWIGLU_ALPHA = 1.702
RMS_EPS = 1e-5
NEG = -1e30
N_BRANCHES = 2
IN_SPLITS = (D_SSM, D_ATTN, D_KV, D_KV, IDX_HEADS * IDX_DIM, IDX_DIM, IDX_HEADS, D_MODEL, D_MODEL)
D_IN = sum(IN_SPLITS)
IN_OFFSETS = tuple(sum(IN_SPLITS[:i + 1]) for i in range(len(IN_SPLITS) - 1))

kernel_name = "hybrid_s5_dsa_moe_block"

def rms_norm(x, g):
    xf = x.astype(jnp.float32)
    out = xf * lax.rsqrt(jnp.mean(xf * xf, axis=-1, keepdims=True) + RMS_EPS) * g.astype(jnp.float32)
    return out.astype(x.dtype)

def rope(x, pos):
    d = x.shape[-1]
    half = d // 2
    inv = ROPE_THETA ** (-jnp.arange(half, dtype=jnp.float32) / half)
    ang = pos[:, None] * inv[None, :]
    cos = jnp.cos(ang)[:, None, :]
    sin = jnp.sin(ang)[:, None, :]
    xf = x.astype(jnp.float32)
    x1, x2 = xf[..., :half], xf[..., half:]
    out = jnp.concatenate([x1 * cos - x2 * sin, x2 * cos + x1 * sin], axis=-1)
    return out.astype(x.dtype)

def _complex_scan_op(e1, e2):
    a1r, a1i, b1r, b1i = e1
    a2r, a2i, b2r, b2i = e2
    ar = a2r * a1r - a2i * a1i
    ai = a2r * a1i + a2i * a1r
    br = a2r * b1r - a2i * b1i + b2r
    bi = a2r * b1i + a2i * b1r + b2i
    return (ar, ai, br, bi)

def s5_mixer(u, lam_re, lam_im, log_dt, b_re, b_im, c_re, c_im, d_skip, w_glu, b_glu):
    f32 = jnp.float32
    bsz, L, _ = u.shape
    uf = u.astype(f32).reshape(bsz, L, N_SSM_GROUPS, SSM_GROUP)
    lr, li = lam_re.astype(f32), lam_im.astype(f32)
    dt = jnp.exp(log_dt.astype(f32))[:, None]
    mag = jnp.exp(lr * dt)
    ar = mag * jnp.cos(li * dt)
    ai = mag * jnp.sin(li * dt)
    nr, ni = ar - 1.0, ai
    den = lr * lr + li * li
    zr = (nr * lr + ni * li) / den
    zi = (ni * lr - nr * li) / den
    br, bi = b_re.astype(f32), b_im.astype(f32)
    bbar_re = zr[:, :, None] * br - zi[:, :, None] * bi
    bbar_im = zr[:, :, None] * bi + zi[:, :, None] * br
    bu_re = jnp.einsum('blgh,gph->blgp', uf, bbar_re)
    bu_im = jnp.einsum('blgh,gph->blgp', uf, bbar_im)
    a_re = jnp.broadcast_to(ar, bu_re.shape)
    a_im = jnp.broadcast_to(ai, bu_re.shape)
    _, _, xr, xi = lax.associative_scan(_complex_scan_op, (a_re, a_im, bu_re, bu_im), axis=1)
    y = (jnp.einsum('blgp,ghp->blgh', xr, c_re.astype(f32))
         - jnp.einsum('blgp,ghp->blgh', xi, c_im.astype(f32))
         + d_skip.astype(f32) * uf)
    y = jax.nn.gelu(y.reshape(bsz, L, D_SSM))
    y = y * jax.nn.sigmoid(y @ w_glu.astype(f32) + b_glu.astype(f32))
    return y.astype(u.dtype)

def dsa_attention(q, k, v, q_idx, k_idx, w_idx):
    f32 = jnp.float32
    bsz, L = q.shape[0], q.shape[1]
    n_sel = min(TOPK, L // 4)
    n_blk = L // Q_BLOCK
    rep = N_HEADS // N_KV_HEADS
    q5 = q.reshape(bsz, L, N_KV_HEADS, rep, HEAD_DIM)
    kif = k_idx.astype(f32)
    key_pos = jnp.arange(L)
    bidx = jnp.arange(bsz)[:, None, None]

    def block(i):
        start = i * Q_BLOCK
        qb = lax.dynamic_slice_in_dim(q5, start, Q_BLOCK, axis=1).astype(f32)
        qib = lax.dynamic_slice_in_dim(q_idx, start, Q_BLOCK, axis=1).astype(f32)
        wib = lax.dynamic_slice_in_dim(w_idx, start, Q_BLOCK, axis=1).astype(f32) * (IDX_HEADS ** -0.5)
        qpos = start + jnp.arange(Q_BLOCK)
        s = jnp.einsum('bthd,bsd->bths', qib, kif) * (IDX_DIM ** -0.5)
        score = jnp.einsum('bths,bth->bts', jax.nn.relu(s), wib)
        causal = key_pos[None, :] <= qpos[:, None]
        score = jnp.where(causal[None], score, NEG)
        _, sel = lax.top_k(score, n_sel)
        valid = sel <= qpos[None, :, None]
        ks = k[bidx, sel].astype(f32)
        vs = v[bidx, sel].astype(f32)
        logits = jnp.einsum('btgrd,btkgd->btgrk', qb, ks) * (HEAD_DIM ** -0.5)
        logits = jnp.where(valid[:, :, None, None, :], logits, NEG)
        p = jax.nn.softmax(logits, axis=-1)
        o = jnp.einsum('btgrk,btkgd->btgrd', p, vs)
        return o.reshape(bsz, Q_BLOCK, D_ATTN).astype(q.dtype)

    out = lax.map(block, jnp.arange(n_blk))
    return out.transpose(1, 0, 2, 3).reshape(bsz, L, D_ATTN)

def moe(h, w_router, b_router, w_moe_in, b_moe_in, w_moe_out, b_moe_out):
    f32 = jnp.float32
    hf = h.reshape(-1, D_MODEL)
    logits = (hf @ w_router + b_router).astype(f32)
    vals, idx = lax.top_k(logits, TOP_K_EXPERTS)
    wts = jax.nn.softmax(vals, axis=-1)
    gates = jnp.sum(jax.nn.one_hot(idx, N_EXPERTS, dtype=f32) * wts[..., None], axis=1)
    out = jnp.zeros(hf.shape, f32)
    for e in range(N_EXPERTS):
        z = hf @ w_moe_in[e] + b_moe_in[e]
        zg = jnp.minimum(z[:, ::2], SWIGLU_LIMIT)
        zl = jnp.clip(z[:, 1::2], -SWIGLU_LIMIT, SWIGLU_LIMIT)
        act = zg * jax.nn.sigmoid(SWIGLU_ALPHA * zg) * (zl + 1.0)
        out = out + gates[:, e:e + 1] * (act @ w_moe_out[e] + b_moe_out[e]).astype(f32)
    return out.reshape(h.shape).astype(h.dtype)

def hybrid_layer(x, norm1_g, w_in, b_gate, ssm_lam_re, ssm_lam_im, ssm_log_dt, ssm_b_re, ssm_b_im,
                 ssm_c_re, ssm_c_im, ssm_d, w_glu, b_glu, w_proj_ssm, w_proj_attn, w_out,
                 norm2_g, w_router, b_router, w_moe_in, b_moe_in, w_moe_out, b_moe_out):
    bsz, L, _ = x.shape
    xn = rms_norm(x, norm1_g)
    proj = xn @ w_in
    u, q, k, v, qi, ki, wi, gs, ga = jnp.split(proj, IN_OFFSETS, axis=-1)
    pos = jnp.arange(L, dtype=jnp.float32)
    q = rope(q.reshape(bsz, L, N_HEADS, HEAD_DIM), pos)
    k = rope(k.reshape(bsz, L, N_KV_HEADS, HEAD_DIM), pos)
    v = v.reshape(bsz, L, N_KV_HEADS, HEAD_DIM)
    qi = rope(qi.reshape(bsz, L, IDX_HEADS, IDX_DIM), pos)
    ki = rope(ki.reshape(bsz, L, 1, IDX_DIM), pos)[:, :, 0]
    y_ssm = s5_mixer(u, ssm_lam_re, ssm_lam_im, ssm_log_dt, ssm_b_re, ssm_b_im,
                     ssm_c_re, ssm_c_im, ssm_d, w_glu, b_glu)
    y_att = dsa_attention(q, k, v, qi, ki, wi)
    g_ssm = jax.nn.sigmoid(gs + b_gate[0])
    g_att = jax.nn.sigmoid(ga + b_gate[1])
    mixed = g_ssm * (y_ssm @ w_proj_ssm) + g_att * (y_att @ w_proj_attn)
    x = x + mixed @ w_out
    x = x + moe(rms_norm(x, norm2_g), w_router, b_router, w_moe_in, b_moe_in, w_moe_out, b_moe_out)
    return x

def setup_inputs(seed: int = 0) -> dict:
    key = jax.random.key(seed)
    ks = jax.random.split(key, 32)
    f32 = jnp.float32

    def nrm(k, shape, scale):
        return jax.random.normal(k, shape, f32) * scale

    G, P, H = N_SSM_GROUPS, SSM_STATE, SSM_GROUP
    n = jnp.arange(P, dtype=f32)
    x = nrm(ks[0], (BATCH, SEQ, D_MODEL), 1.0)
    norm1_g = 1.0 + nrm(ks[1], (DEPTH, D_MODEL), 0.02)
    w_in = nrm(ks[2], (DEPTH, D_MODEL, D_IN), D_MODEL ** -0.5)
    b_gate = nrm(ks[3], (DEPTH, N_BRANCHES, D_MODEL), 0.02)
    ssm_lam_re = -0.5 + nrm(ks[4], (DEPTH, G, P), 0.01)
    ssm_lam_im = math.pi * n[None, None, :] + nrm(ks[5], (DEPTH, G, P), 0.01)
    ssm_log_dt = jax.random.uniform(ks[6], (DEPTH, G), f32, math.log(DT_MIN), math.log(DT_MAX))
    ssm_b_re = nrm(ks[7], (DEPTH, G, P, H), (2.0 * H) ** -0.5)
    ssm_b_im = nrm(ks[8], (DEPTH, G, P, H), (2.0 * H) ** -0.5)
    ssm_c_re = nrm(ks[9], (DEPTH, G, H, P), (2.0 * P) ** -0.5)
    ssm_c_im = nrm(ks[10], (DEPTH, G, H, P), (2.0 * P) ** -0.5)
    ssm_d = nrm(ks[11], (DEPTH, G, H), 1.0)
    w_glu = nrm(ks[12], (DEPTH, D_SSM, D_SSM), D_SSM ** -0.5)
    b_glu = nrm(ks[13], (DEPTH, D_SSM), 0.02)
    w_proj_ssm = nrm(ks[14], (DEPTH, D_SSM, D_MODEL), D_SSM ** -0.5)
    w_proj_attn = nrm(ks[15], (DEPTH, D_ATTN, D_MODEL), D_ATTN ** -0.5)
    w_out = nrm(ks[16], (DEPTH, D_MODEL, D_MODEL), D_MODEL ** -0.5)
    norm2_g = 1.0 + nrm(ks[17], (DEPTH, D_MODEL), 0.02)
    w_router = nrm(ks[18], (DEPTH, D_MODEL, N_EXPERTS), D_MODEL ** -0.5)
    b_router = nrm(ks[19], (DEPTH, N_EXPERTS), 0.01)
    w_moe_in = nrm(ks[20], (DEPTH, N_EXPERTS, D_MODEL, 2 * D_EXPERT), D_MODEL ** -0.5)
    b_moe_in = nrm(ks[21], (DEPTH, N_EXPERTS, 2 * D_EXPERT), 0.01)
    w_moe_out = nrm(ks[22], (DEPTH, N_EXPERTS, D_EXPERT, D_MODEL), D_EXPERT ** -0.5)
    b_moe_out = nrm(ks[23], (DEPTH, N_EXPERTS, D_MODEL), 0.01)
    norm_f_g = 1.0 + nrm(ks[24], (D_MODEL,), 0.02)
    return {"x": x, "norm1_g": norm1_g, "w_in": w_in, "b_gate": b_gate,
            "ssm_lam_re": ssm_lam_re, "ssm_lam_im": ssm_lam_im, "ssm_log_dt": ssm_log_dt,
            "ssm_b_re": ssm_b_re, "ssm_b_im": ssm_b_im, "ssm_c_re": ssm_c_re, "ssm_c_im": ssm_c_im,
            "ssm_d": ssm_d, "w_glu": w_glu, "b_glu": b_glu, "w_proj_ssm": w_proj_ssm,
            "w_proj_attn": w_proj_attn, "w_out": w_out, "norm2_g": norm2_g,
            "w_router": w_router, "b_router": b_router, "w_moe_in": w_moe_in, "b_moe_in": b_moe_in,
            "w_moe_out": w_moe_out, "b_moe_out": b_moe_out, "norm_f_g": norm_f_g}

def reference(x, norm1_g, w_in, b_gate, ssm_lam_re, ssm_lam_im, ssm_log_dt, ssm_b_re, ssm_b_im,
              ssm_c_re, ssm_c_im, ssm_d, w_glu, b_glu, w_proj_ssm, w_proj_attn, w_out,
              norm2_g, w_router, b_router, w_moe_in, b_moe_in, w_moe_out, b_moe_out, norm_f_g):
    h = x
    for l in range(DEPTH):
        h = hybrid_layer(h, norm1_g[l], w_in[l], b_gate[l], ssm_lam_re[l], ssm_lam_im[l], ssm_log_dt[l],
                         ssm_b_re[l], ssm_b_im[l], ssm_c_re[l], ssm_c_im[l], ssm_d[l], w_glu[l], b_glu[l],
                         w_proj_ssm[l], w_proj_attn[l], w_out[l], norm2_g[l], w_router[l], b_router[l],
                         w_moe_in[l], b_moe_in[l], w_moe_out[l], b_moe_out[l])
    return rms_norm(h, norm_f_g)


_drawn_inputs = setup_inputs


def setup_inputs(seed=0):
    import zlib

    import numpy as np

    out = dict(_drawn_inputs(seed))
    spreads = {}
    factors = {'b_gate': 4.233,
     'ssm_lam_re': 200.0,
     'b_glu': 5.161,
     'b_moe_in': 8.0,
     'b_moe_out': 8.0,
     'norm_f_g': 23.297,
     'ssm_log_dt': 14.688,
     'ssm_b_im': 20.086,
     'ssm_c_re': 12.33,
     'ssm_c_im': 15.391,
     'ssm_lam_im': 5.432,
     'ssm_b_re': 8.0}
    for name, (base, spread) in spreads.items():
        noise = np.random.default_rng([zlib.crc32(name.encode()), seed]).standard_normal(out[name].shape)
        drawn = base * np.exp(spread * noise) if base else spread * noise
        out[name] = __import__('jax').numpy.asarray(drawn.astype(out[name].dtype))
    for name, factor in factors.items():
        out[name] = (out[name] * factor).astype(out[name].dtype)
    return out
```

```python
import math
from contextlib import ExitStack

import numpy as np

import concourse.bass as bass
from concourse import mybir

P = 128
T = 256
TT = T // P
D = 1024
KD = D // P
DS = 512
KS = DS // P
G, PS, H = 32, 64, 16
NCH = G * PS // P
NH, NKV, HD = 8, 2, 64
IH, ID = 16, 64
NSEL = min(256, T // 4)
NE, TOPE, F = 32, 4, 1024
KF = F // P
LIMIT, ALPHA = 7.0, 1.702
EPS = 1e-5
NEG = -1e30
GONE = -3e38
FAR = 1024.0
SLOTS = 64
PASSES = T // SLOTS
TWO_PI = 2.0 * math.pi

C_U, C_Q, C_K, C_V, C_QI, C_KI, C_WI, C_GS, C_GA, C_END = 0, 512, 1024, 1152, 1280, 2304, 2368, 2384, 3408, 4432
TOK = [(C_QI + 256 * n, 256) for n in range(4)] + [(C_KI, C_GS - C_KI), (C_K, 256), (C_Q, 256), (C_Q + 256, 256)]
NTOK = C_GS - C_Q

TB_ID, TB_COS, TB_SIN, TB_SLOT, TB_EXP, TB_TRI, TB_ONE, TB_CAUSAL, TB_END = \
    [int(v) for v in np.cumsum([0, P, TT * 64, TT * 32, SLOTS, NE, P, P, TT * T])]


def constant_tables():
    t = np.zeros((P, TB_END), np.float32)
    t[:, TB_ID:TB_ID + P] = np.eye(P)
    inv = (np.float32(10000.0) ** (-np.arange(32, dtype=np.float32) / np.float32(32))).astype(np.float32)
    pos = np.arange(T, dtype=np.float32)
    ang = (pos[:, None] * inv[None, :]).astype(np.float32).astype(np.float64)
    cos, sin = np.cos(ang).astype(np.float32), np.sin(ang).astype(np.float32)
    for tt in range(TT):
        rows = slice(tt * P, tt * P + P)
        t[:, TB_COS + 64 * tt:TB_COS + 64 * tt + 64] = np.concatenate([cos[rows], cos[rows]], 1)
        t[:, TB_SIN + 32 * tt:TB_SIN + 32 * tt + 32] = sin[rows]
        t[:, TB_CAUSAL + T * tt:TB_CAUSAL + T * tt + T] = np.where(
            np.arange(T)[None, :] <= (tt * P + np.arange(P))[:, None], 0.0, NEG)
    t[:, TB_SLOT:TB_SLOT + SLOTS] = np.arange(SLOTS)
    t[:, TB_EXP:TB_EXP + NE] = np.arange(NE)
    t[:, TB_TRI:TB_TRI + P] = np.arange(P)[:, None] < np.arange(P)[None, :]
    t[:, TB_ONE:TB_ONE + P] = 1.0
    return t


JOBS = (["X0", "X1", "X2", "X3", "U0", "U1", "T0", "T1", "T2", "T3", "T4", "T5", "T6", "T7"]
        + ["S0", "S1", "S2", "S3", "QI0", "QI1", "QI2", "QI3", "KK", "Q0", "Q1"]
        + [f"R0_{n}" for n in range(4)] + [f"R1_{n}" for n in range(8)]
        + ["GLU0", "GLU1", "A0", "A1", "A2", "A3"]
        + [f"P0_{n}" for n in range(2)] + [f"P1_{n}" for n in range(4)]
        + ["HX0", "HX1", "HX2", "HX3"])
JOB = {name: n for n, name in enumerate(JOBS)}

CHUNKS = (["U0", "U1"] + [f"T{n}" for n in range(8)] + [f"S{n}" for n in range(4)] + ["GLU"]
          + [f"A{n}" for n in range(4)] + ["PS0", "PA0", "PS1", "PA1"] + [f"W{n}" for n in range(4)]
          + ["GAIN", "BIAS", "BIN"])
CHUNK = {name: n for n, name in enumerate(CHUNKS)}
NSLOT = 4


def build(nc, io, out):
    fp32, i32, u32 = mybir.dt.float32, mybir.dt.int32, mybir.dt.uint32
    ALU, ACT, AX = mybir.AluOpType, mybir.ActivationFunctionType, mybir.AxisListType

    with ExitStack() as ctx:
        def sb(name, shape, dt=fp32):
            return ctx.enter_context(nc.sbuf_tensor(name, shape, dt))

        def sem(name):
            return ctx.enter_context(nc.semaphore(name))

        SW = 2048
        NW_IN, NW_OUT = KD, KF // 2
        NW = NW_IN + NW_OUT
        ring = sb("ring", [P, NW * SW])

        def early(at, *dims):
            n = int(np.prod(dims))
            v = ring[:, at:at + n]
            if len(dims) == 2:
                v = v.rearrange("p (a b) -> p a b", a=dims[0])
            return v

        phase_re, phase_im = early(0, NCH, T), early(NCH * T, NCH, T)
        prod = [early(2 * NCH * T + n * 4 * T, 4, T) for n in range(4)]
        state_re, state_im = early(12288, 4, T), early(13312, 4, T)
        xs_re, xs_im = early(14336, 4, T), early(15360, 4, T)
        b_nat = [early(14336 + 512 * n, 4, P) for n in range(2)]
        c_nat = [early(15360 + 512 * n, 4, P) for n in range(2)]
        gate_s, gate_a = early(16384, KD, T), early(18432, KD, T)
        y_ssm, y_att = early(20480, KS, T), early(21504, KS, T)
        b_t = [early(22528 + 512 * n, 4, P) for n in range(2)]
        c_t = [early(23552 + 512 * n, 4, P) for n in range(2)]

        table = sb("table", [P, TB_END])
        x = sb("x", [P, TT, D])
        xs = sb("xs", [P, TT, D])
        x_t = sb("x_t", [P, KD, T])
        wbuf = sb("wbuf", [P, NSLOT, SW])
        mixed = sb("mixed", [P, KD, T])
        u_in = sb("u_in", [P, KS, T])
        gfin = wbuf[:, CHUNK["GAIN"] % NSLOT, 0:D]
        b_out = wbuf[0:NE, CHUNK["BIAS"] % NSLOT, 0:D]
        b_in = wbuf[0:NE, CHUNK["BIN"] % NSLOT, :]
        vec_rows = sb("vec_rows", [72, P])
        dt_rows = sb("dt_rows", [NCH, P])
        dt_pair = sb("dt_pair", [NCH, 2])
        vec = sb("vec", [P, 72])
        par = sb("par", [P, 24, NCH])
        stat = sb("stat", [P, 64])
        w_rout = sb("w_rout", [P, KD, NE])
        b_rout = sb("b_rout", [P, NE])
        late = sb("late", [P, 7840])
        flag = sb("flag", [1, 1], i32)

        ident = table[:, TB_ID:TB_ID + P]
        cos_t = table[:, TB_COS:TB_COS + TT * 64].rearrange("p (t d) -> p t d", t=TT)
        sin_t = table[:, TB_SIN:TB_SIN + TT * 32].rearrange("p (t d) -> p t d", t=TT)
        slot_no = table[:, TB_SLOT:TB_SLOT + SLOTS]
        exp_no = table[:, TB_EXP:TB_EXP + NE]
        tri = table[:, TB_TRI:TB_TRI + P]
        ones = table[:, TB_ONE:TB_ONE + P]
        causal = table[:, TB_CAUSAL:TB_CAUSAL + TT * T].rearrange("p (t s) -> p t s", t=TT)

        V_G1, V_G2, V_BG, V_BGLU, V_D, V_LR, V_LI = 0, 8, 16, 32, 36, 40, 56
        L_RE, L_IM = vec[:, V_LR:V_LR + NCH], vec[:, V_LI:V_LI + NCH]

        ptok = late[:, 0:TT * NTOK].rearrange("p (t n) -> p t n", t=TT)
        o = TT * NTOK
        score = late[:, o:o + TT * T].rearrange("p (t s) -> p t s", t=TT)
        taken = late[:, o + 512:o + 1024].rearrange("p (t s) -> p t s", t=TT)
        bias = late[:, o + 1024:o + 1536].rearrange("p (t s) -> p t s", t=TT)
        ki_two = late[:, o + 1024:o + 1280].rearrange("p (t n d) -> p t n d", t=TT, n=2)
        relu = late[:, o + 1536:o + 2560].rearrange("p (b s) -> p b s", b=2)
        q_t = late[:, o + 2560:o + 3584].rearrange("p (k t) -> p k t", k=4)
        k_t = late[:, o + 3584:o + 3840]
        ki_t = late[:, o + 3840:o + 4096]
        rope_a, rope_b = mixed, xs
        qi_t = xs[:, :, :].rearrange("p t (k s) -> p (t k) s", s=T)
        logit = xs[:, :, :].rearrange("p t (h s) -> p (t h) s", s=T)
        prob_t = mixed[:, :, :].rearrange("p k t -> p (k t)")
        glu_g = prod[0]
        y_raw, y_gelu = prod[2], prod[3]

        def cut(at, n):
            return late[:, at:at + n]
        h_tok, gate_z, lin_z, sig, act = [cut(512 * n, 512) for n in range(5)]
        h_sel = cut(2560, 512).rearrange("p (j q s) -> p j q s", q=2, s=SLOTS)
        act_t = cut(3072, 512).rearrange("p (j q s) -> p j q s", q=2, s=SLOTS)
        y_tok = cut(3584, 512)
        gated = cut(4096, TT * 2 * SLOTS).rearrange("p (t q s) -> p t q s", t=TT, q=2)
        gated_t = cut(4352, T)
        one_hot = cut(4608, TT * SLOTS).rearrange("p (t s) -> p t s", t=TT)
        chosen = late[0:NE, 4736:4736 + SLOTS]

        def act_tile(k):
            return act_t[:, 2 * (k // 4) + k % 2, k // 2 % 2, :]
        place = cut(5120, TT * NE).rearrange("p (t e) -> p t e", t=TT)
        gates = cut(5184, TT * NE).rearrange("p (t e) -> p t e", t=TT)
        picked = cut(5248, TT * NE).rearrange("p (t e) -> p t e", t=TT)
        rlog = cut(5312, TT * NE).rearrange("p (t e) -> p t e", t=TT)
        top8 = cut(5376, TT * 8).rearrange("p (t k) -> p t k", t=TT)
        top8i = late[:, 5392:5392 + TT * 8].bitcast(u32).rearrange("p (t k) -> p t k", t=TT)
        top8f = cut(5408, TT * 8).rearrange("p (t k) -> p t k", t=TT)
        topw = cut(5424, TT * 8).rearrange("p (t k) -> p t k", t=TT)
        hot4 = cut(5440, TT * TOPE * NE).rearrange("p (t k e) -> p t k e", t=TT, k=TOPE)
        hot4w = cut(5696, TT * TOPE * NE).rearrange("p (t k e) -> p t k e", t=TT, k=TOPE)
        gates_t = late[0:NE, 5952:5952 + T]
        final = xs

        ps = ctx.enter_context(nc.psum_tensor("ps", [P, 8, 512], fp32))
        rot = [ps[:, 0, :], ps[:, 1, :]]

        tables_in, x_in, vec_in, misc_in, bnat_in, cnat_in = [sem(n) for n in (
            "tables_in", "x_in", "vec_in", "misc_in", "bnat_in", "cnat_in")]
        w_slot_in = [sem(f"w_slot_in{n}") for n in range(NSLOT)]
        zeroed = sem("zeroed")
        sum_sq, root, x_norm = sem("sum_sq"), sem("root"), sem("x_norm")
        rot_done, rot_free = sem("rot_done"), sem("rot_free")
        small_t, small_free = sem("small_t"), sem("small_free")
        par_v, par_s = sem("par_v"), sem("par_s")
        c_ready = sem("c_ready")
        bu_done, bu_used, w_rot, scanned, x_state, y_done, y_raw_ok = [sem(n) for n in (
            "bu_done", "bu_used", "w_rot", "scanned", "x_state", "y_done", "y_raw_ok")]
        phase_v, phase_p = sem("phase_v"), sem("phase_p")
        roped = sem("roped")
        relu_used = sem("relu_used")
        gelu_ok, y_ssm_ok = sem("gelu_ok"), sem("y_ssm_ok")
        logit_done, logit_used, row_max, expd, prob_ok, att_done, att_out = [sem(n) for n in (
            "logit_done", "logit_used", "row_max", "expd", "prob_ok", "att_done", "att_out")]
        proj_done, mixed_ok, wout_done, x1_ok = [sem(n) for n in ("proj_done", "mixed_ok", "wout_done", "x1_ok")]
        rlogit, top_ok, top_exp, picked_ok, placed, route_ok, flag_ok, gates_tr, gates_t_ok = [sem(n) for n in (
            "rlogit", "top_ok", "top_exp", "picked_ok", "placed", "route_ok", "flag_ok", "gates_tr",
            "gates_t_ok")]
        moe_in = [sem(f"moe_in{n}") for n in range(NW)]
        chunk_used = sem("chunk_used")
        hot_ok, gathered, h_tok_ok, h_trans, h_sel_ok, chosen_ok, z_gate, z_lin, sig_ok, z_prod, act_ok, act_trans, \
            act_t_ok, y_tok_ok, gated_eq, gated_ok, gated_trans, gated_t_ok, sum_ok = [sem(n) for n in (
                "hot_ok", "gathered", "h_tok_ok", "h_trans", "h_sel_ok", "chosen_ok", "z_gate", "z_lin", "sig_ok",
                "z_prod", "act_ok", "act_trans", "act_t_ok", "y_tok_ok", "gated_eq", "gated_ok", "gated_trans",
                "gated_t_ok", "sum_ok")]
        place_ok = sem("place_ok")
        out_ready, stored = sem("out_ready"), sem("stored")
        v_chain, a_chain, g_chain = sem("v_chain"), sem("a_chain"), sem("g_chain")

        w_in = io["w_in"].rearrange("(k p) n -> p k n", p=P)
        w_glu = io["w_glu"].rearrange("(k p) n -> p k n", p=P)
        w_ps = io["w_proj_ssm"].rearrange("(k p) n -> p k n", p=P)
        w_pa = io["w_proj_attn"].rearrange("(k p) n -> p k n", p=P)
        w_out = io["w_out"].rearrange("(k p) n -> p k n", p=P)

        def chunk_view(name):
            slot = wbuf[:, CHUNK[name] % NSLOT, :]
            wide = slot.rearrange("p (k n) -> p k n", k=KD)
            deep = slot.rearrange("p (k n) -> p k n", k=KS)
            if name == "GAIN":
                return gfin, io["norm_f_g"].unsqueeze(0).to_broadcast([P, D])
            if name == "BIN":
                return b_in, io["b_moe_in"]
            if name == "BIAS":
                return b_out, io["b_moe_out"]
            n = int(name[-1]) if name != "GLU" else 0
            if name == "GLU":
                return deep, w_glu
            if name[:2] == "PS":
                return deep, w_ps[:, :, 512 * n:512 * n + 512]
            if name[:2] == "PA":
                return deep, w_pa[:, :, 512 * n:512 * n + 512]
            if name[0] == "T":
                c, w = TOK[n]
                return wide[:, :, 0:w], w_in[:, :, c:c + w]
            c = {"U": C_U, "S": C_GS, "A": C_GA}.get(name[0])
            src = w_out if c is None else w_in
            return wide, src[:, :, (c or 0) + 256 * n:(c or 0) + 256 * n + 256]

        def chunk_arrived(eng, name):
            n = CHUNK[name]
            eng.wait_ge(w_slot_in[n % NSLOT], 16 * (n // NSLOT + 1))

        def chunk_done(name):
            if name == "GLU":
                return rot_done, JOB["GLU1"] + 1
            if name[:2] in ("PS", "PA"):
                return proj_done, 4 * (int(name[-1]) + 1)
            if name[0] == "W":
                return wout_done, int(name[1]) + 1
            return rot_done, JOB[name] + 1

        def expert_chunk(e, c):
            if c < NW_IN:
                return io["w_moe_in"][bass.ds(e, 1), c * P:(c + 1) * P, :].rearrange("o p n -> p (o n)")
            r = (c - NW_IN) * 2 * P
            return io["w_moe_out"][bass.ds(e, 1), r:r + 2 * P, :].rearrange("o (k p) n -> p (o k) n", p=P)

        def ring_slot(c):
            v = ring[:, c * SW:(c + 1) * SW]
            return v if c < NW_IN else v.rearrange("p (k n) -> p k n", k=2)

        def passes(eng, one_pass):
            one_pass(0, 0)
            eng.wait_ge(flag_ok, 1)
            most = eng.value_load(flag[0:1, 0:1], min_val=0, max_val=T)
            with eng.Fori(1, PASSES) as c:
                with eng.If(most > c * SLOTS):
                    one_pass(c, c * NE)
                eng.end_ifs()

        block = ctx.enter_context(nc.Block())

        @block.sync
        def _(sp):
            sp.dma_start(x[:, :, :], io["x"].rearrange("(t p) d -> p t d", p=P)).then_inc(x_in, 16)
            for name in CHUNKS:
                n = CHUNK[name]
                if n >= NSLOT:
                    sp.wait_ge(*chunk_done(CHUNKS[n - NSLOT]))
                dst, src = chunk_view(name)
                sp.dma_start(dst, src).then_inc(w_slot_in[n % NSLOT], 16)

            def one_pass(c, first):
                def load(e, j, head):
                    for n in range(NW):
                        if head:
                            if n == 0:
                                sp.wait_ge(rot_done, JOB["GLU1"] + 1)
                                sp.wait_ge(rot_free, JOB["GLU1"] + 1)
                                sp.wait_ge(y_ssm_ok, 1)
                            if n == NW_IN:
                                sp.wait_ge(mixed_ok, KD)
                        else:
                            sp.wait_ge(chunk_used, j * NW + (n + 1 - NW))
                        sp.dma_start(ring_slot(n), expert_chunk(e, n)).then_inc(moe_in[n], 16)
                if isinstance(c, int):
                    load(0, 0, True)
                    with sp.Fori(1, NE) as e:
                        load(e, e, False)
                else:
                    with sp.Fori(0, NE) as e:
                        load(e, e + first, False)
            passes(sp, one_pass)
            for t in range(TT):
                sp.wait_ge(out_ready, t + 1)
                sp.dma_start(out[t * P:(t + 1) * P, :], final[:, t, :]).then_inc(stored, 16)
            sp.wait_ge(stored, 16 * TT)

        @block.gpsimd
        def _(gp):
            chain = [0]

            def link(ins):
                chain[0] += 1
                ins.then_inc(g_chain, 1)
                gp.wait_ge(g_chain, chain[0])

            for v in b_nat + c_nat:
                gp.memset(v, 0.0).then_inc(zeroed, 1)

            n = 1
            k = 0
            while n < T:
                lo_re, lo_im = phase_re[:, :, 0:n], phase_im[:, :, 0:n]
                a_re = par[:, 8 + 2 * (k % 2), :].unsqueeze(2).to_broadcast([P, NCH, n])
                a_im = par[:, 9 + 2 * (k % 2), :].unsqueeze(2).to_broadcast([P, NCH, n])
                t1 = ring[:, 2 * NCH * T:2 * NCH * T + NCH * n].rearrange("p (c t) -> p c t", c=NCH)
                t2 = ring[:, 2 * NCH * T + 2048:2 * NCH * T + 2048 + NCH * n].rearrange("p (c t) -> p c t", c=NCH)
                gp.wait_ge(phase_v, k + 1)
                gp.tensor_tensor(t1, lo_re, a_im, ALU.mult)
                link(gp.tensor_tensor(t2, lo_im, a_re, ALU.mult))
                gp.tensor_tensor(phase_im[:, :, n:2 * n], t1, t2, ALU.add).then_inc(phase_p, 1)
                gp.wait_ge(phase_p, k + 1)
                n *= 2
                k += 1

            def rotate_in(i):
                gp.wait_ge(bu_used, i + 1)
                if i:
                    gp.wait_ge(scanned, 2 * i)
                gp.tensor_tensor(state_re, prod[0], prod[1], ALU.add)
                gp.tensor_tensor(state_im, prod[2], prod[3], ALU.subtract).then_inc(w_rot, 1)

            for i in range(4):
                rotate_in(i)
                gp.wait_ge(scanned, 2 * i + 2)
                if i:
                    gp.wait_ge(y_done, i)
                gp.tensor_tensor(xs_re, prod[0], prod[1], ALU.subtract)
                gp.tensor_tensor(xs_im, prod[2], prod[3], ALU.add).then_inc(x_state, 1)

        @block.scalar
        def _(ac):
            ac.dma_start(table[:, :], io["tables"]).then_inc(tables_in, 16)
            rows = [(V_G1, io["norm1_g"], 8), (V_G2, io["norm2_g"], 8), (V_BG, io["b_gate"], 16),
                    (V_BGLU, io["b_glu"], 4), (V_D, io["ssm_d"], 4), (V_LR, io["ssm_lam_re"], NCH),
                    (V_LI, io["ssm_lam_im"], NCH)]
            for at, src, n in rows:
                ac.dma_start(vec_rows[at:at + n, :], src.rearrange("(r c) -> r c", c=P)).then_inc(vec_in, 16)
            ac.dma_start(dt_pair[:, :], io["ssm_log_dt"].rearrange("(j g) -> j g", g=2)).then_inc(vec_in, 16)
            ac.wait_ge(zeroed, 4)
            for n, name in enumerate(("ssm_b_re", "ssm_b_im")):
                src = io[name].rearrange("(j two) p h -> two p j h", two=2)
                for q in range(2):
                    dst = b_nat[n][64 * q:64 * q + 64].rearrange("p a (b two h) -> p two (a b) h", two=2, h=H)
                    ac.dma_start(dst[:, q], src[q]).then_inc(bnat_in, 16)
            for n, name in enumerate(("ssm_c_re", "ssm_c_im")):
                src = io[name].rearrange("(a b) h p -> b h a p", b=8)
                for b in range(8):
                    q = b % 2
                    ac.dma_start(c_nat[n][16 * b:16 * b + 16, :, 64 * q:64 * q + 64], src[b]).then_inc(cnat_in, 16)
            ac.dma_start(w_rout[:, :, :], io["w_router"].rearrange("(k p) e -> p k e", p=P)).then_inc(misc_in, 16)
            ac.dma_start(b_rout[:, :], io["b_router"].unsqueeze(0).to_broadcast([P, NE])).then_inc(misc_in, 16)

            chain = [0]

            def link(ins):
                chain[0] += 1
                ins.then_inc(a_chain, 1)
                ac.wait_ge(a_chain, chain[0])

            def squares(t):
                return ac.activation(mixed[:, 4 * t:4 * t + 4, :], x[:, t, :].rearrange("p (k s) -> p k s", k=4),
                                     ACT.Square, accum_out=stat[:, t:t + 1])

            ac.wait_ge(x_in, 16)
            link(squares(0))
            squares(1).then_inc(sum_sq, 1)
            ac.wait_ge(sum_sq, 2)
            ac.activation(stat[:, 4:6], stat[:, 2:4], ACT.Sqrt).then_inc(root, 1)

            def job(name):
                ac.wait_ge(rot_done, JOB[name] + 1)
                return rot[JOB[name] % 2]

            def norm_t(name, n, gain):
                b = job(name)
                for k in (2 * n, 2 * n + 1):
                    i = ac.activation(x_t[:, k, :], b[:, (k % 2) * T:(k % 2) * T + T], ACT.Copy,
                                      scale=vec[:, gain + k:gain + k + 1])
                i.then_inc(rot_free, 1)

            ac.wait_ge(small_free, 2)
            for n in range(4):
                norm_t(f"X{n}", n, V_G1)
            ac.activation(par[:, 0, :], par[:, 0, :], ACT.Exp).then_inc(par_s, 1)
            ac.wait_ge(par_v, 1)
            ac.activation(par[:, 2, :], par[:, 1, :], ACT.Exp).then_inc(par_s, 1)
            ac.activation(par[:, 5, :], par[:, 4, :], ACT.Sin).then_inc(par_s, 1)
            ac.activation(par[:, 6, :], par[:, 4, :], ACT.Sin, scale=0.5).then_inc(par_s, 1)
            for n in range(2):
                b = job(f"U{n}")
                ac.activation(u_in[:, 2 * n:2 * n + 2, :], b.rearrange("p (k t) -> p k t", k=2), ACT.Copy).then_inc(rot_free, 1)
            for n, (c, w) in enumerate(TOK):
                b = job(f"T{n}")
                ac.activation(ptok[:, :, c - C_Q:c - C_Q + w], b[:, 0:TT * w].rearrange("p (t n) -> p t n", t=TT),
                              ACT.Copy).then_inc(rot_free, 1)

            def gate(letter, dst, at, n):
                b = job(f"{letter}{n}")
                for m in (2 * n, 2 * n + 1):
                    i = ac.activation(dst[:, m, :], b[:, (m % 2) * T:(m % 2) * T + T], ACT.Sigmoid,
                                      bias=vec[:, at + m:at + m + 1])
                i.then_inc(rot_free, 1)

            for n in range(4):
                gate("S", gate_s, V_BG, n)
            for n in range(4):
                b = job(f"QI{n}")
                ac.activation(qi_t[:, 2 * n:2 * n + 2, :], b.rearrange("p (k t) -> p k t", k=2),
                              ACT.Copy).then_inc(rot_free, 1)
            b = job("KK")
            ac.activation(ki_t, b[:, 0:T], ACT.Copy)
            ac.activation(k_t, b[:, T:2 * T], ACT.Copy).then_inc(rot_free, 1)
            for n in range(2):
                b = job(f"Q{n}")
                ac.activation(q_t[:, 2 * n:2 * n + 2, :], b.rearrange("p (k t) -> p k t", k=2),
                              ACT.Copy).then_inc(rot_free, 1)
            r = 0
            for t in range(TT):
                for n in range(4 * (t + 1)):
                    b = job(f"R{t}_{n}")
                    if r >= 2:
                        ac.wait_ge(relu_used, r - 1)
                    ac.activation(relu[:, r % 2, :], b, ACT.Relu).then_inc(rot_free, 1)
                    r += 1
            ac.wait_ge(y_raw_ok, 1)
            ac.activation(y_gelu, y_raw, ACT.Gelu_apprx_tanh).then_inc(gelu_ok, 1)
            for n in range(2):
                b = job(f"GLU{n}")
                for m in (2 * n, 2 * n + 1):
                    i = ac.activation(glu_g[:, m, :], b[:, (m % 2) * T:(m % 2) * T + T], ACT.Sigmoid,
                                      bias=vec[:, V_BGLU + m:V_BGLU + m + 1])
                i.then_inc(rot_free, 1)
            for n in range(4):
                gate("A", gate_a, V_BG + KD, n)
            for t in range(TT):
                w = P * (t + 1)
                ac.wait_ge(row_max, t + 1)
                for h in range(NH):
                    i = ac.activation(logit[:, h, 0:w], logit[:, h, 0:w], ACT.Exp,
                                      bias=stat[:, 8 + h:9 + h], accum_out=stat[:, 16 + h:17 + h])
                i.then_inc(expd, 1)
                for n in range(2 * (t + 1)):
                    b = job(f"P{t}_{n}")
                    if t == 1 and n == 0:
                        ac.wait_ge(att_done, 1)
                    ac.activation(prob_t[:, 512 * n:512 * n + 512], b, ACT.Copy).then_inc(rot_free, 1)
                ac.wait_ge(att_done, t + 1)
                ac.activation(y_att[:, :, t * P:t * P + P], ps[:, 2 + t, :].rearrange("p (k t) -> p k t", k=KS),
                              ACT.Copy).then_inc(att_out, 1)
            ac.wait_ge(x1_ok, KD // 2)
            link(squares(0))
            squares(1).then_inc(sum_sq, 1)
            ac.wait_ge(sum_sq, 4)
            ac.activation(stat[:, 4:6], stat[:, 2:4], ACT.Sqrt).then_inc(root, 1)
            for n in range(4):
                norm_t(f"HX{n}", n, V_G2)
            ac.wait_ge(top_ok, 1)
            ac.activation(topw[:, :, 0:TOPE], topw[:, :, 0:TOPE], ACT.Exp).then_inc(top_exp, 1)

            def one_pass(c, first):
                def gathered_rows(j):
                    ac.wait_ge(gathered, j + 1)
                    ac.activation(h_tok, ps[:, 3, :], ACT.Copy).then_inc(h_tok_ok, 1)

                def body(j, tail=False):
                    ac.wait_ge(z_gate, j + 1)
                    ac.activation(sig, gate_z, ACT.Sigmoid, scale=ALPHA).then_inc(sig_ok, 1)
                    if not tail:
                        gathered_rows(j + 1)
                    ac.wait_ge(act_trans, j + 1)
                    ac.activation(act_t, ps[:, 0, :].rearrange("p (j q s) -> p j q s", q=2, s=SLOTS),
                                  ACT.Copy).then_inc(act_t_ok, 1)
                    ac.wait_ge(chunk_used, j * NW + NW)
                    ac.activation(y_tok, ps[:, 2, :], ACT.Copy).then_inc(y_tok_ok, 1)
                gathered_rows(first)
                body(first)
                with ac.Fori(1, NE - 1) as e:
                    body(e + first)
                body(first + NE - 1, tail=True)
            passes(ac, one_pass)
            ac.wait_ge(x1_ok, KD // 2 + 1)
            link(squares(0))
            ac.wait_ge(x1_ok, KD // 2 + 2)
            squares(1).then_inc(sum_sq, 1)
            ac.wait_ge(sum_sq, 6)
            ac.activation(stat[:, 4:6], stat[:, 2:4], ACT.Sqrt).then_inc(root, 1)

        @block.vector
        def _(ve):
            chain = [0]

            def link(ins):
                chain[0] += 1
                ins.then_inc(v_chain, 1)
                ve.wait_ge(v_chain, chain[0])

            def tt(out_, a, b, op):
                return ve.tensor_tensor(out_, a, b, op)

            def rstd(n):
                ve.wait_ge(sum_sq, 2 * n + 1)
                ve.tensor_scalar(stat[:, 2:4], stat[:, 0:2], 1.0 / D, EPS, ALU.mult, ALU.add).then_inc(sum_sq, 1)
                ve.wait_ge(root, n + 1)
                link(ve.reciprocal(stat[:, 6:8], stat[:, 4:6]))

            ve.wait_ge(vec_in, 16 * 8)
            ve.tensor_copy(dt_rows[:, :].rearrange("j (g p) -> j g p", g=2),
                           dt_pair[:, :].unsqueeze(2).to_broadcast([NCH, 2, PS])).then_inc(small_free, 1)
            ve.wait_ge(small_free, 1)
            ve.wait_ge(small_t, 1)
            ve.tensor_copy(vec[:, :], ps[:, 7, 0:72])
            ve.tensor_copy(par[:, 0, :], ps[:, 7, 128:128 + NCH]).then_inc(small_free, 1)
            ve.wait_ge(small_free, 2)
            rstd(0)
            for t in range(TT):
                ve.tensor_scalar(xs[:, t, :], x[:, t, :], stat[:, 6 + t:7 + t], None, ALU.mult).then_inc(x_norm, 1)
            ve.wait_ge(small_t, 2)
            for n in range(2):
                i = ve.tensor_copy(b_t[n], ps[:, 4 + n, :].rearrange("p (a c) -> p a c", a=4))
            i.then_inc(small_free, 1)

            pr = lambda n: par[:, n, :]
            DT, LRDT, MAG, ANG, RED, SIN_, HALF, COS = 0, 1, 2, 3, 4, 5, 6, 7
            ve.wait_ge(par_s, 1)
            link(tt(pr(LRDT), L_RE, pr(DT), ALU.mult))
            link(tt(pr(ANG), L_IM, pr(DT), ALU.mult))
            magic = 12582912.0
            c1 = 6.28125
            c2 = float(np.float32(round((TWO_PI - c1) * 2 ** 21) / 2 ** 21))
            c3 = TWO_PI - c1 - c2
            link(ve.tensor_scalar(pr(12), pr(ANG), 1.0 / TWO_PI, magic, ALU.mult, ALU.add))
            link(ve.tensor_scalar(pr(13), pr(12), magic, None, ALU.subtract))
            link(ve.scalar_tensor_tensor(pr(14), pr(13), -c1, pr(ANG), ALU.mult, ALU.add))
            link(ve.scalar_tensor_tensor(pr(12), pr(13), -c2, pr(14), ALU.mult, ALU.add))
            link(ve.scalar_tensor_tensor(pr(14), pr(13), -c3, pr(12), ALU.mult, ALU.add))
            ve.tensor_scalar(pr(RED), pr(14), 3.1415925, -3.1415925, ALU.min, ALU.max).then_inc(par_v, 1)
            ve.wait_ge(par_s, 4)
            link(tt(pr(12), pr(HALF), pr(HALF), ALU.mult))
            link(ve.tensor_scalar(pr(8), pr(12), -2.0, 1.0, ALU.mult, ALU.add))
            link(ve.tensor_copy(pr(9), pr(SIN_)))
            ve.memset(phase_re[:, :, 0:1], 1.0)
            ve.memset(phase_im[:, :, 0:1], 0.0).then_inc(phase_v, 1)
            ve.wait_ge(phase_v, 1)
            n, k = 1, 0
            link(tt(pr(16), pr(MAG), pr(8), ALU.mult))
            link(tt(pr(17), pr(MAG), pr(9), ALU.mult))
            ve.wait_ge(rot_done, JOB["X3"] + 1)
            while n < T:
                ar = pr(8 + 2 * (k % 2))
                ai = pr(9 + 2 * (k % 2))
                lo_re, lo_im = phase_re[:, :, 0:n], phase_im[:, :, 0:n]
                t1 = mixed[:, :, :].rearrange("p k t -> p (k t)")[:, 0:NCH * n].rearrange("p (c t) -> p c t", c=NCH)
                t2 = xs[:, :, :].rearrange("p k t -> p (k t)")[:, 0:NCH * n].rearrange("p (c t) -> p c t", c=NCH)
                if k:
                    ve.wait_ge(phase_p, k)
                tt(t1, lo_re, ar.unsqueeze(2).to_broadcast([P, NCH, n]), ALU.mult)
                link(tt(t2, lo_im, ai.unsqueeze(2).to_broadcast([P, NCH, n]), ALU.mult))
                link(tt(phase_re[:, :, n:2 * n], t1, t2, ALU.subtract))
                if 2 * n < T:
                    nr, ni = pr(8 + 2 * ((k + 1) % 2)), pr(9 + 2 * ((k + 1) % 2))
                    tt(pr(12), ar, ar, ALU.mult)
                    tt(pr(13), ai, ai, ALU.mult)
                    link(tt(pr(14), ar, ai, ALU.mult))
                    tt(nr, pr(12), pr(13), ALU.subtract)
                    ve.tensor_scalar(ni, pr(14), 2.0, None, ALU.mult).then_inc(phase_v, 1)
                    ve.wait_ge(phase_v, k + 2)
                n *= 2
                k += 1
            link(ve.tensor_scalar(pr(18), pr(16), -1.0, None, ALU.add))
            tt(pr(12), pr(18), L_RE, ALU.mult)
            link(tt(pr(13), pr(17), L_IM, ALU.mult))
            link(tt(pr(14), pr(12), pr(13), ALU.add))
            tt(pr(12), pr(17), L_RE, ALU.mult)
            link(tt(pr(13), pr(18), L_IM, ALU.mult))
            link(tt(pr(15), pr(12), pr(13), ALU.subtract))
            tt(pr(12), L_RE, L_RE, ALU.mult)
            link(tt(pr(13), L_IM, L_IM, ALU.mult))
            link(tt(pr(19), pr(12), pr(13), ALU.add))
            link(ve.reciprocal(pr(20), pr(19)))
            tt(pr(21), pr(14), pr(20), ALU.mult)
            link(tt(pr(22), pr(15), pr(20), ALU.mult))
            ve.wait_ge(small_t, 3)
            z_re = pr(21).unsqueeze(2).to_broadcast([P, NCH, 32])
            z_im = pr(22).unsqueeze(2).to_broadcast([P, NCH, 32])
            c_re = ps[:, 6, :].rearrange("p (j c) -> p j c", c=32)
            c_im = ps[:, 7, :].rearrange("p (j c) -> p j c", c=32)
            tv = [mixed[:, 2 * n:2 * n + 2, :].rearrange("p k t -> p (k t)").rearrange("p (j c) -> p j c", c=32)
                  for n in range(4)]
            tt(tv[0], c_re, z_re, ALU.mult)
            tt(tv[1], c_im, z_im, ALU.mult)
            tt(tv[2], c_re, z_im, ALU.mult)
            link(tt(tv[3], c_im, z_re, ALU.mult))
            ct = [c_t[n].rearrange("p a (b c) -> p (a b) c", c=32) for n in range(2)]
            tt(ct[0], tv[0], tv[1], ALU.subtract)
            ve.scalar_tensor_tensor(ct[1], tv[2], -1.0, tv[3], ALU.mult, ALU.subtract).then_inc(c_ready, 1)

            pre = phase_re.rearrange("p (a b) t -> p a b t", b=4)
            pim = phase_im.rearrange("p (a b) t -> p a b t", b=4)
            ve.wait_ge(phase_p, 8)
            for i in range(4):
                er, ei = pre[:, :, i, :], pim[:, :, i, :]
                bre = ps[:, 4:6, :].rearrange("p b (j t) -> p (b j) t", t=T)
                bim = ps[:, 6:8, :].rearrange("p b (j t) -> p (b j) t", t=T)
                ve.wait_ge(bu_done, i + 1)
                if i:
                    ve.wait_ge(x_state, i)
                tt(prod[0], bre, er, ALU.mult)
                tt(prod[1], bim, ei, ALU.mult)
                tt(prod[2], bim, er, ALU.mult)
                tt(prod[3], bre, ei, ALU.mult).then_inc(bu_used, 1)
                ve.wait_ge(w_rot, i + 1)
                for a in range(4):
                    j = 4 * a + i
                    decay = par[:, MAG, j:j + 1].to_broadcast([P, T])
                    for s in (state_re, state_im):
                        ins = ve.tensor_tensor_scan(s[:, a, :], decay, s[:, a, :], 0.0, ALU.mult, ALU.add)
                ins.then_inc(scanned, 1)
                ve.wait_ge(scanned, 2 * i + 1)
                tt(prod[0], state_re, er, ALU.mult)
                tt(prod[1], state_im, ei, ALU.mult)
                tt(prod[2], state_im, er, ALU.mult)
                tt(prod[3], state_re, ei, ALU.mult).then_inc(scanned, 1)

            ve.wait_ge(rot_free, JOB["T7"] + 1)

            def rope(c, heads, parts=None):
                src = ptok[:, :, c - C_Q:c - C_Q + 64 * heads].rearrange("p t (h d) -> p t h d", d=64)
                a = mixed[:, :, :].rearrange("p k t -> p (k t)")[:, 0:TT * heads * 64].rearrange(
                    "p (t h d) -> p t h d", t=TT, d=64)
                b = xs[:, :, :].rearrange("p k t -> p (k t)")[:, 0:TT * heads * 64].rearrange(
                    "p (t h d) -> p t h d", t=TT, d=64)
                cb = cos_t.unsqueeze(2).to_broadcast([P, TT, heads, 64])
                sn = sin_t.unsqueeze(2).to_broadcast([P, TT, heads, 32])
                tt(a, src, cb, ALU.mult)
                tt(b[:, :, :, 0:32], src[:, :, :, 32:64], sn, ALU.mult)
                link(tt(b[:, :, :, 32:64], src[:, :, :, 0:32], sn, ALU.mult))
                for hs, dst in parts or [(slice(0, heads), src)]:
                    tt(dst[:, :, :, 0:32], a[:, :, hs, 0:32], b[:, :, hs, 0:32], ALU.subtract)
                    ins = tt(dst[:, :, :, 32:64], a[:, :, hs, 32:64], b[:, :, hs, 32:64], ALU.add)
                ins.then_inc(roped, 1)
                ropes[0] += 1
                ve.wait_ge(roped, ropes[0])
            ropes = [0]
            rope(C_QI, IH)
            rope(C_KI, 1, [(slice(0, 1), ki_two[:, :, n:n + 1, :]) for n in range(2)])
            rope(C_K, NKV)
            qv = ptok[:, :, 0:NH * HD].rearrange("p t (h g d) -> p g t h d", g=2, d=HD)
            rope(C_Q, NH, [(slice(4 * g, 4 * g + 4), qv[:, g]) for g in range(2)])

            ve.wait_ge(y_done, 4)
            for a in range(KS):
                i = ve.scalar_tensor_tensor(y_raw[:, a, :], u_in[:, a, :], vec[:, V_D + a:V_D + a + 1],
                                            ps[:, 2 + a // 2, (a % 2) * T:(a % 2) * T + T], ALU.mult, ALU.add)
            i.then_inc(y_raw_ok, 1)

            wi = ptok[:, :, C_WI - C_Q:C_WI - C_Q + IH]
            link(ve.tensor_scalar(wi, wi, IH ** -0.5 * ID ** -0.5, None, ALU.mult))
            r = 0
            for t in range(TT):
                w = P * (t + 1)
                per = 512 // w
                acc = score[:, t, 0:w]
                for n in range(4 * (t + 1)):
                    ve.wait_ge(rot_free, JOB[f"R{t}_{n}"] + 1)
                    for m in range(per):
                        h = 2 * (n // 2 * per + m) + n % 2
                        s = relu[:, r % 2, m * w:m * w + w]
                        if n == 0 and m == 0:
                            ins = ve.tensor_scalar(acc, s, wi[:, t, h:h + 1], None, ALU.mult)
                        else:
                            ins = ve.scalar_tensor_tensor(acc, s, wi[:, t, h:h + 1], acc, ALU.mult, ALU.add)
                        if m == per - 1:
                            ins.then_inc(relu_used, 1)
                            ve.wait_ge(relu_used, r + 1)
                        else:
                            link(ins)
                    r += 1
            ve.wait_ge(rot_free, JOB["GLU1"] + 1)
            tt(y_ssm, y_gelu, glu_g, ALU.mult).then_inc(y_ssm_ok, 1)
            for t in range(TT):
                w = P * (t + 1)
                link(tt(score[:, t, 0:w], score[:, t, 0:w], causal[:, t, 0:w], ALU.add))
                src = score[:, t, 0:w]
                dst = taken[:, t, 0:w]
                for n in range(NSEL // 8):
                    link(ve.max(stat[:, 24:32], src))
                    link(ve.match_replace(dst, stat[:, 24:32], src, GONE))
                    src = dst
                link(ve.tensor_scalar(dst, dst, GONE, -NEG, ALU.is_equal, ALU.mult))
                link(ve.tensor_scalar(dst, dst, NEG, None, ALU.add))
                link(tt(bias[:, t, 0:w], dst, causal[:, t, 0:w], ALU.min))

            for t in range(TT):
                w = P * (t + 1)
                ve.wait_ge(logit_done, t + 1)
                lg = ps[:, 4:8, :].rearrange("p b (h s) -> p (b h) s", s=T)[:, :, 0:w]
                if t:
                    ve.wait_ge(rot_done, JOB["P0_1"] + 1)
                link(ve.scalar_tensor_tensor(logit[:, :, 0:w], lg, HD ** -0.5,
                                             bias[:, t, 0:w].unsqueeze(1).to_broadcast([P, NH, w]),
                                             ALU.mult, ALU.add))
                ve.tensor_reduce(stat[:, 8:16], logit[:, :, 0:w], AX.X, ALU.max, negate=True).then_inc(row_max, 1)
                ve.wait_ge(expd, t + 1)
                link(ve.reciprocal(stat[:, 32:40], stat[:, 16:24]))
                tt(logit[:, :, 0:w], logit[:, :, 0:w],
                   stat[:, 32:40].unsqueeze(2).to_broadcast([P, NH, w]), ALU.mult).then_inc(prob_ok, 1)

            ve.wait_ge(rot_done, JOB["P1_3"] + 1)
            ve.wait_ge(att_done, 2)
            for m in range(KD):
                ve.wait_ge(proj_done, m + 1)
                ba = ps[:, 4 + m % 4, :]
                t1, t2 = xs[:, m % 2, 0:T], xs[:, m % 2, T:2 * T]
                tt(t1, ba[:, 0:T], gate_s[:, m, :], ALU.mult)
                link(tt(t2, ba[:, T:2 * T], gate_a[:, m, :], ALU.mult))
                tt(mixed[:, m, :], t1, t2, ALU.add).then_inc(mixed_ok, 1)
            for n in range(4):
                ve.wait_ge(wout_done, n + 1)
                part = x[:, :, 256 * n:256 * n + 256]
                tt(part, part, ps[:, n, :].rearrange("p (t c) -> p t c", t=TT), ALU.add).then_inc(x1_ok, 1)
            rstd(1)
            for t in range(TT):
                ve.tensor_scalar(xs[:, t, :], x[:, t, :], stat[:, 6 + t:7 + t], None, ALU.mult).then_inc(x_norm, 1)

            ve.wait_ge(rlogit, 1)
            ve.wait_ge(misc_in, 32)
            link(tt(rlog, ps[:, 2, 0:TT * NE].rearrange("p (t e) -> p t e", t=TT),
                    b_rout[:, :].unsqueeze(1).to_broadcast([P, TT, NE]), ALU.add))
            for t in range(TT):
                link(ve.max(top8[:, t, :], rlog[:, t, :]))
                link(ve.max_index(top8i[:, t, :], top8[:, t, :], rlog[:, t, :]))
            link(ve.tensor_copy(top8f, top8i))
            tt(topw[:, :, 0:TOPE], top8[:, :, 0:TOPE], top8[:, :, 0:1].to_broadcast([P, TT, TOPE]),
               ALU.subtract).then_inc(top_ok, 1)
            for t in range(TT):
                ins = tt(hot4[:, t], exp_no.unsqueeze(1).to_broadcast([P, TOPE, NE]),
                         top8f[:, t, 0:TOPE].unsqueeze(2).to_broadcast([P, TOPE, NE]), ALU.is_equal)
            link(ins)
            ve.tensor_reduce(picked, hot4.rearrange("p t k e -> p t e k"), AX.X, ALU.add).then_inc(picked_ok, 1)
            ve.wait_ge(top_exp, 1)
            link(ve.tensor_reduce(stat[:, 40:42], topw[:, :, 0:TOPE], AX.X, ALU.add))
            link(ve.reciprocal(stat[:, 42:44], stat[:, 40:42]))
            link(tt(topw[:, :, 0:TOPE], topw[:, :, 0:TOPE],
                    stat[:, 42:44].unsqueeze(2).to_broadcast([P, TT, TOPE]), ALU.mult))
            for t in range(TT):
                ins = tt(hot4w[:, t], hot4[:, t], topw[:, t, 0:TOPE].unsqueeze(2).to_broadcast([P, TOPE, NE]),
                         ALU.mult)
            link(ins)
            ve.tensor_reduce(gates, hot4w.rearrange("p t k e -> p t e k"), AX.X, ALU.add).then_inc(route_ok, 1)
            ve.wait_ge(placed, 1)
            link(ve.scalar_tensor_tensor(place, ps[:, 3, 0:TT * NE].rearrange("p (t e) -> p t e", t=TT), FAR,
                                         picked, ALU.add, ALU.mult))
            ve.tensor_scalar(place, place, -FAR, None, ALU.add).then_inc(place_ok, 1)
            link(ve.tensor_reduce(stat[0:1, 44:45], ps[0:1, 3, 64:64 + NE], AX.X, ALU.max))
            ve.tensor_copy(flag[:, :], stat[0:1, 44:45]).then_inc(flag_ok, 1)
            ve.wait_ge(gates_tr, 1)
            ve.tensor_copy(gates_t, ps[0:NE, 2, P:P + T]).then_inc(gates_t_ok, 1)

            def one_pass(c, first):
                if not isinstance(c, int):
                    ve.tensor_scalar(place, place, -float(SLOTS), None, ALU.add).then_inc(place_ok, 1)
                    ve.wait_ge(place_ok, c + 1)
                else:
                    ve.wait_ge(place_ok, 1)

                def column(v, e):
                    return v[:, :, bass.ds(e, 1)].to_broadcast([P, TT, SLOTS])

                slots = slot_no.unsqueeze(1).to_broadcast([P, TT, SLOTS])

                def choose(e):
                    tt(one_hot, slots, column(place, e), ALU.is_equal).then_inc(hot_ok, 1)

                def pick_bias(e):
                    ve.tensor_copy(chosen, ident[0:NE, bass.ds(e, 1)].to_broadcast([NE, SLOTS])).then_inc(chosen_ok, 1)

                def take(j):
                    ve.wait_ge(h_trans, j + 1)
                    tt(h_sel, ps[:, 3, :].rearrange("p (j q s) -> p j q s", q=2, s=SLOTS),
                       vec[:, V_G2:V_G2 + KD].rearrange("p (q j) -> p j q", q=2).unsqueeze(3).to_broadcast(
                           [P, 4, 2, SLOTS]), ALU.mult).then_inc(h_sel_ok, 1)

                def weigh(j, e):
                    for q in range(2):
                        ins = tt(gated[:, :, q], slots, column(place, e), ALU.is_equal)
                    ins.then_inc(gated_eq, 1)
                    ve.wait_ge(gated_eq, j + 1)
                    for q in range(2):
                        ins = tt(gated[:, :, q], gated[:, :, q], column(gates, e), ALU.mult)
                    ins.then_inc(gated_ok, 1)

                def body(j, e, tail=False):
                    if not tail:
                        choose(e + 1)
                    ve.wait_ge(chunk_used, j * NW + NW_IN)
                    z = ps[:, 0:2, :].rearrange("p b (c g) -> p g (b c)", g=2)
                    ve.tensor_scalar(gate_z, z[:, 0], LIMIT, None, ALU.min).then_inc(z_gate, 1)
                    ve.tensor_scalar(lin_z, z[:, 1], LIMIT, -LIMIT, ALU.min, ALU.max).then_inc(z_lin, 1)
                    ve.wait_ge(z_lin, j + 1)
                    ve.scalar_tensor_tensor(act, lin_z, 1.0, gate_z, ALU.add, ALU.mult).then_inc(z_prod, 1)
                    ve.wait_ge(z_prod, j + 1)
                    ve.wait_ge(sig_ok, j + 1)
                    tt(act, act, sig, ALU.mult).then_inc(act_ok, 1)
                    weigh(j, e)
                    if not tail:
                        pick_bias(e + 1)
                        take(j + 1)
                    ve.wait_ge(gated_trans, j + 1)
                    ve.tensor_copy(gated_t, ps[:, 1, 0:T]).then_inc(gated_t_ok, 1)

                choose(0)
                pick_bias(0)
                take(first)
                body(first, 0)
                with ve.Fori(1, NE - 1) as e:
                    body(e + first, e)
                body(first + NE - 1, NE - 1, tail=True)
            passes(ve, one_pass)

            ve.wait_ge(sum_ok, 1)
            for t in range(TT):
                tt(x[:, t, :], x[:, t, :], ps[:, 4 + 2 * t:6 + 2 * t, :].rearrange("p b n -> p (b n)"),
                   ALU.add).then_inc(x1_ok, 1)
            rstd(2)
            chunk_arrived(ve, "GAIN")
            for t in range(TT):
                link(ve.tensor_scalar(final[:, t, :], x[:, t, :], stat[:, 6 + t:7 + t], None, ALU.mult))
                tt(final[:, t, :], final[:, t, :], gfin, ALU.mult).then_inc(out_ready, 1)

        @block.tensor
        def _(pe):
            def job(name):
                n = JOB[name]
                if n >= 2:
                    pe.wait_ge(rot_free, n - 1)
                return rot[n % 2]

            pe.wait_ge(tables_in, 16)
            pe.wait_ge(vec_in, 16 * 8)
            pe.wait_ge(small_free, 1)
            pe.transpose(ps[:, 7, 0:72], vec_rows[:, :], ident[0:72, 0:72])
            pe.transpose(ps[:, 7, 128:128 + NCH], dt_rows[:, :], ident[0:NCH, 0:NCH]).then_inc(small_t, 1)
            def norm_t(letter, first):
                for n in range(4):
                    b = job(f"{letter}{n}")
                    for k in (2 * n, 2 * n + 1):
                        for t in range(TT):
                            pe.wait_ge(x_norm, first + t + 1)
                            i = pe.transpose(b[:, (k % 2) * T + t * P:(k % 2) * T + t * P + P],
                                             xs[:, t, k * P:k * P + P], ident)
                    i.then_inc(rot_done, 1)

            norm_t("X", 0)
            pe.wait_ge(bnat_in, 16 * 4)
            for n in range(2):
                for a in range(4):
                    i = pe.transpose(ps[:, 4 + n, a * P:a * P + P], b_nat[n][:, a, :], ident)
            i.then_inc(small_t, 1)
            pe.wait_ge(cnat_in, 16 * 16)
            pe.wait_ge(small_free, 2)
            for n in range(2):
                for a in range(4):
                    i = pe.transpose(ps[:, 6 + n, a * P:a * P + P], c_nat[n][:, a, :], ident)
            i.then_inc(small_t, 1)

            def feature_job(name, src, kt, first_m, slot):
                b = job(name)
                for m in range(2):
                    for k in range(kt):
                        i = pe.matmul(b[:, m * T:m * T + T], slot[:, k, (first_m + m) * P:(first_m + m + 1) * P],
                                      src[:, k, :], start=(k == 0), stop=(k == kt - 1))
                i.then_inc(rot_done, 1)

            for n in range(2):
                chunk_arrived(pe, f"U{n}")
                if n == 0:
                    pe.wait_ge(rot_free, JOB["X3"] + 1)
                feature_job(f"U{n}", x_t, KD, 0, chunk_view(f"U{n}")[0])

            def bu(i):
                if i == 0:
                    pe.wait_ge(small_free, 3)
                    pe.wait_ge(c_ready, 1)
                    pe.wait_ge(rot_free, JOB["U1"] + 1)
                else:
                    pe.wait_ge(bu_used, i)
                for n in range(2):
                    for a in range(4):
                        ins = pe.matmul(ps[:, 4 + 2 * n + a // 2, (a % 2) * T:(a % 2) * T + T],
                                        b_t[n][32 * i:32 * i + 32, a, :], u_in[32 * i:32 * i + 32, a, :],
                                        start=True, stop=True)
                ins.then_inc(bu_done, 1)

            def y_out(i):
                pe.wait_ge(x_state, i + 1)
                for a in range(4):
                    o_ = ps[32 * i:32 * i + 32, 2 + a // 2, (a % 2) * T:(a % 2) * T + T]
                    pe.matmul(o_, c_t[0][:, a, 32 * i:32 * i + 32], xs_re[:, a, :], start=True, stop=False)
                    ins = pe.matmul(o_, c_t[1][:, a, 32 * i:32 * i + 32], xs_im[:, a, :], start=False, stop=True)
                ins.then_inc(y_done, 1)

            def token_job(n):
                w = TOK[n][1]
                chunk_arrived(pe, f"T{n}")
                slot = chunk_view(f"T{n}")[0]
                b = job(f"T{n}")
                for t in range(TT):
                    for k in range(KD):
                        i = pe.matmul(b[:, t * w:t * w + w], x_t[:, k, t * P:t * P + P], slot[:, k, :],
                                      start=(k == 0), stop=(k == KD - 1))
                i.then_inc(rot_done, 1)

            for n in range(4):
                token_job(n)
            bu(0)
            token_job(4)
            token_job(5)
            bu(1)
            y_out(0)
            token_job(6)
            bu(2)
            y_out(1)
            token_job(7)
            bu(3)
            y_out(2)
            for n in range(4):
                chunk_arrived(pe, f"S{n}")
                feature_job(f"S{n}", x_t, KD, 0, chunk_view(f"S{n}")[0])
                if n == 1:
                    y_out(3)

            def trans_job(name, cols_of):
                b = job(name)
                for n, c in enumerate(cols_of):
                    for t in range(TT):
                        i = pe.transpose(b[:, n * T + t * P:n * T + t * P + P], c(t), ident)
                i.then_inc(rot_done, 1)

            pe.wait_ge(roped, 4)
            q0 = C_QI - C_Q
            for n in range(4):
                trans_job(f"QI{n}", [lambda t, k=k: ptok[:, t, q0 + k * P:q0 + k * P + P] for k in (2 * n, 2 * n + 1)])
            b = job("KK")
            for t in range(TT):
                pe.transpose(b[:, t * P:t * P + P],
                             ki_two[:, t].rearrange("p n d -> p (n d)"), ident)
            for t in range(TT):
                i = pe.transpose(b[:, T + t * P:T + t * P + P], ptok[:, t, C_K - C_Q:C_K - C_Q + P], ident)
            i.then_inc(rot_done, 1)
            for n in range(2):
                trans_job(f"Q{n}", [lambda t, k=k: ptok[:, t, k * P:k * P + P] for k in (2 * n, 2 * n + 1)])

            pe.wait_ge(rot_free, JOB["KK"] + 1)
            for t in range(TT):
                w = P * (t + 1)
                per = 512 // w
                for n in range(4 * (t + 1)):
                    b = job(f"R{t}_{n}")
                    for m in range(per):
                        h = 2 * (n // 2 * per + m) + n % 2
                        r = slice(64 * (h % 2), 64 * (h % 2) + 64)
                        i = pe.matmul(b[:, m * w:m * w + w], qi_t[r, h // 2, t * P:t * P + P], ki_t[r, 0:w],
                                      start=True, stop=True)
                    i.then_inc(rot_done, 1)

            chunk_arrived(pe, "GLU")
            pe.wait_ge(gelu_ok, 1)
            for n in range(2):
                feature_job(f"GLU{n}", y_gelu, KS, 2 * n, chunk_view("GLU")[0])
            for n in range(4):
                chunk_arrived(pe, f"A{n}")
                feature_job(f"A{n}", x_t, KD, 0, chunk_view(f"A{n}")[0])

            pe.wait_ge(rot_free, JOB["Q1"] + 1)

            def logits(t):
                w = P * (t + 1)
                if t:
                    pe.wait_ge(row_max, t)
                for h in range(NH):
                    r = slice(64 * (h // 4), 64 * (h // 4) + 64)
                    i = pe.matmul(ps[:, 4 + h // 2, (h % 2) * T:(h % 2) * T + w], q_t[r, h % 4, t * P:t * P + P],
                                  k_t[r, 0:w], start=True, stop=True)
                i.then_inc(logit_done, 1)

            logits(0)
            v0 = C_V - C_Q
            for t in range(TT):
                pe.wait_ge(prob_ok, t + 1)
                for n in range(2 * (t + 1)):
                    b = job(f"P{t}_{n}")
                    for m in range(4):
                        at = 4 * n + m
                        h, s = at // (t + 1), at % (t + 1)
                        i = pe.transpose(b[:, m * P:m * P + P], logit[:, h, s * P:s * P + P], ident)
                    i.then_inc(rot_done, 1)
                if t == 0:
                    logits(1)
                pe.wait_ge(rot_free, JOB[f"P{t}_{2 * t + 1}"] + 1)
                if t == 0:
                    pe.wait_ge(y_raw_ok, 1)
                for h in range(NH):
                    for s in range(t + 1):
                        at = h * (t + 1) + s
                        base = 64 * (h % 2)
                        i = pe.matmul(ps[base:base + 64, 2 + t, (h // 2) * P:(h // 2) * P + P],
                                      ptok[:, s, v0 + 64 * (h // 4):v0 + 64 * (h // 4) + 64],
                                      prob_t[:, at * P:at * P + P], start=(s == 0), stop=(s == t))
                i.then_inc(att_done, 1)

            pe.wait_ge(y_ssm_ok, 1)
            pe.wait_ge(att_out, 2)
            for m in range(KD):
                if m % 4 == 0:
                    chunk_arrived(pe, f"PS{m // 4}")
                    chunk_arrived(pe, f"PA{m // 4}")
                if m < 4:
                    pe.wait_ge(row_max, 2)
                else:
                    pe.wait_ge(mixed_ok, m - 3)
                b = ps[:, 4 + m % 4, :]
                for n, (name, y) in enumerate((("PS", y_ssm), ("PA", y_att))):
                    slot = chunk_view(f"{name}{m // 4}")[0]
                    for k in range(KS):
                        i = pe.matmul(b[:, n * T:n * T + T], slot[:, k, (m % 4) * P:(m % 4) * P + P], y[:, k, :],
                                      start=(k == 0), stop=(k == KS - 1))
                i.then_inc(proj_done, 1)
            pe.wait_ge(mixed_ok, KD)
            for n in range(4):
                chunk_arrived(pe, f"W{n}")
                slot = chunk_view(f"W{n}")[0]
                for t in range(TT):
                    for k in range(KD):
                        i = pe.matmul(ps[:, n, t * T:t * T + 256], mixed[:, k, t * P:t * P + P], slot[:, k, :],
                                      start=(k == 0), stop=(k == KD - 1))
                i.then_inc(wout_done, 1)

            pe.wait_ge(x1_ok, 4)
            norm_t("HX", TT)
            pe.wait_ge(rot_free, JOB["HX3"] + 1)
            pe.wait_ge(misc_in, 32)
            for t in range(TT):
                for k in range(KD):
                    i = pe.matmul(ps[:, 2, t * NE:t * NE + NE], x_t[:, k, t * P:t * P + P], w_rout[:, k, :],
                                  start=(k == 0), stop=(k == KD - 1))
            i.then_inc(rlogit, 1)
            pe.wait_ge(picked_ok, 1)
            pe.matmul(ps[:, 3, 0:NE], tri, picked[:, 0, :], start=True, stop=True)
            pe.matmul(ps[:, 3, NE:2 * NE], ones, picked[:, 0, :], start=True, stop=False)
            pe.matmul(ps[:, 3, NE:2 * NE], tri, picked[:, 1, :], start=False, stop=True)
            pe.matmul(ps[:, 3, 2 * NE:3 * NE], ones, picked[:, 0, :], start=True, stop=False)
            pe.matmul(ps[:, 3, 2 * NE:3 * NE], ones, picked[:, 1, :], start=False, stop=True).then_inc(placed, 1)
            pe.wait_ge(route_ok, 1)
            for t in range(TT):
                i = pe.transpose(ps[0:NE, 2, P + t * P:P + t * P + P], gates[:, t, :], ident)
            i.then_inc(gates_tr, 1)
            pe.wait_ge(gates_t_ok, 1)
            chunk_arrived(pe, "BIAS")
            chunk_arrived(pe, "BIN")
            for t in range(TT):
                for n in range(2):
                    pe.matmul(ps[:, 4 + 2 * t + n, :], gates_t[:, t * P:t * P + P],
                                  b_out[:, 512 * n:512 * n + 512], start=True, stop=False, skip_group_check=True)

            def one_pass(c, first):
                def gather(j):
                    pe.wait_ge(hot_ok, j + 1)
                    for t in range(TT):
                        for q in range(2):
                            i = pe.matmul(ps[64 * q:64 * q + SLOTS, 3, :], one_hot[:, t, :],
                                          xs[:, t, 512 * q:512 * q + 512], start=(t == 0), stop=(t == TT - 1))
                    i.then_inc(gathered, 1)

                def gather_t(j):
                    pe.wait_ge(h_tok_ok, j + 1)
                    for n in range(4):
                        i = pe.transpose(ps[:, 3, n * P:n * P + P], h_tok[:, n * P:n * P + P], ident)
                    i.then_inc(h_trans, 1)

                def scatter(j):
                    pe.wait_ge(y_tok_ok, j + 1)
                    for t in range(TT):
                        for q in range(2):
                            r = slice(64 * q, 64 * q + SLOTS)
                            pe.matmul(ps[:, 4 + 2 * t + q, :], gated_t[r, t * P:t * P + P], y_tok[r, :],
                                      start=False, stop=False, skip_group_check=True)

                def body(j, head=False, tail=False):
                    pe.wait_ge(h_sel_ok, j + 1)
                    pe.wait_ge(chosen_ok, j + 1)
                    if not head:
                        pe.wait_ge(gated_t_ok, j)
                    for n in range(4):
                        r = slice(64 * (n % 2), 64 * (n % 2) + SLOTS)
                        pe.matmul(ps[r, n // 2, :], chosen, b_in[:, 512 * n:512 * n + 512], start=True, stop=False)
                    for k in range(KD):
                        pe.wait_ge(moe_in[k], 16 * j + 16)
                        w = ring[:, k * SW:(k + 1) * SW]
                        for n in range(4):
                            r = slice(64 * (n % 2), 64 * (n % 2) + SLOTS)
                            i = pe.matmul(ps[r, n // 2, :], h_sel[:, k % 4, k // 4, :], w[:, 512 * n:512 * n + 512],
                                          start=False, stop=(k == KD - 1))
                        i.then_inc(chunk_used, 1)
                    if not head:
                        scatter(j - 1)
                    if not tail:
                        gather(j + 1)
                    pe.wait_ge(act_ok, j + 1)
                    for n in range(4):
                        i = pe.transpose(ps[:, 0, n * P:n * P + P], act[:, n * P:n * P + P], ident)
                    i.then_inc(act_trans, 1)
                    pe.wait_ge(gated_ok, j + 1)
                    for t in range(TT):
                        i = pe.transpose(ps[:, 1, t * P:t * P + P], gated[:, t].rearrange("p q s -> p (q s)"), ident)
                    i.then_inc(gated_trans, 1)
                    if not tail:
                        gather_t(j + 1)
                    pe.wait_ge(act_t_ok, j + 1)
                    for k in range(KF):
                        c_ = NW_IN + k // 2
                        if k % 2 == 0:
                            pe.wait_ge(moe_in[c_], 16 * j + 16)
                        w = ring[:, c_ * SW + (k % 2) * D:c_ * SW + (k % 2) * D + D]
                        for q in range(2):
                            i = pe.matmul(ps[64 * q:64 * q + SLOTS, 2, :], act_tile(k), w[:, 512 * q:512 * q + 512],
                                          start=(k == 0), stop=(k == KF - 1))
                        if k % 2:
                            i.then_inc(chunk_used, 1)

                gather(first)
                gather_t(first)
                body(first, head=True)
                with pe.Fori(1, NE - 1) as e:
                    body(e + first)
                body(first + NE - 1, tail=True)
                pe.wait_ge(gated_t_ok, first + NE)
                scatter(first + NE - 1)
            passes(pe, one_pass)
            pe.matmul(ps[0:1, 3, 0:1], ones[0:1, 0:1], ones[0:1, 0:1], start=True, stop=True).then_inc(sum_ok, 1)


_INS = ["x", "norm1_g", "w_in", "b_gate", "ssm_lam_re", "ssm_lam_im", "ssm_log_dt", "ssm_b_re", "ssm_b_im",
        "ssm_c_re", "ssm_c_im", "ssm_d", "w_glu", "b_glu", "w_proj_ssm", "w_proj_attn", "w_out", "norm2_g",
        "w_router", "b_router", "w_moe_in", "b_moe_in", "w_moe_out", "b_moe_out", "norm_f_g"]
_FLAT = {"norm1_g", "b_gate", "ssm_lam_re", "ssm_lam_im", "ssm_log_dt", "ssm_d", "b_glu", "norm2_g", "b_router",
         "norm_f_g"}


def kernel(**inputs):
    import concourse.bacc as _bacc
    from concourse.bass_utils import run_bass_kernel_spmd as _run

    nc = _bacc.Bacc("TRN2", target_bir_lowering=False, num_devices=1)
    arrays, io = {}, {}
    for name in _INS + ["tables"]:
        if name == "tables":
            a = constant_tables()
        else:
            a = np.ascontiguousarray(inputs[name])
            if name in _FLAT:
                a = a.reshape(-1)
            elif name != "norm_f_g":
                a = a.reshape(a.shape[1:])
        arrays[f"in_{name}"] = a
        io[name] = nc.dram_tensor(f"in_{name}", a.shape, mybir.dt.from_np(a.dtype), kind="ExternalInput").ap()
    out = nc.dram_tensor("out_0", (T, D), mybir.dt.float32, kind="ExternalOutput").ap()
    build(nc, io, out)
    r = _run(nc, [arrays], core_ids=[0])
    return r.results[0]["out_0"].reshape(1, T, D)
```

```python
import math
from contextlib import ExitStack

import numpy as np

import concourse.bass as bass
from concourse import mybir

P = 128
T = 256
TT = T // P
D = 1024
KD = D // P
DS = 512
KS = DS // P
G, PS, H = 32, 64, 16
NCH = G * PS // P
NH, NKV, HD = 8, 2, 64
IH, ID = 16, 64
NSEL = min(256, T // 4)
NE, TOPE, F = 32, 4, 1024
KF = F // P
LIMIT, ALPHA = 7.0, 1.702
EPS = 1e-5
NEG = -1e30
GONE = -3e38
FAR = 1024.0
SLOTS = 64
PASSES = T // SLOTS
TWO_PI = 2.0 * math.pi

C_U, C_Q, C_K, C_V, C_QI, C_KI, C_WI, C_GS, C_GA, C_END = 0, 512, 1024, 1152, 1280, 2304, 2368, 2384, 3408, 4432
TOK = [(C_QI + 221 * n, min(221, C_GS - C_QI - 221 * n)) for n in range(5)] \
    + [(C_K, 256), (C_Q, 256), (C_Q + 256, 256)]
NTOK = C_GS - C_Q

TB_ID, TB_COS, TB_SIN, TB_SLOT, TB_EXP, TB_TRI, TB_ONE, TB_CAUSAL, TB_END = \
    [int(v) for v in np.cumsum([0, P, TT * 64, TT * 32, SLOTS, NE, P, P, TT * T])]


def constant_tables():
    t = np.zeros((P, TB_END), np.float32)
    t[:, TB_ID:TB_ID + P] = np.eye(P)
    inv = (np.float32(10000.0) ** (-np.arange(32, dtype=np.float32) / np.float32(32))).astype(np.float32)
    pos = np.arange(T, dtype=np.float32)
    ang = (pos[:, None] * inv[None, :]).astype(np.float32).astype(np.float64)
    cos, sin = np.cos(ang).astype(np.float32), np.sin(ang).astype(np.float32)
    for tt in range(TT):
        rows = slice(tt * P, tt * P + P)
        t[:, TB_COS + 64 * tt:TB_COS + 64 * tt + 64] = np.concatenate([cos[rows], cos[rows]], 1)
        t[:, TB_SIN + 32 * tt:TB_SIN + 32 * tt + 32] = sin[rows]
        t[:, TB_CAUSAL + T * tt:TB_CAUSAL + T * tt + T] = np.where(
            np.arange(T)[None, :] <= (tt * P + np.arange(P))[:, None], 0.0, NEG)
    t[:, TB_SLOT:TB_SLOT + SLOTS] = np.arange(SLOTS)
    t[:, TB_EXP:TB_EXP + NE] = np.arange(NE)
    t[:, TB_TRI:TB_TRI + P] = np.arange(P)[:, None] < np.arange(P)[None, :]
    t[:, TB_ONE:TB_ONE + P] = 1.0
    return t


JOBS = (["X0", "X1", "X2", "X3", "U0", "U1", "T0", "T1", "T2", "T3", "T4", "T5", "T6", "T7"]
        + ["S0", "S1", "S2", "S3", "QI0", "QI1", "QI2", "QI3", "KK", "Q0", "Q1"]
        + [f"R0_{n}" for n in range(4)] + [f"R1_{n}" for n in range(8)]
        + ["A0", "GLU0", "GLU1", "A1", "P0_0", "P0_1", "A2", "A3", "PS0", "PS1", "PS2", "PS3"]
        + [f"P1_{n}" for n in range(4)] + ["HX0", "HX1", "HX2", "HX3"])
JOB = {name: n for n, name in enumerate(JOBS)}

CHUNKS = (["U0", "U1"] + [f"T{n}" for n in range(8)] + [f"S{n}" for n in range(4)] + ["A0", "GLU", "A1", "A2", "A3"]
          + ["PS0", "PS1", "PA0", "PA1"] + [f"W{n}" for n in range(4)]
          + ["GAIN", "BIAS", "BIN"])
CHUNK = {name: n for n, name in enumerate(CHUNKS)}
NSLOT = 4
SLOT = {name: n % NSLOT for n, name in enumerate(CHUNKS)}
SLOT["BIAS"], SLOT["BIN"] = SLOT["GAIN"], (SLOT["GAIN"] + 1) % NSLOT


def loads_until(name):
    last = CHUNK["BIAS" if name == "GAIN" else name]
    return sum(1 for c in CHUNKS[:last + 1] if SLOT[c] == SLOT[name])


def before(name):
    return [c for c in CHUNKS[:CHUNK[name]] if SLOT[c] == SLOT[name] and c != "GAIN"][-1]


def build(nc, io, out):
    fp32, i32, u32 = mybir.dt.float32, mybir.dt.int32, mybir.dt.uint32
    ALU, ACT, AX = mybir.AluOpType, mybir.ActivationFunctionType, mybir.AxisListType

    with ExitStack() as ctx:
        def sb(name, shape, dt=fp32):
            return ctx.enter_context(nc.sbuf_tensor(name, shape, dt))

        def sem(name):
            return ctx.enter_context(nc.semaphore(name))

        SW = 2048
        NW_IN, NW_OUT = KD, KF // 2
        NW = NW_IN + NW_OUT
        ring = sb("ring", [P, NW * SW])

        def early(at, *dims):
            n = int(np.prod(dims))
            v = ring[:, at:at + n]
            if len(dims) == 2:
                v = v.rearrange("p (a b) -> p a b", a=dims[0])
            return v

        phase_re, phase_im = early(0, NCH, T), early(NCH * T, NCH, T)
        prod = [early(2 * NCH * T + n * 4 * T, 4, T) for n in range(4)]
        state_re, state_im = early(12288, 4, T), early(13312, 4, T)
        xs_re, xs_im = early(14336, 4, T), early(15360, 4, T)
        b_nat = [early(14336 + 512 * n, 4, P) for n in range(2)]
        c_nat = [early(15360 + 512 * n, 4, P) for n in range(2)]
        gate_s, gate_a = early(16384, KD, T), early(18432, KD, T)
        prod_out = [early(18432 + n * 4 * T, 4, T) for n in range(4)]
        p_ssm = early(14336, KD, T)
        y_ssm, y_att = early(20480, KS, T), early(21504, KS, T)
        c_t = [early(23552 + 512 * n, 4, P) for n in range(2)]

        table = sb("table", [P, TB_END])
        x = sb("x", [P, TT, D])
        xs = sb("xs", [P, TT, D])
        x_t = sb("x_t", [P, KD, T])
        wbuf = sb("wbuf", [P, NSLOT, SW])
        mixed = sb("mixed", [P, KD, T])
        u_in = sb("u_in", [P, KS, T])
        gfin = wbuf[:, SLOT["GAIN"], 0:D]
        b_out = wbuf[0:NE, SLOT["BIAS"], D:2 * D]
        b_in = wbuf[:, SLOT["BIN"], :]
        vec_rows = sb("vec_rows", [72, P])
        dt_rows = sb("dt_rows", [NCH, P])
        dt_pair = sb("dt_pair", [NCH, 2])
        vec = sb("vec", [P, 72])
        par = sb("par", [P, 24, NCH])
        stat = sb("stat", [P, 64])
        w_rout = sb("w_rout", [P, KD, NE])
        b_rout = sb("b_rout", [P, NE])
        late = sb("late", [P, 7840])
        flag = sb("flag", [1, 1], i32)

        ident = table[:, TB_ID:TB_ID + P]
        cos_t = table[:, TB_COS:TB_COS + TT * 64].rearrange("p (t d) -> p t d", t=TT)
        sin_t = table[:, TB_SIN:TB_SIN + TT * 32].rearrange("p (t d) -> p t d", t=TT)
        slot_no = table[:, TB_SLOT:TB_SLOT + SLOTS]
        exp_no = table[:, TB_EXP:TB_EXP + NE]
        tri = table[:, TB_TRI:TB_TRI + P]
        ones = table[:, TB_ONE:TB_ONE + P]
        causal = table[:, TB_CAUSAL:TB_CAUSAL + TT * T].rearrange("p (t s) -> p t s", t=TT)

        V_G1, V_G2, V_BG, V_BGLU, V_D, V_LR, V_LI = 0, 8, 16, 32, 36, 40, 56
        L_RE, L_IM = vec[:, V_LR:V_LR + NCH], vec[:, V_LI:V_LI + NCH]

        ptok = late[:, 0:TT * NTOK].rearrange("p (t n) -> p t n", t=TT)
        o = TT * NTOK
        b_t = [late[:, o + 2048 * n:o + 2048 * n + 2048].rearrange("p (j c) -> p j c", c=P) for n in range(2)]
        score = late[:, o:o + TT * T].rearrange("p (t s) -> p t s", t=TT)
        taken = late[:, o + 512:o + 1024].rearrange("p (t s) -> p t s", t=TT)
        bias = late[:, o + 1024:o + 1536].rearrange("p (t s) -> p t s", t=TT)
        ki_two = late[:, o + 1024:o + 1280].rearrange("p (t n d) -> p t n d", t=TT, n=2)
        relu = late[:, o + 1536:o + 2560].rearrange("p (b s) -> p b s", b=2)
        q_t = late[:, o + 2560:o + 3584].rearrange("p (k t) -> p k t", k=4)
        k_t = early(22528, 2, T)
        ki_t = late[:, o + 3584:o + 4096].rearrange("p (n s) -> p n s", n=2)
        rope_a, rope_b = mixed, xs
        qi_t = xs[:, :, :].rearrange("p t (k s) -> p (t k) s", s=T)
        logit = xs[:, :, :].rearrange("p t (h s) -> p (t h) s", s=T)
        prob_t = mixed[:, :, :].rearrange("p k t -> p (k t)")
        glu_g = prod[0]
        y_raw, y_gelu = prod[2], prod[3]

        def cut(at, n):
            return late[:, at:at + n]
        h_tok, gate_z, lin_z, sig, act = [cut(512 * n, 512) for n in range(5)]
        h_sel = cut(2560, 512).rearrange("p (j q s) -> p j q s", q=2, s=SLOTS)
        act_t = cut(3072, 512).rearrange("p (j q s) -> p j q s", q=2, s=SLOTS)
        y_tok = cut(3584, 512)
        gated = cut(4096, TT * 2 * SLOTS).rearrange("p (t q s) -> p t q s", t=TT, q=2)
        gated_t = cut(6208, 2 * T).rearrange("p (q t) -> p q t", q=2)
        one_hot = cut(4608, TT * SLOTS).rearrange("p (t s) -> p t s", t=TT)
        chosen = cut(4736, SLOTS)

        def act_tile(k):
            return act_t[:, 2 * (k // 4) + k % 2, k // 2 % 2, :]
        place = cut(5120, TT * NE).rearrange("p (t e) -> p t e", t=TT)
        gates = cut(5184, TT * NE).rearrange("p (t e) -> p t e", t=TT)
        picked = cut(5248, TT * NE).rearrange("p (t e) -> p t e", t=TT)
        rlog = cut(5312, TT * NE).rearrange("p (t e) -> p t e", t=TT)
        top8 = cut(5376, TT * 8).rearrange("p (t k) -> p t k", t=TT)
        top8i = late[:, 5392:5392 + TT * 8].bitcast(u32).rearrange("p (t k) -> p t k", t=TT)
        top8f = cut(5408, TT * 8).rearrange("p (t k) -> p t k", t=TT)
        topw = cut(5424, TT * 8).rearrange("p (t k) -> p t k", t=TT)
        hot4 = cut(5440, TT * TOPE * NE).rearrange("p (t k e) -> p t k e", t=TT, k=TOPE)
        hot4w = cut(5696, TT * TOPE * NE).rearrange("p (t k e) -> p t k e", t=TT, k=TOPE)
        rsum = cut(4352, T)
        gates_t = late[0:NE, 5952:5952 + T]
        final = xs

        ps = ctx.enter_context(nc.psum_tensor("ps", [P, 8, 512], fp32))
        rot = [ps[:, 0, :], ps[:, 1, :]]

        NX = 4
        extra = [wbuf[:, SLOT["W2"], :], wbuf[:, SLOT["W3"], :],
                 mixed[:, :, :].rearrange("p k t -> p (k t)"),
                 x_t[:, :, :].rearrange("p k t -> p (k t)")]

        tables_in, x_in, vec_in, misc_in, bnat_in, cnat_in = [sem(n) for n in (
            "tables_in", "x_in", "vec_in", "misc_in", "bnat_in", "cnat_in")]
        w_slot_in = [sem(f"w_slot_in{n}") for n in range(NSLOT)]
        zeroed = sem("zeroed")
        sum_sq, root, x_norm = sem("sum_sq"), sem("root"), sem("x_norm")
        rot_done, rot_free = sem("rot_done"), sem("rot_free")
        small_t, small_free = sem("small_t"), sem("small_free")
        par_v, par_s = sem("par_v"), sem("par_s")
        b_ready, c_ready = sem("b_ready"), sem("c_ready")
        bu_done, bu_used, w_rot, scanned, x_state, y_done, y_raw_ok = [sem(n) for n in (
            "bu_done", "bu_used", "w_rot", "scanned", "x_state", "y_done", "y_raw_ok")]
        phase_v, phase_p = sem("phase_v"), sem("phase_p")
        roped = sem("roped")
        relu_used = sem("relu_used")
        gelu_ok, y_ssm_ok = sem("gelu_ok"), sem("y_ssm_ok")
        logit_done, logit_used, row_max, expd, prob_ok, att_done, att_out = [sem(n) for n in (
            "logit_done", "logit_used", "row_max", "expd", "prob_ok", "att_done", "att_out")]
        gated_a = sem("gated_a")
        proj_done, mixed_ok, wout_done, x1_ok = [sem(n) for n in ("proj_done", "mixed_ok", "wout_done", "x1_ok")]
        rlogit_sb = sem("rlogit_sb")
        rlogit, top_ok, top_exp, picked_ok, placed, route_ok, flag_ok, gates_tr, gates_t_ok = [sem(n) for n in (
            "rlogit", "top_ok", "top_exp", "picked_ok", "placed", "route_ok", "flag_ok", "gates_tr",
            "gates_t_ok")]
        moe_in = [sem(f"moe_in{n}") for n in range(NW)]
        extra_in = [sem(f"extra_in{n}") for n in range(NX)]
        chunk_used = sem("chunk_used")
        hot_ok, gathered, h_tok_ok, h_trans, h_sel_ok, chosen_ok, z_gate, z_lin, sig_ok, z_prod, act_ok, act_trans, \
            act_t_ok, y_tok_ok, gated_eq, gated_ok, gated_trans, gated_t_ok, sum_ok = [sem(n) for n in (
                "hot_ok", "gathered", "h_tok_ok", "h_trans", "h_sel_ok", "chosen_ok", "z_gate", "z_lin", "sig_ok",
                "z_prod", "act_ok", "act_trans", "act_t_ok", "y_tok_ok", "gated_eq", "gated_ok", "gated_trans",
                "gated_t_ok", "sum_ok")]
        place_ok = sem("place_ok")
        out_ready, stored = sem("out_ready"), sem("stored")
        v_chain, a_chain, g_chain = sem("v_chain"), sem("a_chain"), sem("g_chain")

        w_in = io["w_in"].rearrange("(k p) n -> p k n", p=P)
        w_glu = io["w_glu"].rearrange("(k p) n -> p k n", p=P)
        w_ps = io["w_proj_ssm"].rearrange("(k p) n -> p k n", p=P)
        w_pa = io["w_proj_attn"].rearrange("(k p) n -> p k n", p=P)
        w_out = io["w_out"].rearrange("(k p) n -> p k n", p=P)

        def chunk_view(name):
            slot = wbuf[:, SLOT[name], :]
            wide = slot.rearrange("p (k n) -> p k n", k=KD)
            deep = slot.rearrange("p (k n) -> p k n", k=KS)
            if name == "GAIN":
                return gfin, io["norm_f_g"].unsqueeze(0).to_broadcast([P, D])
            if name == "BIN":
                return b_in[0:NE], io["b_moe_in"]
            if name == "BIAS":
                return b_out, io["b_moe_out"]
            n = int(name[-1]) if name != "GLU" else 0
            if name == "GLU":
                return deep, w_glu
            if name[:2] == "PS":
                return deep, w_ps[:, :, 512 * n:512 * n + 512]
            if name[:2] == "PA":
                return deep, w_pa[:, :, 512 * n:512 * n + 512]
            if name[0] == "T":
                c, w = TOK[n]
                return wide[:, :, 0:w], w_in[:, :, c:c + w]
            c = {"U": C_U, "S": C_GS, "A": C_GA}.get(name[0])
            src = w_out if c is None else w_in
            return wide, src[:, :, (c or 0) + 256 * n:(c or 0) + 256 * n + 256]

        def chunk_arrived(eng, name):
            eng.wait_ge(w_slot_in[SLOT[name]], 16 * loads_until(name))

        def chunk_done(name):
            if name == "GLU":
                return rot_done, JOB["GLU1"] + 1
            if name[:2] == "PS":
                return rot_done, JOB[f"PS{2 * int(name[-1]) + 1}"] + 1
            if name[:2] == "PA":
                return proj_done, 2 * (int(name[-1]) + 1)
            if name[0] == "W":
                return wout_done, int(name[1]) + 1
            return rot_done, JOB[name] + 1

        def expert_chunk(e, c):
            if c < NW_IN:
                return io["w_moe_in"][bass.ds(e, 1), c * P:(c + 1) * P, :].rearrange("o p n -> p (o n)")
            r = (c - NW_IN) * 2 * P
            return io["w_moe_out"][bass.ds(e, 1), r:r + 2 * P, :].rearrange("o (k p) n -> p (o k) n", p=P)

        def ring_slot(c):
            v = ring[:, c * SW:(c + 1) * SW]
            return v if c < NW_IN else v.rearrange("p (k n) -> p k n", k=2)

        def passes(eng, one_pass):
            one_pass(0, 0)
            eng.wait_ge(flag_ok, 1)
            most = eng.value_load(flag[0:1, 0:1], min_val=0, max_val=T)
            with eng.Fori(1, PASSES) as c:
                with eng.If(most > c * SLOTS):
                    one_pass(c, c * NE)
                eng.end_ifs()

        def split(n):
            return NCH if n < 32 else 10

        block = ctx.enter_context(nc.Block())

        @block.sync
        def _(sp):
            sp.dma_start(x[:, :, :], io["x"].rearrange("(t p) d -> p t d", p=P)).then_inc(x_in, 16)
            sp.wait_ge(x_in, 16)

            def load(name):
                if CHUNK[name] >= NSLOT:
                    sp.wait_ge(*chunk_done(before(name)))
                dst, src = chunk_view(name)
                sp.dma_start(dst, src).then_inc(w_slot_in[SLOT[name]], 16)

            load("U0")
            load("U1")
            sp.wait_ge(zeroed, 4)
            for n, name in enumerate(("ssm_b_re", "ssm_b_im")):
                src = io[name].rearrange("(j two) p h -> two p j h", two=2)
                for q in range(2):
                    dst = b_nat[n][64 * q:64 * q + 64].rearrange("p a (b two h) -> p two (a b) h", two=2, h=H)
                    sp.dma_start(dst[:, q], src[q]).then_inc(bnat_in, 16)
            for n, name in enumerate(("ssm_c_re", "ssm_c_im")):
                src = io[name].rearrange("(a b) h p -> b h a p", b=8)
                for b in range(8):
                    q = b % 2
                    sp.dma_start(c_nat[n][16 * b:16 * b + 16, :, 64 * q:64 * q + 64], src[b]).then_inc(cnat_in, 16)
            for name in CHUNKS[2:CHUNK["W2"]]:
                load(name)
            sp.wait_ge(rot_free, JOB["GLU1"] + 1)
            sp.wait_ge(y_ssm_ok, 1)
            for n in range(NW_IN - 1):
                sp.dma_start(ring_slot(n), expert_chunk(0, n)).then_inc(moe_in[n], 16)
            load("W2")
            load("W3")
            sp.wait_ge(mixed_ok, 4)
            for n in range(NW_IN - 1, NW):
                sp.dma_start(ring_slot(n), expert_chunk(0, n)).then_inc(moe_in[n], 16)
            load("GAIN")
            load("BIAS")
            load("BIN")
            for n, done in enumerate(((wout_done, 3), (wout_done, 4), (wout_done, 4), (rlogit, 1))):
                sp.wait_ge(*done)
                sp.dma_start(extra[n], expert_chunk(1, n)).then_inc(extra_in[n], 16)

            def one_pass(c, first):
                def load_chunk(e, j, n):
                    sp.wait_ge(chunk_used, j * NW + (n + 1 - NW))
                    sp.dma_start(ring_slot(n), expert_chunk(e, n)).then_inc(moe_in[n], 16)
                if isinstance(c, int):
                    for n in range(NX):
                        sp.wait_ge(chunk_used, n + 1)
                        sp.dma_start(ring_slot(n), expert_chunk(2, n)).then_inc(moe_in[n], 16)
                    for n in range(NX, NW):
                        load_chunk(1, 1, n)
                    for n in range(NX, NW):
                        load_chunk(2, 2, n)
                    with sp.Fori(3, NE) as e:
                        for n in range(NW):
                            load_chunk(e, e, n)
                else:
                    with sp.Fori(0, NE) as e:
                        for n in range(NW):
                            load_chunk(e, e + first, n)
            passes(sp, one_pass)
            for t in range(TT):
                sp.wait_ge(out_ready, t + 1)
                sp.dma_start(out[t * P:(t + 1) * P, :], final[:, t, :]).then_inc(stored, 16)
            sp.wait_ge(stored, 16 * TT)

        @block.gpsimd
        def _(gp):
            chain = [0]

            def link(ins):
                chain[0] += 1
                ins.then_inc(g_chain, 1)
                gp.wait_ge(g_chain, chain[0])

            for v in b_nat + c_nat + b_t + [k_t]:
                gp.memset(v, 0.0).then_inc(zeroed, 1)

            n = 1
            k = 0
            while n < T:
                lo_re, lo_im = phase_re[:, :, 0:n], phase_im[:, :, 0:n]
                a_re = par[:, 8 + 2 * (k % 2), :].unsqueeze(2).to_broadcast([P, NCH, n])
                a_im = par[:, 9 + 2 * (k % 2), :].unsqueeze(2).to_broadcast([P, NCH, n])
                t1 = ring[:, 2 * NCH * T:2 * NCH * T + NCH * n].rearrange("p (c t) -> p c t", c=NCH)
                t2 = ring[:, 2 * NCH * T + 2048:2 * NCH * T + 2048 + NCH * n].rearrange("p (c t) -> p c t", c=NCH)
                m = split(n)
                gp.wait_ge(phase_v, k + 1)
                gp.tensor_tensor(t1[:, 0:m], lo_re[:, 0:m], a_im[:, 0:m], ALU.mult)
                link(gp.tensor_tensor(t2[:, 0:m], lo_im[:, 0:m], a_re[:, 0:m], ALU.mult))
                gp.tensor_tensor(phase_im[:, 0:m, n:2 * n], t1[:, 0:m], t2[:, 0:m], ALU.add).then_inc(phase_p, 1)
                gp.wait_ge(phase_p, k + 1)
                n *= 2
                k += 1

            def rope(c, heads, job, parts=None):
                src = ptok[:, :, c - C_Q:c - C_Q + 64 * heads].rearrange("p t (h d) -> p t h d", d=64)
                a = mixed[:, :, :].rearrange("p k t -> p (k t)")[:, 0:TT * heads * 64].rearrange(
                    "p (t h d) -> p t h d", t=TT, d=64)
                b = xs[:, :, :].rearrange("p k t -> p (k t)")[:, 0:TT * heads * 64].rearrange(
                    "p (t h d) -> p t h d", t=TT, d=64)
                cb = cos_t.unsqueeze(2).to_broadcast([P, TT, heads, 64])
                sn = sin_t.unsqueeze(2).to_broadcast([P, TT, heads, 32])
                gp.wait_ge(rot_free, JOB[job] + 1)
                gp.tensor_tensor(a, src, cb, ALU.mult)
                gp.tensor_tensor(b[:, :, :, 0:32], src[:, :, :, 32:64], sn, ALU.mult)
                link(gp.tensor_tensor(b[:, :, :, 32:64], src[:, :, :, 0:32], sn, ALU.mult))
                for hs, dst in parts or [(slice(0, heads), src)]:
                    gp.tensor_tensor(dst[:, :, :, 0:32], a[:, :, hs, 0:32], b[:, :, hs, 0:32], ALU.subtract)
                    ins = gp.tensor_tensor(dst[:, :, :, 32:64], a[:, :, hs, 32:64], b[:, :, hs, 32:64], ALU.add)
                ins.then_inc(roped, 1)
                ropes[0] += 1
                gp.wait_ge(roped, ropes[0])
            ropes = [0]

            def rotated(i):
                gp.wait_ge(scanned, 2 * i + 2)
                if i:
                    gp.wait_ge(y_done, i)
                gp.tensor_tensor(xs_re, prod_out[0], prod_out[1], ALU.subtract)
                gp.tensor_tensor(xs_im, prod_out[2], prod_out[3], ALU.add).then_inc(x_state, 1)

            gp.wait_ge(c_ready, 1)
            gp.wait_ge(tables_in, 16)
            rope(C_QI, IH, "T4")
            rotated(0)
            rope(C_K, NKV, "T5")
            rotated(1)
            gp.wait_ge(bu_done, 4)
            rope(C_KI, 1, "T4", [(slice(0, 1), ki_two[:, :, n:n + 1, :]) for n in range(2)])
            rotated(2)
            qv = ptok[:, :, 0:NH * HD].rearrange("p t (h g d) -> p g t h d", g=2, d=HD)
            rope(C_Q, NH, "T7", [(slice(4 * g, 4 * g + 4), qv[:, g]) for g in range(2)])
            rotated(3)
            gp.memset(ki_t, 0.0).then_inc(zeroed, 1)
            gp.wait_ge(att_done, 2)
            gp.memset(gated_t, 0.0).then_inc(zeroed, 1)
            gp.wait_ge(*chunk_done(before("BIN")))
            for n in range(1, 4):
                gp.wait_ge(zeroed, 8 + n)
                gp.memset(b_in[32 * n:32 * n + 32, :], 0.0).then_inc(zeroed, 1)

        @block.scalar
        def _(ac):
            ac.dma_start(table[:, :], io["tables"]).then_inc(tables_in, 16)
            rows = [(V_G1, io["norm1_g"], 8), (V_G2, io["norm2_g"], 8), (V_BG, io["b_gate"], 16),
                    (V_BGLU, io["b_glu"], 4), (V_D, io["ssm_d"], 4), (V_LR, io["ssm_lam_re"], NCH),
                    (V_LI, io["ssm_lam_im"], NCH)]
            for at, src, n in rows:
                ac.dma_start(vec_rows[at:at + n, :], src.rearrange("(r c) -> r c", c=P)).then_inc(vec_in, 16)
            ac.dma_start(dt_pair[:, :], io["ssm_log_dt"].rearrange("(j g) -> j g", g=2)).then_inc(vec_in, 16)
            ac.dma_start(w_rout[:, :, :], io["w_router"].rearrange("(k p) e -> p k e", p=P)).then_inc(misc_in, 16)
            ac.dma_start(b_rout[:, :], io["b_router"].unsqueeze(0).to_broadcast([P, NE])).then_inc(misc_in, 16)

            chain = [0]

            def link(ins):
                chain[0] += 1
                ins.then_inc(a_chain, 1)
                ac.wait_ge(a_chain, chain[0])

            def squares(t):
                return ac.activation(mixed[:, 4 * t:4 * t + 4, :], x[:, t, :].rearrange("p (k s) -> p k s", k=4),
                                     ACT.Square, accum_out=stat[:, t:t + 1])

            ac.wait_ge(x_in, 16)
            link(squares(0))
            squares(1).then_inc(sum_sq, 1)
            ac.wait_ge(sum_sq, 2)
            ac.activation(stat[:, 4:6], stat[:, 2:4], ACT.Sqrt).then_inc(root, 1)

            def job(name):
                ac.wait_ge(rot_done, JOB[name] + 1)
                return rot[JOB[name] % 2]

            def norm_t(name, n, gain):
                b = job(name)
                for k in (2 * n, 2 * n + 1):
                    i = ac.activation(x_t[:, k, :], b[:, (k % 2) * T:(k % 2) * T + T], ACT.Copy,
                                      scale=vec[:, gain + k:gain + k + 1])
                i.then_inc(rot_free, 1)

            ac.wait_ge(small_free, 2)
            for n in range(4):
                norm_t(f"X{n}", n, V_G1)
            ac.activation(par[:, 0, :], par[:, 0, :], ACT.Exp).then_inc(par_s, 1)
            ac.wait_ge(par_v, 1)
            ac.activation(par[:, 2, :], par[:, 1, :], ACT.Exp).then_inc(par_s, 1)
            ac.activation(par[:, 5, :], par[:, 4, :], ACT.Sin).then_inc(par_s, 1)
            ac.activation(par[:, 6, :], par[:, 4, :], ACT.Sin, scale=0.5).then_inc(par_s, 1)
            ac.wait_ge(zeroed, 6)
            ac.wait_ge(small_t, 2)
            for n in range(2):
                for i in range(4):
                    r = slice(32 * i, 32 * i + 32)
                    ins = ac.activation(b_t[n].rearrange("p (a b) c -> p a b c", b=4)[r, :, i, :],
                                        ps[r, 4 + n, :].rearrange("p (a c) -> p a c", a=4), ACT.Copy)
            ins.then_inc(b_ready, 1)
            for n in range(2):
                b = job(f"U{n}")
                ac.activation(u_in[:, 2 * n:2 * n + 2, :], b.rearrange("p (k t) -> p k t", k=2), ACT.Copy).then_inc(rot_free, 1)
            for n, (c, w) in enumerate(TOK):
                b = job(f"T{n}")
                ac.activation(ptok[:, :, c - C_Q:c - C_Q + w], b[:, 0:TT * w].rearrange("p (t n) -> p t n", t=TT),
                              ACT.Copy).then_inc(rot_free, 1)

            def gate(letter, dst, at, n):
                b = job(f"{letter}{n}")
                for m in (2 * n, 2 * n + 1):
                    i = ac.activation(dst[:, m, :], b[:, (m % 2) * T:(m % 2) * T + T], ACT.Sigmoid,
                                      bias=vec[:, at + m:at + m + 1])
                i.then_inc(rot_free, 1)

            for n in range(4):
                gate("S", gate_s, V_BG, n)
            for n in range(4):
                b = job(f"QI{n}")
                ac.activation(qi_t[:, 2 * n:2 * n + 2, :], b.rearrange("p (k t) -> p k t", k=2),
                              ACT.Copy).then_inc(rot_free, 1)
            b = job("KK")
            ac.wait_ge(zeroed, 8)
            for n in range(2):
                r = slice(64 * n, 64 * n + 64)
                ac.activation(ki_t[r, n, :], b[r, 0:T], ACT.Copy)
                i = ac.activation(k_t[r, n, :], b[r, T:2 * T], ACT.Copy)
            i.then_inc(rot_free, 1)
            for n in range(2):
                b = job(f"Q{n}")
                ac.activation(q_t[:, 2 * n:2 * n + 2, :], b.rearrange("p (k t) -> p k t", k=2),
                              ACT.Copy).then_inc(rot_free, 1)
            ac.wait_ge(y_raw_ok, 1)
            ac.activation(y_gelu, y_raw, ACT.Gelu_apprx_tanh).then_inc(gelu_ok, 1)
            r = 0
            for t in range(TT):
                for n in range(4 * (t + 1)):
                    b = job(f"R{t}_{n}")
                    if r >= 2:
                        ac.wait_ge(relu_used, r - 1)
                    ac.activation(relu[:, r % 2, :], b, ACT.Relu).then_inc(rot_free, 1)
                    r += 1

            def exponentials(t):
                w = P * (t + 1)
                ac.wait_ge(row_max, t + 1)
                for h in range(NH):
                    i = ac.activation(logit[:, h, 0:w], logit[:, h, 0:w], ACT.Exp,
                                      bias=stat[:, 8 + h:9 + h], accum_out=stat[:, 16 + h:17 + h])
                i.then_inc(expd, 1)

            def attended(t):
                for n in range(2 * (t + 1)):
                    b = job(f"P{t}_{n}")
                    ac.activation(prob_t[:, 512 * n:512 * n + 512], b, ACT.Copy).then_inc(rot_free, 1)
                ac.wait_ge(att_done, t + 1)
                ac.activation(y_att[:, :, t * P:t * P + P], ps[:, 2 + t, :].rearrange("p (k t) -> p k t", k=KS),
                              ACT.Copy).then_inc(att_out, 1)

            gate("A", gate_a, V_BG + KD, 0)
            exponentials(0)
            for n in range(2):
                b = job(f"GLU{n}")
                for m in (2 * n, 2 * n + 1):
                    i = ac.activation(glu_g[:, m, :], b[:, (m % 2) * T:(m % 2) * T + T], ACT.Sigmoid,
                                      bias=vec[:, V_BGLU + m:V_BGLU + m + 1])
                i.then_inc(rot_free, 1)
            gate("A", gate_a, V_BG + KD, 1)
            attended(0)
            gate("A", gate_a, V_BG + KD, 2)
            exponentials(1)
            gate("A", gate_a, V_BG + KD, 3)
            for n in range(4):
                b = job(f"PS{n}")
                ac.activation(p_ssm[:, 2 * n:2 * n + 2, :], b.rearrange("p (k t) -> p k t", k=2),
                              ACT.Copy).then_inc(rot_free, 1)
            attended(1)
            for n in range(4):
                ac.wait_ge(x1_ok, n + 1)
                for t in range(TT):
                    i = ac.activation(late[:, 0:256], x[:, t, 256 * n:256 * n + 256], ACT.Square,
                                      accum_out=stat[:, 48 + TT * n + t:49 + TT * n + t])
                    if n < 3 or t == 0:
                        link(i)
                if n == 3:
                    i.then_inc(sum_sq, 1)
                if n:
                    norm_t(f"HX{n - 1}", n - 1, V_G2)
            norm_t("HX3", 3, V_G2)
            ac.wait_ge(sum_sq, 4)
            ac.activation(stat[:, 4:6], stat[:, 2:4], ACT.Sqrt).then_inc(root, 1)
            ac.wait_ge(rlogit, 1)
            ac.activation(rsum, ps[:, 2, 0:T], ACT.Copy).then_inc(rlogit_sb, 1)
            ac.wait_ge(top_ok, 1)
            ac.activation(topw[:, :, 0:TOPE], topw[:, :, 0:TOPE], ACT.Exp).then_inc(top_exp, 1)

            def one_pass(c, first):
                def gathered_rows(j):
                    ac.wait_ge(gathered, j + 1)
                    ac.activation(h_tok, ps[:, 3, :], ACT.Copy).then_inc(h_tok_ok, 1)

                def body(j, tail=False):
                    ac.wait_ge(z_gate, j + 1)
                    ac.activation(sig, gate_z, ACT.Sigmoid, scale=ALPHA).then_inc(sig_ok, 1)
                    if not tail:
                        gathered_rows(j + 1)
                    ac.wait_ge(act_trans, j + 1)
                    ac.activation(act_t, ps[:, 0, :].rearrange("p (j q s) -> p j q s", q=2, s=SLOTS),
                                  ACT.Copy).then_inc(act_t_ok, 1)
                    ac.wait_ge(chunk_used, j * NW + NW)
                    ac.activation(y_tok, ps[:, 2, :], ACT.Copy).then_inc(y_tok_ok, 1)
                gathered_rows(first)
                body(first)
                with ac.Fori(1, NE - 1) as e:
                    body(e + first)
                body(first + NE - 1, tail=True)
            passes(ac, one_pass)
            ac.wait_ge(x1_ok, KD // 2 + 1)
            link(squares(0))
            ac.wait_ge(x1_ok, KD // 2 + 2)
            squares(1).then_inc(sum_sq, 1)
            ac.wait_ge(sum_sq, 6)
            ac.activation(stat[:, 4:6], stat[:, 2:4], ACT.Sqrt).then_inc(root, 1)

        @block.vector
        def _(ve):
            chain = [0]

            def link(ins):
                chain[0] += 1
                ins.then_inc(v_chain, 1)
                ve.wait_ge(v_chain, chain[0])

            def tt(out_, a, b, op):
                return ve.tensor_tensor(out_, a, b, op)

            def rstd(n):
                ve.wait_ge(sum_sq, 2 * n + 1)
                ve.tensor_scalar(stat[:, 2:4], stat[:, 0:2], 1.0 / D, EPS, ALU.mult, ALU.add).then_inc(sum_sq, 1)
                ve.wait_ge(root, n + 1)
                link(ve.reciprocal(stat[:, 6:8], stat[:, 4:6]))

            ve.wait_ge(vec_in, 16 * 8)
            ve.tensor_copy(dt_rows[:, :].rearrange("j (g p) -> j g p", g=2),
                           dt_pair[:, :].unsqueeze(2).to_broadcast([NCH, 2, PS])).then_inc(small_free, 1)
            ve.wait_ge(small_free, 1)
            ve.wait_ge(small_t, 1)
            ve.tensor_copy(vec[:, :], ps[:, 7, 0:72])
            ve.tensor_copy(par[:, 0, :], ps[:, 7, 128:128 + NCH]).then_inc(small_free, 1)
            ve.wait_ge(small_free, 2)
            rstd(0)
            for t in range(TT):
                ve.tensor_scalar(xs[:, t, :], x[:, t, :], stat[:, 6 + t:7 + t], None, ALU.mult).then_inc(x_norm, 1)

            pr = lambda n: par[:, n, :]
            DT, LRDT, MAG, ANG, RED, SIN_, HALF, COS = 0, 1, 2, 3, 4, 5, 6, 7
            ve.wait_ge(par_s, 1)
            link(tt(pr(LRDT), L_RE, pr(DT), ALU.mult))
            link(tt(pr(ANG), L_IM, pr(DT), ALU.mult))
            magic = 12582912.0
            c1 = 6.28125
            c2 = float(np.float32(round((TWO_PI - c1) * 2 ** 21) / 2 ** 21))
            c3 = TWO_PI - c1 - c2
            link(ve.tensor_scalar(pr(12), pr(ANG), 1.0 / TWO_PI, magic, ALU.mult, ALU.add))
            link(ve.tensor_scalar(pr(13), pr(12), magic, None, ALU.subtract))
            link(ve.scalar_tensor_tensor(pr(14), pr(13), -c1, pr(ANG), ALU.mult, ALU.add))
            link(ve.scalar_tensor_tensor(pr(12), pr(13), -c2, pr(14), ALU.mult, ALU.add))
            link(ve.scalar_tensor_tensor(pr(14), pr(13), -c3, pr(12), ALU.mult, ALU.add))
            ve.tensor_scalar(pr(RED), pr(14), 3.1415925, -3.1415925, ALU.min, ALU.max).then_inc(par_v, 1)
            ve.wait_ge(par_s, 4)
            link(tt(pr(12), pr(HALF), pr(HALF), ALU.mult))
            link(ve.tensor_scalar(pr(8), pr(12), -2.0, 1.0, ALU.mult, ALU.add))
            link(ve.tensor_copy(pr(9), pr(SIN_)))
            ve.memset(phase_re[:, :, 0:1], 1.0)
            ve.memset(phase_im[:, :, 0:1], 0.0).then_inc(phase_v, 1)
            ve.wait_ge(phase_v, 1)
            n, k = 1, 0
            link(tt(pr(16), pr(MAG), pr(8), ALU.mult))
            link(tt(pr(17), pr(MAG), pr(9), ALU.mult))
            ve.wait_ge(rot_done, JOB["X3"] + 1)
            while n < T:
                ar = pr(8 + 2 * (k % 2))
                ai = pr(9 + 2 * (k % 2))
                lo_re, lo_im = phase_re[:, :, 0:n], phase_im[:, :, 0:n]
                t1 = mixed[:, :, :].rearrange("p k t -> p (k t)")[:, 0:NCH * n].rearrange("p (c t) -> p c t", c=NCH)
                t2 = xs[:, :, :].rearrange("p k t -> p (k t)")[:, 0:NCH * n].rearrange("p (c t) -> p c t", c=NCH)
                if k:
                    ve.wait_ge(phase_p, k)
                tt(t1, lo_re, ar.unsqueeze(2).to_broadcast([P, NCH, n]), ALU.mult)
                link(tt(t2, lo_im, ai.unsqueeze(2).to_broadcast([P, NCH, n]), ALU.mult))
                link(tt(phase_re[:, :, n:2 * n], t1, t2, ALU.subtract))
                m = split(n)
                if m < NCH:
                    tt(t1[:, m:], lo_re[:, m:], ai[:, m:].unsqueeze(2).to_broadcast([P, NCH - m, n]), ALU.mult)
                    link(tt(t2[:, m:], lo_im[:, m:], ar[:, m:].unsqueeze(2).to_broadcast([P, NCH - m, n]), ALU.mult))
                    link(tt(phase_im[:, m:, n:2 * n], t1[:, m:], t2[:, m:], ALU.add))
                if 2 * n < T:
                    nr, ni = pr(8 + 2 * ((k + 1) % 2)), pr(9 + 2 * ((k + 1) % 2))
                    tt(pr(12), ar, ar, ALU.mult)
                    tt(pr(13), ai, ai, ALU.mult)
                    link(tt(pr(14), ar, ai, ALU.mult))
                    tt(nr, pr(12), pr(13), ALU.subtract)
                    ve.tensor_scalar(ni, pr(14), 2.0, None, ALU.mult).then_inc(phase_v, 1)
                    ve.wait_ge(phase_v, k + 2)
                n *= 2
                k += 1
            link(ve.tensor_scalar(pr(18), pr(16), -1.0, None, ALU.add))
            tt(pr(12), pr(18), L_RE, ALU.mult)
            link(tt(pr(13), pr(17), L_IM, ALU.mult))
            link(tt(pr(14), pr(12), pr(13), ALU.add))
            tt(pr(12), pr(17), L_RE, ALU.mult)
            link(tt(pr(13), pr(18), L_IM, ALU.mult))
            link(tt(pr(15), pr(12), pr(13), ALU.subtract))
            tt(pr(12), L_RE, L_RE, ALU.mult)
            link(tt(pr(13), L_IM, L_IM, ALU.mult))
            link(tt(pr(19), pr(12), pr(13), ALU.add))
            link(ve.reciprocal(pr(20), pr(19)))
            tt(pr(21), pr(14), pr(20), ALU.mult)
            link(tt(pr(22), pr(15), pr(20), ALU.mult))
            ve.wait_ge(small_t, 3)
            z_re = pr(21).unsqueeze(2).to_broadcast([P, NCH, 32])
            z_im = pr(22).unsqueeze(2).to_broadcast([P, NCH, 32])
            c_re = ps[:, 6, :].rearrange("p (j c) -> p j c", c=32)
            c_im = ps[:, 7, :].rearrange("p (j c) -> p j c", c=32)
            tv = [mixed[:, 2 * n:2 * n + 2, :].rearrange("p k t -> p (k t)").rearrange("p (j c) -> p j c", c=32)
                  for n in range(4)]
            tt(tv[0], c_re, z_re, ALU.mult)
            tt(tv[1], c_im, z_im, ALU.mult)
            tt(tv[2], c_re, z_im, ALU.mult)
            link(tt(tv[3], c_im, z_re, ALU.mult))
            ct = [c_t[n].rearrange("p a (b c) -> p (a b) c", c=32) for n in range(2)]
            tt(ct[0], tv[0], tv[1], ALU.subtract)
            ve.scalar_tensor_tensor(ct[1], tv[2], -1.0, tv[3], ALU.mult, ALU.subtract).then_inc(c_ready, 1)

            ve.wait_ge(phase_p, 8)
            for i in range(4):
                er, ei = phase_re[:, 4 * i:4 * i + 4, :], phase_im[:, 4 * i:4 * i + 4, :]
                bre = ps[:, 4:6, :].rearrange("p b (j t) -> p (b j) t", t=T)
                bim = ps[:, 6:8, :].rearrange("p b (j t) -> p (b j) t", t=T)
                ve.wait_ge(bu_done, i + 1)
                tt(prod[0], bre, er, ALU.mult)
                tt(prod[1], bim, ei, ALU.mult)
                tt(prod[2], bim, er, ALU.mult)
                tt(prod[3], bre, ei, ALU.mult).then_inc(bu_used, 1)
                ve.wait_ge(bu_used, i + 1)
                tt(state_re, prod[0], prod[1], ALU.add)
                tt(state_im, prod[2], prod[3], ALU.subtract).then_inc(w_rot, 1)
                ve.wait_ge(w_rot, i + 1)
                for a in range(4):
                    j = 4 * i + a
                    decay = par[:, MAG, j:j + 1].to_broadcast([P, T])
                    for s in (state_re, state_im):
                        ins = ve.tensor_tensor_scan(s[:, a, :], decay, s[:, a, :], 0.0, ALU.mult, ALU.add)
                ins.then_inc(scanned, 1)
                ve.wait_ge(scanned, 2 * i + 1)
                if i:
                    ve.wait_ge(x_state, i)
                tt(prod_out[0], state_re, er, ALU.mult)
                tt(prod_out[1], state_im, ei, ALU.mult)
                tt(prod_out[2], state_im, er, ALU.mult)
                tt(prod_out[3], state_re, ei, ALU.mult).then_inc(scanned, 1)

            ve.wait_ge(y_done, 4)
            for a in range(KS):
                i = ve.scalar_tensor_tensor(y_raw[:, a, :], u_in[:, a, :], vec[:, V_D + a:V_D + a + 1],
                                            ps[:, 2 + a // 2, (a % 2) * T:(a % 2) * T + T], ALU.mult, ALU.add)
            i.then_inc(y_raw_ok, 1)

            wi = ptok[:, :, C_WI - C_Q:C_WI - C_Q + IH]
            link(ve.tensor_scalar(wi, wi, IH ** -0.5 * ID ** -0.5, None, ALU.mult))
            r = 0
            for t in range(TT):
                w = P * (t + 1)
                per = 512 // w
                acc = score[:, t, 0:w]
                for n in range(4 * (t + 1)):
                    ve.wait_ge(rot_free, JOB[f"R{t}_{n}"] + 1)
                    for m in range(per):
                        h = n * per + m
                        s = relu[:, r % 2, m * w:m * w + w]
                        if n == 0 and m == 0:
                            ins = ve.tensor_scalar(acc, s, wi[:, t, h:h + 1], None, ALU.mult)
                        else:
                            ins = ve.scalar_tensor_tensor(acc, s, wi[:, t, h:h + 1], acc, ALU.mult, ALU.add)
                        if m == per - 1:
                            ins.then_inc(relu_used, 1)
                            ve.wait_ge(relu_used, r + 1)
                        else:
                            link(ins)
                    r += 1

            def choose_keys(t):
                w = P * (t + 1)
                link(tt(score[:, t, 0:w], score[:, t, 0:w], causal[:, t, 0:w], ALU.add))
                src = score[:, t, 0:w]
                dst = taken[:, t, 0:w]
                for n in range(NSEL // 8):
                    link(ve.max(stat[:, 24:32], src))
                    link(ve.match_replace(dst, stat[:, 24:32], src, GONE))
                    src = dst
                link(ve.tensor_scalar(dst, dst, GONE, -NEG, ALU.is_equal, ALU.mult))
                link(ve.tensor_scalar(dst, dst, NEG, None, ALU.add))
                link(tt(bias[:, t, 0:w], dst, causal[:, t, 0:w], ALU.min))

            def mask(t):
                w = P * (t + 1)
                ve.wait_ge(logit_done, t + 1)
                lg = ps[:, 4:8, :].rearrange("p b (h s) -> p (b h) s", s=T)[:, :, 0:w]
                if t:
                    ve.wait_ge(rot_done, JOB["P0_1"] + 1)
                link(ve.scalar_tensor_tensor(logit[:, :, 0:w], lg, HD ** -0.5,
                                             bias[:, t, 0:w].unsqueeze(1).to_broadcast([P, NH, w]),
                                             ALU.mult, ALU.add))
                ve.tensor_reduce(stat[:, 8:16], logit[:, :, 0:w], AX.X, ALU.max, negate=True).then_inc(row_max, 1)

            def probabilities(t):
                w = P * (t + 1)
                ve.wait_ge(expd, t + 1)
                link(ve.reciprocal(stat[:, 32:40], stat[:, 16:24]))
                tt(logit[:, :, 0:w], logit[:, :, 0:w],
                   stat[:, 32:40].unsqueeze(2).to_broadcast([P, NH, w]), ALU.mult).then_inc(prob_ok, 1)

            choose_keys(0)
            mask(0)
            choose_keys(1)
            probabilities(0)
            ve.wait_ge(rot_free, JOB["GLU1"] + 1)
            tt(y_ssm, y_gelu, glu_g, ALU.mult).then_inc(y_ssm_ok, 1)
            mask(1)
            probabilities(1)
            ve.wait_ge(rot_free, JOB["PS3"] + 1)
            link(tt(p_ssm, p_ssm, gate_s, ALU.mult))
            ve.wait_ge(att_done, 2)
            for n in range(4):
                ve.wait_ge(proj_done, n + 1)
                two = mixed[:, 2 * n:2 * n + 2, :]
                tt(two, ps[:, 4 + n, :].rearrange("p (k t) -> p k t", k=2), gate_a[:, 2 * n:2 * n + 2, :],
                   ALU.mult).then_inc(gated_a, 1)
                ve.wait_ge(gated_a, n + 1)
                tt(two, two, p_ssm[:, 2 * n:2 * n + 2, :], ALU.add).then_inc(mixed_ok, 1)
            for n in range(4):
                ve.wait_ge(wout_done, n + 1)
                part = x[:, :, 256 * n:256 * n + 256]
                tt(part, part, ps[:, 4 + n, :].rearrange("p (t c) -> p t c", t=TT), ALU.add).then_inc(x1_ok, 1)
            ve.wait_ge(sum_sq, 3)
            link(ve.tensor_reduce(stat[:, 0:2], stat[:, 48:56].rearrange("p (n t) -> p t n", t=TT), AX.X, ALU.add))
            rstd(1)
            for t in range(TT):
                ve.tensor_scalar(xs[:, t, :], x[:, t, :], stat[:, 6 + t:7 + t], None, ALU.mult).then_inc(x_norm, 1)

            ve.wait_ge(rlogit, 2)
            ve.wait_ge(misc_in, 32)
            link(ve.tensor_reduce(rlog, ps[:, 3, 0:TT * P].rearrange("p (t c e) -> p t e c", t=TT, c=4), AX.X, ALU.add))
            link(tt(rlog, rlog, stat[:, 6:8].unsqueeze(2).to_broadcast([P, TT, NE]), ALU.mult))
            link(tt(rlog, rlog,
                    b_rout[:, :].unsqueeze(1).to_broadcast([P, TT, NE]), ALU.add))
            for t in range(TT):
                link(ve.max(top8[:, t, :], rlog[:, t, :]))
                link(ve.max_index(top8i[:, t, :], top8[:, t, :], rlog[:, t, :]))
            link(ve.tensor_copy(top8f, top8i))
            tt(topw[:, :, 0:TOPE], top8[:, :, 0:TOPE], top8[:, :, 0:1].to_broadcast([P, TT, TOPE]),
               ALU.subtract).then_inc(top_ok, 1)
            for t in range(TT):
                ins = tt(hot4[:, t], exp_no.unsqueeze(1).to_broadcast([P, TOPE, NE]),
                         top8f[:, t, 0:TOPE].unsqueeze(2).to_broadcast([P, TOPE, NE]), ALU.is_equal)
            link(ins)
            ve.tensor_reduce(picked, hot4.rearrange("p t k e -> p t e k"), AX.X, ALU.add).then_inc(picked_ok, 1)
            ve.wait_ge(top_exp, 1)
            link(ve.tensor_reduce(stat[:, 40:42], topw[:, :, 0:TOPE], AX.X, ALU.add))
            link(ve.reciprocal(stat[:, 42:44], stat[:, 40:42]))
            link(tt(topw[:, :, 0:TOPE], topw[:, :, 0:TOPE],
                    stat[:, 42:44].unsqueeze(2).to_broadcast([P, TT, TOPE]), ALU.mult))
            for t in range(TT):
                ins = tt(hot4w[:, t], hot4[:, t], topw[:, t, 0:TOPE].unsqueeze(2).to_broadcast([P, TOPE, NE]),
                         ALU.mult)
            link(ins)
            ve.tensor_reduce(gates, hot4w.rearrange("p t k e -> p t e k"), AX.X, ALU.add).then_inc(route_ok, 1)
            ve.wait_ge(placed, 1)
            link(ve.scalar_tensor_tensor(place, ps[:, 3, 0:TT * NE].rearrange("p (t e) -> p t e", t=TT), FAR,
                                         picked, ALU.add, ALU.mult))
            ve.tensor_scalar(place, place, -FAR, None, ALU.add).then_inc(place_ok, 1)
            link(ve.tensor_reduce(stat[0:1, 44:45], ps[0:1, 3, 64:64 + NE], AX.X, ALU.max))
            ve.tensor_copy(flag[:, :], stat[0:1, 44:45]).then_inc(flag_ok, 1)
            ve.wait_ge(gates_tr, 1)
            ve.tensor_copy(gates_t, ps[0:NE, 2, P:P + T]).then_inc(gates_t_ok, 1)

            def one_pass(c, first):
                if not isinstance(c, int):
                    ve.tensor_scalar(place, place, -float(SLOTS), None, ALU.add).then_inc(place_ok, 1)
                    ve.wait_ge(place_ok, c + 1)
                else:
                    ve.wait_ge(place_ok, 1)

                def column(v, e):
                    return v[:, :, bass.ds(e, 1)].to_broadcast([P, TT, SLOTS])

                slots = slot_no.unsqueeze(1).to_broadcast([P, TT, SLOTS])

                def choose(e):
                    tt(one_hot, slots, column(place, e), ALU.is_equal).then_inc(hot_ok, 1)

                def pick_bias(e):
                    ve.tensor_copy(chosen, ident[:, bass.ds(e, 1)].to_broadcast([P, SLOTS])).then_inc(chosen_ok, 1)

                def take(j):
                    ve.wait_ge(h_trans, j + 1)
                    tt(h_sel, ps[:, 3, :].rearrange("p (j q s) -> p j q s", q=2, s=SLOTS),
                       vec[:, V_G2:V_G2 + KD].rearrange("p (q j) -> p j q", q=2).unsqueeze(3).to_broadcast(
                           [P, 4, 2, SLOTS]), ALU.mult).then_inc(h_sel_ok, 1)

                def weigh(j, e):
                    for q in range(2):
                        ins = tt(gated[:, :, q], slots, column(place, e), ALU.is_equal)
                    ins.then_inc(gated_eq, 1)
                    ve.wait_ge(gated_eq, j + 1)
                    for q in range(2):
                        ins = tt(gated[:, :, q], gated[:, :, q], column(gates, e), ALU.mult)
                    ins.then_inc(gated_ok, 1)

                def body(j, e, tail=False):
                    if not tail:
                        choose(e + 1)
                    ve.wait_ge(chunk_used, j * NW + NW_IN)
                    z = ps[:, 0:2, :].rearrange("p b (c g) -> p g (b c)", g=2)
                    ve.tensor_scalar(gate_z, z[:, 0], LIMIT, None, ALU.min).then_inc(z_gate, 1)
                    ve.tensor_scalar(lin_z, z[:, 1], LIMIT, -LIMIT, ALU.min, ALU.max).then_inc(z_lin, 1)
                    ve.wait_ge(z_lin, j + 1)
                    ve.scalar_tensor_tensor(act, lin_z, 1.0, gate_z, ALU.add, ALU.mult).then_inc(z_prod, 1)
                    ve.wait_ge(z_prod, j + 1)
                    ve.wait_ge(sig_ok, j + 1)
                    tt(act, act, sig, ALU.mult).then_inc(act_ok, 1)
                    weigh(j, e)
                    if not tail:
                        pick_bias(e + 1)
                        take(j + 1)
                    ve.wait_ge(gated_trans, j + 1)
                    for q in range(2):
                        r = slice(64 * q, 64 * q + SLOTS)
                        ins = ve.tensor_copy(gated_t[r, q, :], ps[r, 1, 0:T])
                    ins.then_inc(gated_t_ok, 1)

                if isinstance(c, int):
                    ve.wait_ge(zeroed, 12)
                choose(0)
                pick_bias(0)
                take(first)
                body(first, 0)
                with ve.Fori(1, NE - 1) as e:
                    body(e + first, e)
                body(first + NE - 1, NE - 1, tail=True)
            passes(ve, one_pass)

            ve.wait_ge(sum_ok, 1)
            for t in range(TT):
                tt(x[:, t, :], x[:, t, :], ps[:, 4 + 2 * t:6 + 2 * t, :].rearrange("p b n -> p (b n)"),
                   ALU.add).then_inc(x1_ok, 1)
            rstd(2)
            chunk_arrived(ve, "GAIN")
            for t in range(TT):
                ve.scalar_tensor_tensor(final[:, t, :], x[:, t, :], stat[:, 6 + t:7 + t], gfin, ALU.mult,
                                        ALU.mult).then_inc(out_ready, 1)

        @block.tensor
        def _(pe):
            def job(name):
                n = JOB[name]
                if n >= 2:
                    pe.wait_ge(rot_free, n - 1)
                return rot[n % 2]

            pe.wait_ge(tables_in, 16)
            pe.wait_ge(vec_in, 16 * 8)
            pe.wait_ge(small_free, 1)
            pe.transpose(ps[:, 7, 0:72], vec_rows[:, :], ident[0:72, 0:72])
            pe.transpose(ps[:, 7, 128:128 + NCH], dt_rows[:, :], ident[0:NCH, 0:NCH]).then_inc(small_t, 1)
            def norm_t(name, n, src):
                b = job(name)
                for k in (2 * n, 2 * n + 1):
                    for t in range(TT):
                        i = pe.transpose(b[:, (k % 2) * T + t * P:(k % 2) * T + t * P + P],
                                         src[:, t, k * P:k * P + P], ident)
                i.then_inc(rot_done, 1)

            pe.wait_ge(x_norm, TT)
            for n in range(4):
                norm_t(f"X{n}", n, xs)
            pe.wait_ge(bnat_in, 16 * 4)
            for n in range(2):
                for a in range(4):
                    i = pe.transpose(ps[:, 4 + n, a * P:a * P + P], b_nat[n][:, a, :], ident)
            i.then_inc(small_t, 1)
            pe.wait_ge(cnat_in, 16 * 16)
            pe.wait_ge(small_free, 2)
            for n in range(2):
                for a in range(4):
                    i = pe.transpose(ps[:, 6 + n, a * P:a * P + P], c_nat[n][:, a, :], ident)
            i.then_inc(small_t, 1)

            def feature_job(name, src, kt, first_m, slot):
                b = job(name)
                for m in range(2):
                    for k in range(kt):
                        i = pe.matmul(b[:, m * T:m * T + T], slot[:, k, (first_m + m) * P:(first_m + m + 1) * P],
                                      src[:, k, :], start=(k == 0), stop=(k == kt - 1))
                i.then_inc(rot_done, 1)

            for n in range(2):
                chunk_arrived(pe, f"U{n}")
                if n == 0:
                    pe.wait_ge(rot_free, JOB["X3"] + 1)
                feature_job(f"U{n}", x_t, KD, 0, chunk_view(f"U{n}")[0])

            def bu(i):
                if i == 0:
                    pe.wait_ge(b_ready, 1)
                    pe.wait_ge(c_ready, 1)
                    pe.wait_ge(rot_free, JOB["U1"] + 1)
                else:
                    pe.wait_ge(bu_used, i)
                for n in range(2):
                    for a in range(4):
                        ins = pe.matmul(ps[:, 4 + 2 * n + a // 2, (a % 2) * T:(a % 2) * T + T],
                                        b_t[n][:, 4 * i + a, :], u_in[:, i, :], start=True, stop=True)
                ins.then_inc(bu_done, 1)

            def y_out(i):
                pe.wait_ge(x_state, i + 1)
                for n, v in enumerate((xs_re, xs_im)):
                    for a in range(4):
                        ins = pe.matmul(ps[32 * a:32 * a + 32, 2 + i // 2, (i % 2) * T:(i % 2) * T + T],
                                        c_t[n][:, i, 32 * a:32 * a + 32], v[:, a, :], start=(n == 0), stop=(n == 1))
                ins.then_inc(y_done, 1)

            def token_job(n):
                w = TOK[n][1]
                chunk_arrived(pe, f"T{n}")
                slot = chunk_view(f"T{n}")[0]
                b = job(f"T{n}")
                for t in range(TT):
                    for k in range(KD):
                        i = pe.matmul(b[:, t * w:t * w + w], x_t[:, k, t * P:t * P + P], slot[:, k, :],
                                      start=(k == 0), stop=(k == KD - 1))
                i.then_inc(rot_done, 1)

            def gate_job(letter, n):
                chunk_arrived(pe, f"{letter}{n}")
                feature_job(f"{letter}{n}", x_t, KD, 0, chunk_view(f"{letter}{n}")[0])

            for n in range(4):
                token_job(n)
            bu(0)
            token_job(4)
            token_job(5)
            bu(1)
            token_job(6)
            y_out(0)
            token_job(7)
            bu(2)
            gate_job("S", 0)
            y_out(1)
            bu(3)
            gate_job("S", 1)
            gate_job("S", 2)
            y_out(2)
            gate_job("S", 3)
            y_out(3)

            def trans_job(name, cols_of):
                b = job(name)
                for n, c in enumerate(cols_of):
                    for t in range(TT):
                        i = pe.transpose(b[:, n * T + t * P:n * T + t * P + P], c(t), ident)
                i.then_inc(rot_done, 1)

            pe.wait_ge(roped, 4)
            q0 = C_QI - C_Q
            for n in range(4):
                trans_job(f"QI{n}", [lambda t, k=k: ptok[:, t, q0 + k * P:q0 + k * P + P] for k in (2 * n, 2 * n + 1)])
            b = job("KK")
            for t in range(TT):
                pe.transpose(b[:, t * P:t * P + P],
                             ki_two[:, t].rearrange("p n d -> p (n d)"), ident)
            for t in range(TT):
                i = pe.transpose(b[:, T + t * P:T + t * P + P], ptok[:, t, C_K - C_Q:C_K - C_Q + P], ident)
            i.then_inc(rot_done, 1)
            for n in range(2):
                trans_job(f"Q{n}", [lambda t, k=k: ptok[:, t, k * P:k * P + P] for k in (2 * n, 2 * n + 1)])

            pe.wait_ge(rot_free, JOB["KK"] + 1)
            for t in range(TT):
                w = P * (t + 1)
                per = 512 // w
                for n in range(4 * (t + 1)):
                    b = job(f"R{t}_{n}")
                    for m in range(per // 2):
                        i = pe.matmul(b[:, 2 * m * w:2 * m * w + 2 * w], qi_t[:, n * per // 2 + m, t * P:t * P + P],
                                      ki_t[:, :, 0:w], start=True, stop=True)
                    i.then_inc(rot_done, 1)

            pe.wait_ge(rot_free, JOB["Q1"] + 1)

            def logits(t):
                w = P * (t + 1)
                if t:
                    pe.wait_ge(row_max, t)
                for h in range(NH // 2):
                    i = pe.matmul(ps[:, 4 + h, :].rearrange("p (n s) -> p n s", n=2)[:, :, 0:w],
                                  q_t[:, h, t * P:t * P + P], k_t[:, :, 0:w], start=True, stop=True)
                i.then_inc(logit_done, 1)

            def attend(t):
                pe.wait_ge(prob_ok, t + 1)
                for n in range(2 * (t + 1)):
                    b = job(f"P{t}_{n}")
                    for m in range(4):
                        at = 4 * n + m
                        h, s = at // (t + 1), at % (t + 1)
                        i = pe.transpose(b[:, m * P:m * P + P], logit[:, h, s * P:s * P + P], ident)
                    i.then_inc(rot_done, 1)
                pe.wait_ge(rot_free, JOB[f"P{t}_{2 * t + 1}"] + 1)
                for h in range(NH):
                    for s in range(t + 1):
                        at = (2 * (h % 4) + h // 4) * (t + 1) + s
                        base = 64 * (h % 2)
                        i = pe.matmul(ps[base:base + 64, 2 + t, (h // 2) * P:(h // 2) * P + P],
                                      ptok[:, s, v0 + 64 * (h // 4):v0 + 64 * (h // 4) + 64],
                                      prob_t[:, at * P:at * P + P], start=(s == 0), stop=(s == t))
                i.then_inc(att_done, 1)

            v0 = C_V - C_Q
            logits(0)
            gate_job("A", 0)
            chunk_arrived(pe, "GLU")
            pe.wait_ge(gelu_ok, 1)
            for n in range(2):
                feature_job(f"GLU{n}", y_gelu, KS, 2 * n, chunk_view("GLU")[0])
            gate_job("A", 1)
            logits(1)
            attend(0)
            gate_job("A", 2)
            gate_job("A", 3)
            pe.wait_ge(y_ssm_ok, 1)
            for n in range(4):
                if n % 2 == 0:
                    chunk_arrived(pe, f"PS{n // 2}")
                feature_job(f"PS{n}", y_ssm, KS, 2 * (n % 2), chunk_view(f"PS{n // 2}")[0])
            attend(1)
            pe.wait_ge(att_out, 2)
            pe.wait_ge(row_max, 2)
            for n in range(4):
                if n % 2 == 0:
                    chunk_arrived(pe, f"PA{n // 2}")
                slot = chunk_view(f"PA{n // 2}")[0]
                for m in range(2):
                    for k in range(KS):
                        at = (2 * (n % 2) + m) * P
                        i = pe.matmul(ps[:, 4 + n, m * T:m * T + T], slot[:, k, at:at + P], y_att[:, k, :],
                                      start=(k == 0), stop=(k == KS - 1))
                i.then_inc(proj_done, 1)
            pe.wait_ge(mixed_ok, 4)
            for n in range(4):
                chunk_arrived(pe, f"W{n}")
                slot = chunk_view(f"W{n}")[0]
                for t in range(TT):
                    for k in range(KD):
                        i = pe.matmul(ps[:, 4 + n, t * T:t * T + 256], mixed[:, k, t * P:t * P + P], slot[:, k, :],
                                      start=(k == 0), stop=(k == KD - 1))
                i.then_inc(wout_done, 1)
                if n:
                    pe.wait_ge(x1_ok, n)
                    norm_t(f"HX{n - 1}", n - 1, x)
            pe.wait_ge(x1_ok, 4)
            norm_t("HX3", 3, x)

            for k in range(KD):
                c = k % 4
                if k == 0:
                    pe.wait_ge(rot_free, JOB["HX2"] + 1)
                    pe.wait_ge(misc_in, 32)
                if k == 6:
                    pe.wait_ge(rot_free, JOB["HX3"] + 1)
                i = pe.matmul(ps[32 * c:32 * c + 32, 2, 0:T], w_rout[:, k, :], x_t[:, k, :],
                              start=(k < 4), stop=(k >= 4))
            i.then_inc(rlogit, 1)
            pe.wait_ge(rlogit_sb, 1)
            for t in range(TT):
                i = pe.transpose(ps[:, 3, t * P:t * P + P], rsum[:, t * P:t * P + P], ident)
            i.then_inc(rlogit, 1)
            pe.wait_ge(picked_ok, 1)
            pe.matmul(ps[:, 3, 0:NE], tri, picked[:, 0, :], start=True, stop=True)
            pe.matmul(ps[:, 3, NE:2 * NE], ones, picked[:, 0, :], start=True, stop=False)
            pe.matmul(ps[:, 3, NE:2 * NE], tri, picked[:, 1, :], start=False, stop=True)
            pe.matmul(ps[:, 3, 2 * NE:3 * NE], ones, picked[:, 0, :], start=True, stop=False)
            pe.matmul(ps[:, 3, 2 * NE:3 * NE], ones, picked[:, 1, :], start=False, stop=True).then_inc(placed, 1)
            pe.wait_ge(route_ok, 1)
            for t in range(TT):
                i = pe.transpose(ps[0:NE, 2, P + t * P:P + t * P + P], gates[:, t, :], ident)
            i.then_inc(gates_tr, 1)
            def one_pass(c, first):
                def gather(j):
                    pe.wait_ge(hot_ok, j + 1)
                    for t in range(TT):
                        for q in range(2):
                            i = pe.matmul(ps[64 * q:64 * q + SLOTS, 3, :], one_hot[:, t, :],
                                          xs[:, t, 512 * q:512 * q + 512], start=(t == 0), stop=(t == TT - 1))
                    i.then_inc(gathered, 1)

                def gather_t(j):
                    pe.wait_ge(h_tok_ok, j + 1)
                    for n in range(4):
                        i = pe.transpose(ps[:, 3, n * P:n * P + P], h_tok[:, n * P:n * P + P], ident)
                    i.then_inc(h_trans, 1)

                def scatter(j):
                    pe.wait_ge(y_tok_ok, j + 1)
                    for t in range(TT):
                        for q in range(2):
                            pe.matmul(ps[:, 4 + 2 * t + q, :], gated_t[:, q, t * P:t * P + P], y_tok,
                                      start=False, stop=False, skip_group_check=True)

                def body(j, head=False, tail=False, ahead=False):
                    pe.wait_ge(h_sel_ok, j + 1)
                    pe.wait_ge(chosen_ok, j + 1)
                    if not head:
                        pe.wait_ge(gated_t_ok, j)
                    for n in range(4):
                        r = slice(64 * (n % 2), 64 * (n % 2) + SLOTS)
                        pe.matmul(ps[r, n // 2, :], chosen, b_in[:, 512 * n:512 * n + 512], start=True, stop=False)
                    for k in range(KD):
                        if ahead and k < NX:
                            pe.wait_ge(extra_in[k], 16)
                            w = extra[k]
                        else:
                            pe.wait_ge(moe_in[k], 16 * j + (0 if k < NX and not (head and isinstance(c, int)) else 16))
                            w = ring[:, k * SW:(k + 1) * SW]
                        for n in range(4):
                            r = slice(64 * (n % 2), 64 * (n % 2) + SLOTS)
                            i = pe.matmul(ps[r, n // 2, :], h_sel[:, k % 4, k // 4, :], w[:, 512 * n:512 * n + 512],
                                          start=False, stop=(k == KD - 1))
                        i.then_inc(chunk_used, 1)
                    if not head:
                        scatter(j - 1)
                    elif isinstance(c, int):
                        pe.wait_ge(gates_t_ok, 1)
                        chunk_arrived(pe, "BIAS")
                        for t in range(TT):
                            for q in range(2):
                                pe.matmul(ps[:, 4 + 2 * t + q, :], gates_t[:, t * P:t * P + P],
                                          b_out[:, 512 * q:512 * q + 512], start=True, stop=False,
                                          skip_group_check=True)
                    if not tail:
                        gather(j + 1)
                    pe.wait_ge(act_ok, j + 1)
                    for n in range(4):
                        i = pe.transpose(ps[:, 0, n * P:n * P + P], act[:, n * P:n * P + P], ident)
                    i.then_inc(act_trans, 1)
                    pe.wait_ge(gated_ok, j + 1)
                    for t in range(TT):
                        i = pe.transpose(ps[:, 1, t * P:t * P + P], gated[:, t].rearrange("p q s -> p (q s)"), ident)
                    i.then_inc(gated_trans, 1)
                    if not tail:
                        gather_t(j + 1)
                    pe.wait_ge(act_t_ok, j + 1)
                    for k in range(KF):
                        c_ = NW_IN + k // 2
                        if k % 2 == 0:
                            pe.wait_ge(moe_in[c_], 16 * j + 16)
                        w = ring[:, c_ * SW + (k % 2) * D:c_ * SW + (k % 2) * D + D]
                        for q in range(2):
                            i = pe.matmul(ps[64 * q:64 * q + SLOTS, 2, :], act_tile(k), w[:, 512 * q:512 * q + 512],
                                          start=(k == 0), stop=(k == KF - 1))
                        if k % 2:
                            i.then_inc(chunk_used, 1)

                gather(first)
                gather_t(first)
                if isinstance(c, int):
                    chunk_arrived(pe, "BIN")
                    pe.wait_ge(zeroed, 12)
                body(first, head=True)
                if isinstance(c, int):
                    body(1, ahead=True)
                with pe.Fori(2 if isinstance(c, int) else 1, NE - 1) as e:
                    body(e + first)
                body(first + NE - 1, tail=True)
                pe.wait_ge(gated_t_ok, first + NE)
                scatter(first + NE - 1)
            passes(pe, one_pass)
            pe.matmul(ps[0:1, 3, 0:1], ones[0:1, 0:1], ones[0:1, 0:1], start=True, stop=True).then_inc(sum_ok, 1)


_INS = ["x", "norm1_g", "w_in", "b_gate", "ssm_lam_re", "ssm_lam_im", "ssm_log_dt", "ssm_b_re", "ssm_b_im",
        "ssm_c_re", "ssm_c_im", "ssm_d", "w_glu", "b_glu", "w_proj_ssm", "w_proj_attn", "w_out", "norm2_g",
        "w_router", "b_router", "w_moe_in", "b_moe_in", "w_moe_out", "b_moe_out", "norm_f_g"]
_FLAT = {"norm1_g", "b_gate", "ssm_lam_re", "ssm_lam_im", "ssm_log_dt", "ssm_d", "b_glu", "norm2_g", "b_router",
         "norm_f_g"}


def kernel(**inputs):
    import concourse.bacc as _bacc
    from concourse.bass_utils import run_bass_kernel_spmd as _run

    nc = _bacc.Bacc("TRN2", target_bir_lowering=False, num_devices=1)
    arrays, io = {}, {}
    for name in _INS + ["tables"]:
        if name == "tables":
            a = constant_tables()
        else:
            a = np.ascontiguousarray(inputs[name])
            if name in _FLAT:
                a = a.reshape(-1)
            elif name != "norm_f_g":
                a = a.reshape(a.shape[1:])
        arrays[f"in_{name}"] = a
        io[name] = nc.dram_tensor(f"in_{name}", a.shape, mybir.dt.from_np(a.dtype), kind="ExternalInput").ap()
    out = nc.dram_tensor("out_0", (T, D), mybir.dt.float32, kind="ExternalOutput").ap()
    build(nc, io, out)
    r = _run(nc, [arrays], core_ids=[0])
    return r.results[0]["out_0"].reshape(1, T, D)
```

```python
import math
from contextlib import ExitStack

import numpy as np

import concourse.bass as bass
from concourse import mybir

P = 128
T = 256
TT = T // P
D = 1024
KD = D // P
DS = 512
KS = DS // P
G, PS, H = 32, 64, 16
NCH = G * PS // P
NH, NKV, HD = 8, 2, 64
IH, ID = 16, 64
NSEL = min(256, T // 4)
NE, TOPE, F = 32, 4, 1024
KF = F // P
LIMIT, ALPHA = 7.0, 1.702
EPS = 1e-5
NEG = -1e30
GONE = -3e38
FAR = 1024.0
SLOTS = 64
PASSES = T // SLOTS
NX = 9
LEAD = 6
TWO_PI = 2.0 * math.pi

C_U, C_Q, C_K, C_V, C_QI, C_KI, C_WI, C_GS, C_GA, C_END = 0, 512, 1024, 1152, 1280, 2304, 2368, 2384, 3408, 4432
TOK = [(C_QI + 221 * n, min(221, C_GS - C_QI - 221 * n)) for n in range(5)] \
    + [(C_K, 256), (C_Q, 256), (C_Q + 256, 256)]
NTOK = C_GS - C_Q

TB_COS, TB_SIN, TB_CAUSAL, TB_ID, TB_SLOT, TB_EXP, TB_TRI, TB_ONE, TB_END = \
    [int(v) for v in np.cumsum([0, TT * 64, TT * 32, TT * T, P, SLOTS, NE, P, P])]
MIX_TABLES = TB_ID


def constant_tables():
    t = np.zeros((P, TB_END), np.float32)
    t[:, TB_ID:TB_ID + P] = np.eye(P)
    inv = (np.float32(10000.0) ** (-np.arange(32, dtype=np.float32) / np.float32(32))).astype(np.float32)
    pos = np.arange(T, dtype=np.float32)
    ang = (pos[:, None] * inv[None, :]).astype(np.float32).astype(np.float64)
    cos, sin = np.cos(ang).astype(np.float32), np.sin(ang).astype(np.float32)
    for tt in range(TT):
        rows = slice(tt * P, tt * P + P)
        t[:, TB_COS + 64 * tt:TB_COS + 64 * tt + 64] = np.concatenate([cos[rows], cos[rows]], 1)
        t[:, TB_SIN + 32 * tt:TB_SIN + 32 * tt + 32] = sin[rows]
        t[:, TB_CAUSAL + T * tt:TB_CAUSAL + T * tt + T] = np.where(
            np.arange(T)[None, :] <= (tt * P + np.arange(P))[:, None], 0.0, NEG)
    t[:, TB_SLOT:TB_SLOT + SLOTS] = FAR + np.arange(SLOTS)
    t[:, TB_EXP:TB_EXP + NE] = np.arange(NE)
    t[:, TB_TRI:TB_TRI + P] = np.arange(P)[:, None] < np.arange(P)[None, :]
    t[:, TB_ONE:TB_ONE + P] = 1.0
    return t


JOBS = (["X0", "X1", "X2", "X3", "U0", "U1", "T0", "T1", "T2", "T3", "T4", "T5", "T6", "T7"]
        + ["S0", "S1", "S2", "S3", "QI0", "QI1", "QI2", "QI3", "KK", "Q0", "Q1"]
        + [f"R0_{n}" for n in range(4)] + [f"R1_{n}" for n in range(8)]
        + ["A0", "GLU0", "GLU1", "A1", "P0_0", "P0_1", "A2", "A3", "PS0", "PS1", "PS2", "PS3"]
        + [f"P1_{n}" for n in range(4)] + ["HX0", "HX1", "HX2", "HX3"])
JOB = {name: n for n, name in enumerate(JOBS)}

CHUNKS = (["U0", "U1"] + [f"T{n}" for n in range(8)] + [f"S{n}" for n in range(4)] + ["A0", "GLU", "A1", "A2", "A3"]
          + ["PS0", "PS1", "PA0", "PA1"] + [f"W{n}" for n in range(4)])
CHUNK = {name: n for n, name in enumerate(CHUNKS)}
NSLOT = 4
SLOT = {name: n % NSLOT for n, name in enumerate(CHUNKS)}


def loads_until(name):
    return CHUNK[name] // NSLOT + 1


def before(name):
    return CHUNKS[CHUNK[name] - NSLOT]


def build(nc, io, out):
    fp32, i32, u32 = mybir.dt.float32, mybir.dt.int32, mybir.dt.uint32
    ALU, ACT, AX = mybir.AluOpType, mybir.ActivationFunctionType, mybir.AxisListType

    with ExitStack() as ctx:
        def sb(name, shape, dt=fp32):
            return ctx.enter_context(nc.sbuf_tensor(name, shape, dt))

        def sem(name):
            return ctx.enter_context(nc.semaphore(name))

        SW = 2048
        NW_IN, NW_OUT = KD, KF // 2
        NW = NW_IN + NW_OUT
        ring = sb("ring", [P, NW * SW])

        def early(at, *dims):
            n = int(np.prod(dims))
            v = ring[:, at:at + n]
            if len(dims) == 2:
                v = v.rearrange("p (a b) -> p a b", a=dims[0])
            return v

        phase_re, phase_im = early(0, NCH, T), early(NCH * T, NCH, T)
        prod = [early(2 * NCH * T + n * 4 * T, 4, T) for n in range(4)]
        state_re, state_im = early(12288, 4, T), early(13312, 4, T)
        xs_re, xs_im = early(14336, 4, T), early(15360, 4, T)
        b_nat = [early(14336 + 512 * n, 4, P) for n in range(2)]
        c_nat = [early(15360 + 512 * n, 4, P) for n in range(2)]
        gate_s, gate_a = early(16384, KD, T), early(18432, KD, T)
        prod_out = [early(18432 + n * 4 * T, 4, T) for n in range(4)]
        p_ssm = early(14336, KD, T)
        y_ssm, y_att = early(20480, KS, T), early(21504, KS, T)
        c_t = [early(23552 + 512 * n, 4, P) for n in range(2)]

        table = sb("table", [P, TB_END - MIX_TABLES])
        x = sb("x", [P, TT, D])
        xs = sb("xs", [P, TT, D])
        x_t = sb("x_t", [P, KD, T])
        wbuf = sb("wbuf", [P, NSLOT, SW])
        mixed = sb("mixed", [P, KD, T])
        u_in = sb("u_in", [P, KS, T])
        b_in, b_out = [u_in[:, 2 * n:2 * n + 2, :].rearrange("p k t -> p (k t)") for n in range(2)]
        vec_rows = sb("vec_rows", [72, P])
        dt_rows = sb("dt_rows", [NCH, P])
        dt_pair = sb("dt_pair", [NCH, 2])
        vec = sb("vec", [P, 72])
        par = sb("par", [P, 24, NCH])
        stat = sb("stat", [P, 64])
        LATE = TT * NTOK + 2 * NCH * P
        ROUT = LATE + MIX_TABLES
        late = sb("late", [P, ROUT + (KD + 1) * NE])
        w_rout = late[:, ROUT:ROUT + KD * NE].rearrange("p (k e) -> p k e", k=KD)
        b_rout = late[:, ROUT + KD * NE:ROUT + (KD + 1) * NE]
        flag = sb("flag", [1, 1], i32)

        def constants(at, n):
            return table[:, at - MIX_TABLES:at - MIX_TABLES + n]

        def mixers_constants(at, n):
            return late[:, LATE + at:LATE + at + n]
        ident = constants(TB_ID, P)
        slot_no = constants(TB_SLOT, SLOTS)
        exp_no = constants(TB_EXP, NE)
        tri = constants(TB_TRI, P)
        ones = constants(TB_ONE, P)
        cos_t = mixers_constants(TB_COS, TT * 64).rearrange("p (t d) -> p t d", t=TT)
        sin_t = mixers_constants(TB_SIN, TT * 32).rearrange("p (t d) -> p t d", t=TT)
        causal = mixers_constants(TB_CAUSAL, TT * T).rearrange("p (t s) -> p t s", t=TT)

        V_G1, V_G2, V_BG, V_BGLU, V_D, V_LR, V_LI = 0, 8, 16, 32, 36, 40, 56
        L_RE, L_IM = vec[:, V_LR:V_LR + NCH], vec[:, V_LI:V_LI + NCH]

        ptok = late[:, 0:TT * NTOK].rearrange("p (t n) -> p t n", t=TT)
        o = TT * NTOK
        b_t = [late[:, o + 2048 * n:o + 2048 * n + 2048].rearrange("p (j c) -> p j c", c=P) for n in range(2)]
        score = late[:, o:o + TT * T].rearrange("p (t s) -> p t s", t=TT)
        taken = late[:, o + 512:o + 1024].rearrange("p (t s) -> p t s", t=TT)
        bias = late[:, o + 1024:o + 1536].rearrange("p (t s) -> p t s", t=TT)
        ki_two = late[:, o + 1024:o + 1280].rearrange("p (t n d) -> p t n d", t=TT, n=2)
        relu = late[:, o + 1536:o + 2560].rearrange("p (b s) -> p b s", b=2)
        q_t = late[:, o + 2560:o + 3584].rearrange("p (k t) -> p k t", k=4)
        k_t = early(22528, 2, T)
        ki_t = late[:, o + 3584:o + 4096].rearrange("p (n s) -> p n s", n=2)
        rope_a, rope_b = mixed, xs
        qi_t = xs[:, :, :].rearrange("p t (k s) -> p (t k) s", s=T)
        logit = xs[:, :, :].rearrange("p t (h s) -> p (t h) s", s=T)
        prob_t = mixed[:, :, :].rearrange("p k t -> p (k t)")
        glu_g = prod[0]
        y_raw, y_gelu = prod[2], prod[3]

        def cut(at, n):
            return late[:, at:at + n]
        h_tok, gate_z, lin_z, sig = [cut(512 * n, 512) for n in range(4)]
        act = lin_z
        h_sel = cut(2048, 512).rearrange("p (j q s) -> p j q s", q=2, s=SLOTS)
        act_t = cut(2560, 512).rearrange("p (j q s) -> p j q s", q=2, s=SLOTS)
        y_tok = h_tok
        gated = cut(3072, TT * 2 * SLOTS).rearrange("p (t q s) -> p t q s", t=TT, q=2)
        one_hot = cut(3328, TT * SLOTS).rearrange("p (t s) -> p t s", t=TT)
        chosen = cut(3456, 4 * SLOTS).rearrange("p (n s) -> p n s", n=4)

        def act_tile(k):
            return act_t[:, 2 * (k // 4) + k % 2, k // 2 % 2, :]
        place = cut(3712, TT * NE).rearrange("p (t e) -> p t e", t=TT)
        gates_two = cut(3776, TT * 2 * NE).rearrange("p (t q e) -> p t q e", t=TT, q=2)
        gates = gates_two[:, :, 0, :]
        gates_t = late[0:2 * NE, 3904:3904 + T]
        gated_t = cut(4160, 2 * T).rearrange("p (q t) -> p q t", q=2)
        rsum = cut(512, T)
        picked = cut(768, TT * NE).rearrange("p (t e) -> p t e", t=TT)
        rlog = cut(832, TT * NE).rearrange("p (t e) -> p t e", t=TT)
        top8 = cut(896, TT * 8).rearrange("p (t k) -> p t k", t=TT)
        top8i = late[:, 912:912 + TT * 8].bitcast(u32).rearrange("p (t k) -> p t k", t=TT)
        top8f = cut(928, TT * 8).rearrange("p (t k) -> p t k", t=TT)
        topw = cut(944, TT * 8).rearrange("p (t k) -> p t k", t=TT)
        hot4 = cut(960, TT * TOPE * NE).rearrange("p (t k e) -> p t k e", t=TT, k=TOPE)
        hot4w = cut(1216, TT * TOPE * NE).rearrange("p (t k e) -> p t k e", t=TT, k=TOPE)
        final = xs

        ps = ctx.enter_context(nc.psum_tensor("ps", [P, 8, 512], fp32))
        rot = [ps[:, 0, :], ps[:, 1, :]]

        extra = [wbuf[:, SLOT[f"W{n}"], :] for n in range(4)] \
            + [cut(4672, SW), mixed[:, :, :].rearrange("p k t -> p (k t)"),
               x_t[:, :, :].rearrange("p k t -> p (k t)"), x[:, :, :].rearrange("p t d -> p (t d)"),
               cut(4672 + SW, SW)]
        gfin = ring[:, 0:D]

        ident_in, tables_in, vec_in, misc_in, bnat_in, cnat_in = [sem(n) for n in (
            "ident_in", "tables_in", "vec_in", "misc_in", "bnat_in", "cnat_in")]
        x_in = [sem(f"x_in{t}") for t in range(TT)]
        spare_ok = sem("spare_ok")
        w_slot_in = [sem(f"w_slot_in{n}") for n in range(NSLOT)]
        zeroed = sem("zeroed")
        sum_sq, root, x_norm = sem("sum_sq"), sem("root"), sem("x_norm")
        rot_done, rot_free = sem("rot_done"), sem("rot_free")
        small_t, small_free = sem("small_t"), sem("small_free")
        par_v, par_s = sem("par_v"), sem("par_s")
        b_ready, c_ready = sem("b_ready"), sem("c_ready")
        bu_done, bu_used, w_rot, scanned, x_state, y_done, y_raw_ok = [sem(n) for n in (
            "bu_done", "bu_used", "w_rot", "scanned", "x_state", "y_done", "y_raw_ok")]
        phase_v, phase_p = sem("phase_v"), sem("phase_p")
        roped = sem("roped")
        relu_used = sem("relu_used")
        gelu_ok, y_ssm_ok = sem("gelu_ok"), sem("y_ssm_ok")
        logit_done, logit_used, row_max, expd, prob_ok, att_done, att_out = [sem(n) for n in (
            "logit_done", "logit_used", "row_max", "expd", "prob_ok", "att_done", "att_out")]
        gated_a = sem("gated_a")
        proj_done, mixed_ok, wout_done, x1_ok = [sem(n) for n in ("proj_done", "mixed_ok", "wout_done", "x1_ok")]
        rlogit_sb = sem("rlogit_sb")
        rlogit, top_ok, top_exp, picked_ok, placed, route_ok, flag_ok, gates_tr, gates_t_ok = [sem(n) for n in (
            "rlogit", "top_ok", "top_exp", "picked_ok", "placed", "route_ok", "flag_ok", "gates_tr",
            "gates_t_ok")]
        moe_in = [sem(f"moe_in{n}") for n in range(NW)]
        extra_in = [sem(f"extra_in{n}") for n in range(NX)]
        b_in_in, b_out_in, gfin_in = sem("b_in_in"), sem("b_out_in"), sem("gfin_in")
        chunk_used = sem("chunk_used")
        hot_ok, gathered, h_tok_ok, h_trans, h_sel_ok, chosen_ok, z_gate, z_lin, sig_ok, z_prod, act_ok, act_trans, \
            act_t_ok, y_tok_ok, gated_eq, gated_ok, gated_trans, gated_t_ok, sum_ok = [sem(n) for n in (
                "hot_ok", "gathered", "h_tok_ok", "h_trans", "h_sel_ok", "chosen_ok", "z_gate", "z_lin", "sig_ok",
                "z_prod", "act_ok", "act_trans", "act_t_ok", "y_tok_ok", "gated_eq", "gated_ok", "gated_trans",
                "gated_t_ok", "sum_ok")]
        place_ok = sem("place_ok")
        first_rstd, rstd_ok = sem("first_rstd"), sem("rstd_ok")
        sum_open, squared, tile_ok, first_sum_ok, under_gains = sem("sum_open"), sem("squared"), sem("tile_ok"), sem("first_sum_ok"), sem("under_gains")
        out_ready, stored = [sem(f"out_ready{t}") for t in range(TT)], sem("stored")
        v_chain, a_chain, g_chain = sem("v_chain"), sem("a_chain"), sem("g_chain")

        w_in = io["w_in"].rearrange("(k p) n -> p k n", p=P)
        w_glu = io["w_glu"].rearrange("(k p) n -> p k n", p=P)
        w_ps = io["w_proj_ssm"].rearrange("(k p) n -> p k n", p=P)
        w_pa = io["w_proj_attn"].rearrange("(k p) n -> p k n", p=P)
        w_out = io["w_out"].rearrange("(k p) n -> p k n", p=P)

        vector_rows = [(V_G1, io["norm1_g"], 8), (V_G2, io["norm2_g"], 8), (V_BG, io["b_gate"], 16),
                       (V_BGLU, io["b_glu"], 4), (V_D, io["ssm_d"], 4), (V_LR, io["ssm_lam_re"], NCH),
                       (V_LI, io["ssm_lam_im"], NCH)]

        def chunk_view(name):
            slot = wbuf[:, SLOT[name], :]
            wide = slot.rearrange("p (k n) -> p k n", k=KD)
            deep = slot.rearrange("p (k n) -> p k n", k=KS)
            n = int(name[-1]) if name != "GLU" else 0
            if name == "GLU":
                return deep, w_glu
            if name[:2] == "PS":
                return deep, w_ps[:, :, 512 * n:512 * n + 512]
            if name[:2] == "PA":
                return deep, w_pa[:, :, 512 * n:512 * n + 512]
            if name[0] == "T":
                c, w = TOK[n]
                return wide[:, :, 0:w], w_in[:, :, c:c + w]
            c = {"U": C_U, "S": C_GS, "A": C_GA}.get(name[0])
            src = w_out if c is None else w_in
            return wide, src[:, :, (c or 0) + 256 * n:(c or 0) + 256 * n + 256]

        def chunk_arrived(eng, name):
            eng.wait_ge(w_slot_in[SLOT[name]], 16 * loads_until(name))

        def chunk_done(name):
            if name == "GLU":
                return rot_done, JOB["GLU1"] + 1
            if name[:2] == "PS":
                return rot_done, JOB[f"PS{2 * int(name[-1]) + 1}"] + 1
            if name[:2] == "PA":
                return proj_done, 2 * (int(name[-1]) + 1)
            if name[0] == "W":
                return wout_done, int(name[1]) + 1
            return rot_done, JOB[name] + 1

        def expert_chunk(e, c):
            if c < NW_IN:
                return io["w_moe_in"][bass.ds(e, 1), c * P:(c + 1) * P, :].rearrange("o p n -> p (o n)")
            r = (c - NW_IN) * 2 * P
            return io["w_moe_out"][bass.ds(e, 1), r:r + 2 * P, :].rearrange("o (k p) n -> p (o k) n", p=P)

        def shaped(v, c):
            return v if c < NW_IN else v.rearrange("p (k n) -> p k n", k=2)

        def ring_slot(c):
            return shaped(ring[:, c * SW:(c + 1) * SW], c)

        def extra_place(c):
            return shaped(extra[c], c)

        def passes(eng, one_pass):
            one_pass(0, 0)
            eng.wait_ge(flag_ok, 1)
            most = eng.value_load(flag[0:1, 0:1], min_val=0, max_val=T)
            with eng.If(most > SLOTS):
                with eng.Fori(1, PASSES) as c:
                    with eng.If(most > c * SLOTS):
                        one_pass(c, c * NE)
                    eng.end_ifs()
            eng.end_ifs()

        def split(n):
            return NCH if n < 32 else 10

        block = ctx.enter_context(nc.Block())

        @block.sync
        def _(sp):
            sp.dma_start(x[:, 0, :], io["x"][0:P, :]).then_inc(x_in[0], 16)
            for at, src, n in vector_rows:
                sp.dma_start(vec_rows[at:at + n, :], src.rearrange("(r c) -> r c", c=P)).then_inc(vec_in, 16)
            sp.dma_start(dt_pair[:, :], io["ssm_log_dt"].rearrange("(j g) -> j g", g=2)).then_inc(vec_in, 16)

            def load(name):
                if CHUNK[name] >= NSLOT:
                    sp.wait_ge(*chunk_done(before(name)))
                dst, src = chunk_view(name)
                sp.dma_start(dst, src).then_inc(w_slot_in[SLOT[name]], 16)

            load("U0")
            load("U1")
            sp.wait_ge(zeroed, 4)
            for n, name in enumerate(("ssm_b_re", "ssm_b_im")):
                src = io[name].rearrange("(j two) p h -> two p j h", two=2)
                for q in range(2):
                    dst = b_nat[n][64 * q:64 * q + 64].rearrange("p a (b two h) -> p two (a b) h", two=2, h=H)
                    sp.dma_start(dst[:, q], src[q]).then_inc(bnat_in, 16)
            for n, name in enumerate(("ssm_c_re", "ssm_c_im")):
                src = io[name].rearrange("(a b) h p -> b h a p", b=8)
                for b in range(8):
                    q = b % 2
                    sp.dma_start(c_nat[n][16 * b:16 * b + 16, :, 64 * q:64 * q + 64], src[b]).then_inc(cnat_in, 16)
            sp.dma_start(w_rout[:, :, :], io["w_router"].rearrange("(k p) e -> p k e", p=P)).then_inc(misc_in, 16)
            sp.dma_start(b_rout[:, :], io["b_router"].unsqueeze(0).to_broadcast([P, NE])).then_inc(misc_in, 16)
            def load_first(slots):
                for n in slots:
                    sp.dma_start(ring_slot(n), expert_chunk(0, n)).then_inc(moe_in[n], 16)

            for name in CHUNKS[2:CHUNK["A3"]]:
                load(name)
            sp.wait_ge(scanned, 8)
            load_first((0, 1, 2, 3, 6))
            for name in CHUNKS[CHUNK["A3"]:CHUNK["W2"]]:
                load(name)
            sp.wait_ge(rot_free, JOB["GLU1"] + 1)
            sp.wait_ge(y_ssm_ok, 1)
            load_first((4, 5))
            sp.wait_ge(att_done, 2)
            sp.dma_start(extra_place(4), expert_chunk(1, 4)).then_inc(extra_in[4], 16)
            load("W2")
            load("W3")
            sp.wait_ge(mixed_ok, 4)
            load_first(range(7, NW))
            for n in range(4):
                sp.dma_start(b_in[NE * n:NE * n + NE], io["b_moe_in"][:, 512 * n:512 * n + 512]).then_inc(b_in_in, 16)
            for n in range(2):
                sp.dma_start(b_out[NE * n:NE * n + NE], io["b_moe_out"][:, 512 * n:512 * n + 512]).then_inc(
                    b_out_in, 16)
            for n, done in ((0, (wout_done, 1)), (1, (wout_done, 2)), (2, (wout_done, 3)), (3, (wout_done, 4)),
                            (5, (wout_done, 4)), (6, (rlogit, 1)), (8, (top_ok, 1)), (7, (sum_open, 1))):
                sp.wait_ge(*done)
                if n == 7:
                    sp.wait_ge(x_norm, 2 * TT)
                sp.dma_start(extra_place(n), expert_chunk(1, n)).then_inc(extra_in[n], 16)

            def one_pass(c, first):
                def load_chunk(e, n, odd):
                    sp.wait_ge(chunk_used, (e + first - (2 if n < NX else 1)) * NW + n + 1)
                    dst, done = (extra_place(n), extra_in[n]) if odd and n < NX else (ring_slot(n), moe_in[n])
                    sp.dma_start(dst, expert_chunk(e, n)).then_inc(done, 16)
                if isinstance(c, int):
                    for e in range(2, LEAD + 1):
                        for n in range(NX):
                            load_chunk(e, n, e % 2)
                        for n in range(NX, NW):
                            load_chunk(e - 1, n, (e - 1) % 2)
                    for n in range(NX, NW):
                        load_chunk(LEAD, n, 0)
                    for n in range(NW):
                        load_chunk(LEAD + 1, n, 1)
                with sp.Fori(LEAD // 2 + 1 if isinstance(c, int) else 0, NE // 2) as m:
                    for odd in range(2):
                        for n in range(NW):
                            load_chunk(2 * m + odd, n, odd)
            passes(sp, one_pass)
            sp.dma_start(gfin, io["norm_f_g"].unsqueeze(0).to_broadcast([P, D])).then_inc(gfin_in, 16)
            for t in range(TT):
                sp.wait_ge(out_ready[t], 1)
                sp.dma_start(out[t * P:(t + 1) * P, :], final[:, t, :]).then_inc(stored, 16)
            sp.wait_ge(stored, 16 * TT)

        @block.gpsimd
        def _(gp):
            chain = [0]

            def link(ins):
                chain[0] += 1
                ins.then_inc(g_chain, 1)
                gp.wait_ge(g_chain, chain[0])

            gp.memset(stat[:, 60:61], 1.0).then_inc(spare_ok, 1)
            for v in b_nat + c_nat + b_t + [k_t]:
                gp.memset(v, 0.0).then_inc(zeroed, 1)

            n = 1
            k = 0
            while n < T:
                lo_re, lo_im = phase_re[:, :, 0:n], phase_im[:, :, 0:n]
                a_re = par[:, 8 + 2 * (k % 2), :].unsqueeze(2).to_broadcast([P, NCH, n])
                a_im = par[:, 9 + 2 * (k % 2), :].unsqueeze(2).to_broadcast([P, NCH, n])
                t1 = ring[:, 2 * NCH * T:2 * NCH * T + NCH * n].rearrange("p (c t) -> p c t", c=NCH)
                t2 = ring[:, 2 * NCH * T + 2048:2 * NCH * T + 2048 + NCH * n].rearrange("p (c t) -> p c t", c=NCH)
                m = split(n)
                gp.wait_ge(phase_v, k + 1)
                gp.tensor_tensor(t1[:, 0:m], lo_re[:, 0:m], a_im[:, 0:m], ALU.mult)
                link(gp.tensor_tensor(t2[:, 0:m], lo_im[:, 0:m], a_re[:, 0:m], ALU.mult))
                gp.tensor_tensor(phase_im[:, 0:m, n:2 * n], t1[:, 0:m], t2[:, 0:m], ALU.add).then_inc(phase_p, 1)
                gp.wait_ge(phase_p, k + 1)
                n *= 2
                k += 1

            def rope(c, heads, job, parts=None):
                src = ptok[:, :, c - C_Q:c - C_Q + 64 * heads].rearrange("p t (h d) -> p t h d", d=64)
                a = mixed[:, :, :].rearrange("p k t -> p (k t)")[:, 0:TT * heads * 64].rearrange(
                    "p (t h d) -> p t h d", t=TT, d=64)
                b = xs[:, :, :].rearrange("p k t -> p (k t)")[:, 0:TT * heads * 64].rearrange(
                    "p (t h d) -> p t h d", t=TT, d=64)
                cb = cos_t.unsqueeze(2).to_broadcast([P, TT, heads, 64])
                sn = sin_t.unsqueeze(2).to_broadcast([P, TT, heads, 32])
                gp.wait_ge(rot_free, JOB[job] + 1)
                gp.tensor_tensor(a, src, cb, ALU.mult)
                gp.tensor_tensor(b[:, :, :, 0:32], src[:, :, :, 32:64], sn, ALU.mult)
                link(gp.tensor_tensor(b[:, :, :, 32:64], src[:, :, :, 0:32], sn, ALU.mult))
                for hs, dst in parts or [(slice(0, heads), src)]:
                    gp.tensor_tensor(dst[:, :, :, 0:32], a[:, :, hs, 0:32], b[:, :, hs, 0:32], ALU.subtract)
                    ins = gp.tensor_tensor(dst[:, :, :, 32:64], a[:, :, hs, 32:64], b[:, :, hs, 32:64], ALU.add)
                ins.then_inc(roped, 1)
                ropes[0] += 1
                gp.wait_ge(roped, ropes[0])
            ropes = [0]

            def rotated(i):
                gp.wait_ge(scanned, 2 * i + 2)
                if i:
                    gp.wait_ge(y_done, i)
                gp.tensor_tensor(xs_re, prod_out[0], prod_out[1], ALU.subtract)
                gp.tensor_tensor(xs_im, prod_out[2], prod_out[3], ALU.add).then_inc(x_state, 1)

            gp.wait_ge(c_ready, 1)
            gp.wait_ge(tables_in, 32)
            rope(C_QI, IH, "T4")
            rotated(0)
            rope(C_K, NKV, "T5")
            rotated(1)
            gp.wait_ge(bu_done, 4)
            rope(C_KI, 1, "T4", [(slice(0, 1), ki_two[:, :, n:n + 1, :]) for n in range(2)])
            rotated(2)
            qv = ptok[:, :, 0:NH * HD].rearrange("p t (h g d) -> p g t h d", g=2, d=HD)
            rope(C_Q, NH, "T7", [(slice(4 * g, 4 * g + 4), qv[:, g]) for g in range(2)])
            rotated(3)
            gp.memset(ki_t, 0.0).then_inc(zeroed, 1)
            gp.wait_ge(att_done, 2)
            gp.memset(gated_t, 0.0).then_inc(zeroed, 1)

        @block.scalar
        def _(ac):
            ac.dma_start(ident, io["tables"][:, TB_ID:TB_ID + P]).then_inc(ident_in, 16)
            ac.dma_start(x[:, 1, :], io["x"][P:2 * P, :]).then_inc(x_in[1], 16)
            ac.dma_start(mixers_constants(0, MIX_TABLES), io["tables"][:, 0:MIX_TABLES]).then_inc(tables_in, 16)
            ac.dma_start(constants(TB_SLOT, TB_END - TB_SLOT), io["tables"][:, TB_SLOT:]).then_inc(tables_in, 16)

            chain = [0]

            def link(ins):
                chain[0] += 1
                ins.then_inc(a_chain, 1)
                ac.wait_ge(a_chain, chain[0])

            def squares(t):
                return ac.activation(mixed[:, 4 * t:4 * t + 4, :], x[:, t, :].rearrange("p (k s) -> p k s", k=4),
                                     ACT.Square, accum_out=stat[:, t:t + 1])

            def ready(function):
                link(ac.activation(stat[:, 61:62], stat[:, 60:61], function))

            ac.wait_ge(spare_ok, 1)
            ready(ACT.Sqrt)
            ac.wait_ge(x_in[0], 16)
            link(squares(0))
            ac.wait_ge(x_in[1], 16)
            squares(1).then_inc(sum_sq, 1)
            ac.wait_ge(sum_sq, 2)
            ac.activation(stat[:, 4:6], stat[:, 2:4], ACT.Sqrt).then_inc(root, 1)

            def job(name):
                ac.wait_ge(rot_done, JOB[name] + 1)
                return rot[JOB[name] % 2]

            def norm_t(name, n, gain):
                b = job(name)
                for k in (2 * n, 2 * n + 1):
                    i = ac.activation(x_t[:, k, :], b[:, (k % 2) * T:(k % 2) * T + T], ACT.Copy,
                                      scale=vec[:, gain + k:gain + k + 1])
                i.then_inc(rot_free, 1)

            ac.wait_ge(small_free, 2)
            for n in range(4):
                norm_t(f"X{n}", n, V_G1)
            ac.activation(par[:, 0, :], par[:, 0, :], ACT.Exp).then_inc(par_s, 1)
            ac.wait_ge(par_v, 1)
            ac.activation(par[:, 2, :], par[:, 1, :], ACT.Exp).then_inc(par_s, 1)
            ac.activation(par[:, 5, :], par[:, 4, :], ACT.Sin).then_inc(par_s, 1)
            ac.activation(par[:, 6, :], par[:, 4, :], ACT.Sin, scale=0.5).then_inc(par_s, 1)
            ac.wait_ge(zeroed, 6)
            ac.wait_ge(small_t, 2)
            for n in range(2):
                for i in range(4):
                    r = slice(32 * i, 32 * i + 32)
                    ins = ac.activation(b_t[n].rearrange("p (a b) c -> p a b c", b=4)[r, :, i, :],
                                        ps[r, 4 + n, :].rearrange("p (a c) -> p a c", a=4), ACT.Copy)
            ins.then_inc(b_ready, 1)
            for n in range(2):
                b = job(f"U{n}")
                ac.activation(u_in[:, 2 * n:2 * n + 2, :], b.rearrange("p (k t) -> p k t", k=2), ACT.Copy).then_inc(rot_free, 1)
            for n, (c, w) in enumerate(TOK):
                b = job(f"T{n}")
                ac.activation(ptok[:, :, c - C_Q:c - C_Q + w], b[:, 0:TT * w].rearrange("p (t n) -> p t n", t=TT),
                              ACT.Copy).then_inc(rot_free, 1)

            def gate(letter, dst, at, n):
                b = job(f"{letter}{n}")
                for m in (2 * n, 2 * n + 1):
                    i = ac.activation(dst[:, m, :], b[:, (m % 2) * T:(m % 2) * T + T], ACT.Sigmoid,
                                      bias=vec[:, at + m:at + m + 1])
                i.then_inc(rot_free, 1)

            for n in range(4):
                gate("S", gate_s, V_BG, n)
            for n in range(4):
                b = job(f"QI{n}")
                ac.activation(qi_t[:, 2 * n:2 * n + 2, :], b.rearrange("p (k t) -> p k t", k=2),
                              ACT.Copy).then_inc(rot_free, 1)
            b = job("KK")
            ac.wait_ge(zeroed, 8)
            for n in range(2):
                r = slice(64 * n, 64 * n + 64)
                ac.activation(ki_t[r, n, :], b[r, 0:T], ACT.Copy)
                i = ac.activation(k_t[r, n, :], b[r, T:2 * T], ACT.Copy)
            i.then_inc(rot_free, 1)
            for n in range(2):
                b = job(f"Q{n}")
                ac.activation(q_t[:, 2 * n:2 * n + 2, :], b.rearrange("p (k t) -> p k t", k=2),
                              ACT.Copy).then_inc(rot_free, 1)
            ac.wait_ge(y_raw_ok, 1)
            ac.activation(y_gelu, y_raw, ACT.Gelu_apprx_tanh).then_inc(gelu_ok, 1)
            r = 0
            for t in range(TT):
                for n in range(4 * (t + 1)):
                    b = job(f"R{t}_{n}")
                    if r >= 2:
                        ac.wait_ge(relu_used, r - 1)
                    ac.activation(relu[:, r % 2, :], b, ACT.Relu).then_inc(rot_free, 1)
                    r += 1

            def exponentials(t):
                w = P * (t + 1)
                ac.wait_ge(row_max, t + 1)
                for h in range(NH):
                    i = ac.activation(logit[:, h, 0:w], logit[:, h, 0:w], ACT.Exp,
                                      bias=stat[:, 8 + h:9 + h], accum_out=stat[:, 16 + h:17 + h])
                i.then_inc(expd, 1)

            def attended(t):
                for n in range(2 * (t + 1)):
                    b = job(f"P{t}_{n}")
                    ac.activation(prob_t[:, 512 * n:512 * n + 512], b, ACT.Copy).then_inc(rot_free, 1)
                ac.wait_ge(att_done, t + 1)
                ac.activation(y_att[:, :, t * P:t * P + P], ps[:, 2 + t, :].rearrange("p (k t) -> p k t", k=KS),
                              ACT.Copy).then_inc(att_out, 1)

            gate("A", gate_a, V_BG + KD, 0)
            exponentials(0)
            for n in range(2):
                b = job(f"GLU{n}")
                for m in (2 * n, 2 * n + 1):
                    i = ac.activation(glu_g[:, m, :], b[:, (m % 2) * T:(m % 2) * T + T], ACT.Sigmoid,
                                      bias=vec[:, V_BGLU + m:V_BGLU + m + 1])
                i.then_inc(rot_free, 1)
            gate("A", gate_a, V_BG + KD, 1)
            attended(0)
            gate("A", gate_a, V_BG + KD, 2)
            exponentials(1)
            gate("A", gate_a, V_BG + KD, 3)
            for n in range(4):
                b = job(f"PS{n}")
                ac.activation(p_ssm[:, 2 * n:2 * n + 2, :], b.rearrange("p (k t) -> p k t", k=2),
                              ACT.Copy).then_inc(rot_free, 1)
            attended(1)
            ready(ACT.Sqrt)
            for n in range(4):
                ac.wait_ge(x1_ok, n + 1)
                for t in range(TT):
                    i = ac.activation(late[:, 0:256], x[:, t, 256 * n:256 * n + 256], ACT.Square,
                                      accum_out=stat[:, 48 + TT * n + t:49 + TT * n + t])
                    if n < 3 or t == 0:
                        link(i)
                if n == 3:
                    i.then_inc(sum_sq, 1)
                if n:
                    norm_t(f"HX{n - 1}", n - 1, V_G2)
            ac.wait_ge(sum_sq, 4)
            ac.activation(stat[:, 4:6], stat[:, 2:4], ACT.Sqrt).then_inc(root, 1)
            norm_t("HX3", 3, V_G2)
            ac.wait_ge(rlogit, 1)
            ac.activation(rsum, ps[:, 2, 0:T], ACT.Copy).then_inc(rlogit_sb, 1)
            ready(ACT.Exp)
            ac.wait_ge(rstd_ok, 1)
            for t in range(TT):
                ac.activation(xs[:, t, :], x[:, t, :], ACT.Copy, scale=stat[:, 6 + t:7 + t]).then_inc(x_norm, 1)
            ac.wait_ge(top_ok, 1)
            ac.activation(topw[:, :, 0:TOPE], topw[:, :, 0:TOPE], ACT.Exp).then_inc(top_exp, 1)

            def one_pass(c, first):
                def gathered_rows(j):
                    ac.wait_ge(gathered, j + 1)
                    ac.activation(h_tok, ps[:, 3, :], ACT.Copy).then_inc(h_tok_ok, 1)

                def body(j, tail=False):
                    ac.wait_ge(z_gate, j + 1)
                    ac.activation(sig, gate_z, ACT.Sigmoid, scale=ALPHA).then_inc(sig_ok, 1)
                    if not tail:
                        gathered_rows(j + 1)
                    ac.wait_ge(act_trans, j + 1)
                    ac.activation(act_t, ps[:, 0, :].rearrange("p (j q s) -> p j q s", q=2, s=SLOTS),
                                  ACT.Copy).then_inc(act_t_ok, 1)
                    ac.wait_ge(chunk_used, j * NW + NW)
                    ac.activation(y_tok, ps[:, 2, :], ACT.Copy).then_inc(y_tok_ok, 1)
                gathered_rows(first)
                body(first)
                with ac.Fori(1, NE - 1) as e:
                    body(e + first)
                body(first + NE - 1, tail=True)
            passes(ac, one_pass)
            ready(ACT.Sqrt)
            for n, bank_free in enumerate(((tile_ok, 1), (under_gains, 1), (sum_ok, 1), (under_gains, 3))):
                ac.wait_ge(*bank_free)
                ac.activation(late[:, 512 * n + 512:512 * n + 1024], ps[:, 4 + n, :], ACT.Square,
                              accum_out=stat[:, 48 + n:49 + n]).then_inc(squared if n < 3 else sum_sq, 1)
            ac.wait_ge(sum_sq, 6)
            ac.activation(stat[:, 4:6], stat[:, 2:4], ACT.Sqrt).then_inc(root, 1)
            ac.wait_ge(rstd_ok, 2)
            ac.wait_ge(under_gains, 4)
            ac.activation(final[:, 1, :], final[:, 1, :], ACT.Copy, scale=stat[:, 7:8]).then_inc(out_ready[1], 1)

        @block.vector
        def _(ve):
            chain = [0]

            def link(ins):
                chain[0] += 1
                ins.then_inc(v_chain, 1)
                ve.wait_ge(v_chain, chain[0])

            def tt(out_, a, b, op):
                return ve.tensor_tensor(out_, a, b, op)

            def rstd(n, done):
                ve.wait_ge(sum_sq, 2 * n + 1)
                ve.tensor_scalar(stat[:, 2:4], stat[:, 0:2], 1.0 / D, EPS, ALU.mult, ALU.add).then_inc(sum_sq, 1)
                ve.wait_ge(root, n + 1)
                ve.reciprocal(stat[:, 6:8], stat[:, 4:6]).then_inc(done, 1)
                ve.wait_ge(done, max(n, 1))

            rstd(0, first_rstd)
            for t in range(TT):
                ve.tensor_scalar(xs[:, t, :], x[:, t, :], stat[:, 6 + t:7 + t], None, ALU.mult).then_inc(x_norm, 1)
            ve.wait_ge(vec_in, 16 * 8)
            ve.tensor_copy(dt_rows[:, :].rearrange("j (g p) -> j g p", g=2),
                           dt_pair[:, :].unsqueeze(2).to_broadcast([NCH, 2, PS])).then_inc(small_free, 1)
            ve.wait_ge(small_free, 1)
            ve.wait_ge(small_t, 1)
            ve.tensor_copy(vec[:, :], ps[:, 7, 0:72])
            ve.tensor_copy(par[:, 0, :], ps[:, 7, 128:128 + NCH]).then_inc(small_free, 1)
            ve.wait_ge(small_free, 2)
            ve.wait_ge(tables_in, 32)
            pr = lambda n: par[:, n, :]
            DT, LRDT, MAG, ANG, RED, SIN_, HALF, COS = 0, 1, 2, 3, 4, 5, 6, 7
            ve.wait_ge(par_s, 1)
            link(tt(pr(LRDT), L_RE, pr(DT), ALU.mult))
            link(tt(pr(ANG), L_IM, pr(DT), ALU.mult))
            magic = 12582912.0
            c1 = 6.28125
            c2 = float(np.float32(round((TWO_PI - c1) * 2 ** 21) / 2 ** 21))
            c3 = TWO_PI - c1 - c2
            link(ve.tensor_scalar(pr(12), pr(ANG), 1.0 / TWO_PI, magic, ALU.mult, ALU.add))
            link(ve.tensor_scalar(pr(13), pr(12), magic, None, ALU.subtract))
            link(ve.scalar_tensor_tensor(pr(14), pr(13), -c1, pr(ANG), ALU.mult, ALU.add))
            link(ve.scalar_tensor_tensor(pr(12), pr(13), -c2, pr(14), ALU.mult, ALU.add))
            link(ve.scalar_tensor_tensor(pr(14), pr(13), -c3, pr(12), ALU.mult, ALU.add))
            ve.tensor_scalar(pr(RED), pr(14), 3.1415925, -3.1415925, ALU.min, ALU.max).then_inc(par_v, 1)
            ve.wait_ge(par_s, 4)
            link(tt(pr(12), pr(HALF), pr(HALF), ALU.mult))
            link(ve.tensor_scalar(pr(8), pr(12), -2.0, 1.0, ALU.mult, ALU.add))
            link(ve.tensor_copy(pr(9), pr(SIN_)))
            ve.memset(phase_re[:, :, 0:1], 1.0)
            ve.memset(phase_im[:, :, 0:1], 0.0).then_inc(phase_v, 1)
            ve.wait_ge(phase_v, 1)
            n, k = 1, 0
            link(tt(pr(16), pr(MAG), pr(8), ALU.mult))
            link(tt(pr(17), pr(MAG), pr(9), ALU.mult))
            ve.wait_ge(rot_done, JOB["X3"] + 1)
            while n < T:
                ar = pr(8 + 2 * (k % 2))
                ai = pr(9 + 2 * (k % 2))
                lo_re, lo_im = phase_re[:, :, 0:n], phase_im[:, :, 0:n]
                t1 = mixed[:, :, :].rearrange("p k t -> p (k t)")[:, 0:NCH * n].rearrange("p (c t) -> p c t", c=NCH)
                t2 = xs[:, :, :].rearrange("p k t -> p (k t)")[:, 0:NCH * n].rearrange("p (c t) -> p c t", c=NCH)
                if k:
                    ve.wait_ge(phase_p, k)
                tt(t1, lo_re, ar.unsqueeze(2).to_broadcast([P, NCH, n]), ALU.mult)
                link(tt(t2, lo_im, ai.unsqueeze(2).to_broadcast([P, NCH, n]), ALU.mult))
                link(tt(phase_re[:, :, n:2 * n], t1, t2, ALU.subtract))
                m = split(n)
                if m < NCH:
                    tt(t1[:, m:], lo_re[:, m:], ai[:, m:].unsqueeze(2).to_broadcast([P, NCH - m, n]), ALU.mult)
                    link(tt(t2[:, m:], lo_im[:, m:], ar[:, m:].unsqueeze(2).to_broadcast([P, NCH - m, n]), ALU.mult))
                    link(tt(phase_im[:, m:, n:2 * n], t1[:, m:], t2[:, m:], ALU.add))
                if 2 * n < T:
                    nr, ni = pr(8 + 2 * ((k + 1) % 2)), pr(9 + 2 * ((k + 1) % 2))
                    tt(pr(12), ar, ar, ALU.mult)
                    tt(pr(13), ai, ai, ALU.mult)
                    link(tt(pr(14), ar, ai, ALU.mult))
                    tt(nr, pr(12), pr(13), ALU.subtract)
                    ve.tensor_scalar(ni, pr(14), 2.0, None, ALU.mult).then_inc(phase_v, 1)
                    ve.wait_ge(phase_v, k + 2)
                n *= 2
                k += 1
            link(ve.tensor_scalar(pr(18), pr(16), -1.0, None, ALU.add))
            tt(pr(12), pr(18), L_RE, ALU.mult)
            link(tt(pr(13), pr(17), L_IM, ALU.mult))
            link(tt(pr(14), pr(12), pr(13), ALU.add))
            tt(pr(12), pr(17), L_RE, ALU.mult)
            link(tt(pr(13), pr(18), L_IM, ALU.mult))
            link(tt(pr(15), pr(12), pr(13), ALU.subtract))
            tt(pr(12), L_RE, L_RE, ALU.mult)
            link(tt(pr(13), L_IM, L_IM, ALU.mult))
            link(tt(pr(19), pr(12), pr(13), ALU.add))
            link(ve.reciprocal(pr(20), pr(19)))
            tt(pr(21), pr(14), pr(20), ALU.mult)
            link(tt(pr(22), pr(15), pr(20), ALU.mult))
            ve.wait_ge(small_t, 3)
            z_re = pr(21).unsqueeze(2).to_broadcast([P, NCH, 32])
            z_im = pr(22).unsqueeze(2).to_broadcast([P, NCH, 32])
            c_re = ps[:, 6, :].rearrange("p (j c) -> p j c", c=32)
            c_im = ps[:, 7, :].rearrange("p (j c) -> p j c", c=32)
            tv = [mixed[:, 2 * n:2 * n + 2, :].rearrange("p k t -> p (k t)").rearrange("p (j c) -> p j c", c=32)
                  for n in range(4)]
            tt(tv[0], c_re, z_re, ALU.mult)
            tt(tv[1], c_im, z_im, ALU.mult)
            tt(tv[2], c_re, z_im, ALU.mult)
            link(tt(tv[3], c_im, z_re, ALU.mult))
            ct = [c_t[n].rearrange("p a (b c) -> p (a b) c", c=32) for n in range(2)]
            tt(ct[0], tv[0], tv[1], ALU.subtract)
            ve.scalar_tensor_tensor(ct[1], tv[2], -1.0, tv[3], ALU.mult, ALU.subtract).then_inc(c_ready, 1)

            ve.wait_ge(phase_p, 8)
            for i in range(4):
                er, ei = phase_re[:, 4 * i:4 * i + 4, :], phase_im[:, 4 * i:4 * i + 4, :]
                bre = ps[:, 4:6, :].rearrange("p b (j t) -> p (b j) t", t=T)
                bim = ps[:, 6:8, :].rearrange("p b (j t) -> p (b j) t", t=T)
                ve.wait_ge(bu_done, i + 1)
                tt(prod[0], bre, er, ALU.mult)
                tt(prod[1], bim, ei, ALU.mult)
                tt(prod[2], bim, er, ALU.mult)
                tt(prod[3], bre, ei, ALU.mult).then_inc(bu_used, 1)
                ve.wait_ge(bu_used, i + 1)
                tt(state_re, prod[0], prod[1], ALU.add)
                tt(state_im, prod[2], prod[3], ALU.subtract).then_inc(w_rot, 1)
                ve.wait_ge(w_rot, i + 1)
                for a in range(4):
                    j = 4 * i + a
                    decay = par[:, MAG, j:j + 1].to_broadcast([P, T])
                    for s in (state_re, state_im):
                        ins = ve.tensor_tensor_scan(s[:, a, :], decay, s[:, a, :], 0.0, ALU.mult, ALU.add)
                ins.then_inc(scanned, 1)
                ve.wait_ge(scanned, 2 * i + 1)
                if i:
                    ve.wait_ge(x_state, i)
                tt(prod_out[0], state_re, er, ALU.mult)
                tt(prod_out[1], state_im, ei, ALU.mult)
                tt(prod_out[2], state_im, er, ALU.mult)
                tt(prod_out[3], state_re, ei, ALU.mult).then_inc(scanned, 1)

            ve.wait_ge(y_done, 4)
            for a in range(KS):
                i = ve.scalar_tensor_tensor(y_raw[:, a, :], u_in[:, a, :], vec[:, V_D + a:V_D + a + 1],
                                            ps[:, 2 + a // 2, (a % 2) * T:(a % 2) * T + T], ALU.mult, ALU.add)
            i.then_inc(y_raw_ok, 1)

            wi = ptok[:, :, C_WI - C_Q:C_WI - C_Q + IH]
            link(ve.tensor_scalar(wi, wi, IH ** -0.5 * ID ** -0.5, None, ALU.mult))
            r = 0
            for t in range(TT):
                w = P * (t + 1)
                per = 512 // w
                acc = score[:, t, 0:w]
                for n in range(4 * (t + 1)):
                    ve.wait_ge(rot_free, JOB[f"R{t}_{n}"] + 1)
                    for m in range(per):
                        h = n * per + m
                        s = relu[:, r % 2, m * w:m * w + w]
                        if n == 0 and m == 0:
                            ins = ve.tensor_scalar(acc, s, wi[:, t, h:h + 1], None, ALU.mult)
                        else:
                            ins = ve.scalar_tensor_tensor(acc, s, wi[:, t, h:h + 1], acc, ALU.mult, ALU.add)
                        if m == per - 1:
                            ins.then_inc(relu_used, 1)
                            ve.wait_ge(relu_used, r + 1)
                        else:
                            link(ins)
                    r += 1

            def choose_keys(t):
                w = P * (t + 1)
                link(tt(score[:, t, 0:w], score[:, t, 0:w], causal[:, t, 0:w], ALU.add))
                src = score[:, t, 0:w]
                dst = taken[:, t, 0:w]
                for n in range(NSEL // 8):
                    link(ve.max(stat[:, 24:32], src))
                    link(ve.match_replace(dst, stat[:, 24:32], src, GONE))
                    src = dst
                link(ve.tensor_scalar(dst, dst, GONE, -NEG, ALU.is_equal, ALU.mult))
                link(ve.tensor_scalar(dst, dst, NEG, None, ALU.add))
                link(tt(bias[:, t, 0:w], dst, causal[:, t, 0:w], ALU.min))

            def mask(t):
                w = P * (t + 1)
                ve.wait_ge(logit_done, t + 1)
                lg = ps[:, 4:8, :].rearrange("p b (h s) -> p (b h) s", s=T)[:, :, 0:w]
                if t:
                    ve.wait_ge(rot_done, JOB["P0_1"] + 1)
                link(ve.scalar_tensor_tensor(logit[:, :, 0:w], lg, HD ** -0.5,
                                             bias[:, t, 0:w].unsqueeze(1).to_broadcast([P, NH, w]),
                                             ALU.mult, ALU.add))
                ve.tensor_reduce(stat[:, 8:16], logit[:, :, 0:w], AX.X, ALU.max, negate=True).then_inc(row_max, 1)

            def probabilities(t):
                w = P * (t + 1)
                ve.wait_ge(expd, t + 1)
                link(ve.reciprocal(stat[:, 32:40], stat[:, 16:24]))
                tt(logit[:, :, 0:w], logit[:, :, 0:w],
                   stat[:, 32:40].unsqueeze(2).to_broadcast([P, NH, w]), ALU.mult).then_inc(prob_ok, 1)

            choose_keys(0)
            mask(0)
            choose_keys(1)
            probabilities(0)
            ve.wait_ge(rot_free, JOB["GLU1"] + 1)
            tt(y_ssm, y_gelu, glu_g, ALU.mult).then_inc(y_ssm_ok, 1)
            mask(1)
            probabilities(1)
            ve.wait_ge(rot_free, JOB["PS3"] + 1)
            link(tt(p_ssm, p_ssm, gate_s, ALU.mult))
            ve.wait_ge(att_done, 2)
            for n in range(4):
                ve.wait_ge(proj_done, n + 1)
                two = mixed[:, 2 * n:2 * n + 2, :]
                tt(two, ps[:, 4 + n, :].rearrange("p (k t) -> p k t", k=2), gate_a[:, 2 * n:2 * n + 2, :],
                   ALU.mult).then_inc(gated_a, 1)
                ve.wait_ge(gated_a, n + 1)
                tt(two, two, p_ssm[:, 2 * n:2 * n + 2, :], ALU.add).then_inc(mixed_ok, 1)
            for n in range(4):
                ve.wait_ge(wout_done, n + 1)
                part = x[:, :, 256 * n:256 * n + 256]
                tt(part, part, ps[:, 4 + n, :].rearrange("p (t c) -> p t c", t=TT), ALU.add).then_inc(x1_ok, 1)
            ve.wait_ge(sum_sq, 3)
            link(ve.tensor_reduce(stat[:, 0:2], stat[:, 48:56].rearrange("p (n t) -> p t n", t=TT), AX.X, ALU.add))
            rstd(1, rstd_ok)

            ve.wait_ge(rlogit, 2)
            ve.wait_ge(misc_in, 32)
            link(ve.tensor_reduce(rlog, ps[:, 3, 0:TT * P].rearrange("p (t c e) -> p t e c", t=TT, c=4), AX.X, ALU.add))
            link(tt(rlog, rlog, stat[:, 6:8].unsqueeze(2).to_broadcast([P, TT, NE]), ALU.mult))
            link(tt(rlog, rlog,
                    b_rout[:, :].unsqueeze(1).to_broadcast([P, TT, NE]), ALU.add))
            for t in range(TT):
                ins = ve.max(top8[:, t, :], rlog[:, t, :])
            link(ins)
            for t in range(TT):
                ins = ve.max_index(top8i[:, t, :], top8[:, t, :], rlog[:, t, :])
            link(ins)
            ve.tensor_copy(top8f, top8i).then_inc(v_chain, 1)
            chain[0] += 1
            tt(topw[:, :, 0:TOPE], top8[:, :, 0:TOPE], top8[:, :, 0:1].to_broadcast([P, TT, TOPE]),
               ALU.subtract).then_inc(top_ok, 1)
            ve.wait_ge(v_chain, chain[0])
            for t in range(TT):
                ins = tt(hot4[:, t], exp_no.unsqueeze(1).to_broadcast([P, TOPE, NE]),
                         top8f[:, t, 0:TOPE].unsqueeze(2).to_broadcast([P, TOPE, NE]), ALU.is_equal)
            link(ins)
            ve.tensor_reduce(picked, hot4.rearrange("p t k e -> p t e k"), AX.X, ALU.add).then_inc(picked_ok, 1)
            ve.wait_ge(placed, 1)
            ve.scalar_tensor_tensor(place, ps[:, 3, 0:TT * NE].rearrange("p (t e) -> p t e", t=TT), FAR,
                                    picked, ALU.add, ALU.mult).then_inc(place_ok, 1)

            def gate_weights():
                ve.wait_ge(top_exp, 1)
                link(ve.tensor_reduce(stat[:, 40:42], topw[:, :, 0:TOPE], AX.X, ALU.add))
                link(ve.reciprocal(stat[:, 42:44], stat[:, 40:42]))
                link(tt(topw[:, :, 0:TOPE], topw[:, :, 0:TOPE],
                        stat[:, 42:44].unsqueeze(2).to_broadcast([P, TT, TOPE]), ALU.mult))
                for t in range(TT):
                    ins = tt(hot4w[:, t], hot4[:, t], topw[:, t, 0:TOPE].unsqueeze(2).to_broadcast([P, TOPE, NE]),
                             ALU.mult)
                link(ins)
                for q in range(2):
                    ins = ve.tensor_reduce(gates_two[:, :, q, :], hot4w.rearrange("p t k e -> p t e k"), AX.X,
                                           ALU.add)
                ins.then_inc(route_ok, 1)

            def gates_out():
                ve.wait_ge(gates_tr, 1)
                link(ve.tensor_reduce(stat[0:1, 44:45], ps[0:1, 2, T:T + NE], AX.X, ALU.max))
                ve.tensor_copy(flag[:, :], stat[0:1, 44:45]).then_inc(flag_ok, 1)
                ve.tensor_copy(gates_t, ps[0:2 * NE, 2, 0:T]).then_inc(gates_t_ok, 1)

            def one_pass(c, first):
                if not isinstance(c, int):
                    ve.tensor_scalar(place, place, -float(SLOTS), None, ALU.add).then_inc(place_ok, 1)
                    ve.wait_ge(place_ok, c + 1)
                else:
                    ve.wait_ge(place_ok, 1)

                def column(v, e):
                    return v[:, :, bass.ds(e, 1)].to_broadcast([P, TT, SLOTS])

                slots = slot_no.unsqueeze(1).to_broadcast([P, TT, SLOTS])

                def choose(e):
                    tt(one_hot, slots, column(place, e), ALU.is_equal).then_inc(hot_ok, 1)

                def pick_bias(e):
                    ve.tensor_copy(chosen, ident.rearrange("p (n e) -> p n e", n=4)[:, :, bass.ds(e, 1)].to_broadcast(
                        [P, 4, SLOTS])).then_inc(chosen_ok, 1)

                def take(j):
                    ve.wait_ge(h_trans, j + 1)
                    tt(h_sel, ps[:, 3, :].rearrange("p (j q s) -> p j q s", q=2, s=SLOTS),
                       vec[:, V_G2:V_G2 + KD].rearrange("p (q j) -> p j q", q=2).unsqueeze(3).to_broadcast(
                           [P, 4, 2, SLOTS]), ALU.mult).then_inc(h_sel_ok, 1)

                def weigh(j, e):
                    for q in range(2):
                        ins = tt(gated[:, :, q], slots, column(place, e), ALU.is_equal)
                    ins.then_inc(gated_eq, 1)
                    ve.wait_ge(gated_eq, j + 1)
                    for q in range(2):
                        ins = tt(gated[:, :, q], gated[:, :, q], column(gates, e), ALU.mult)
                    ins.then_inc(gated_ok, 1)

                def body(j, e, tail=False):
                    if not tail:
                        choose(e + 1)
                    ve.wait_ge(chunk_used, j * NW + NW_IN)
                    z = ps[:, 0:2, :].rearrange("p b (c g) -> p g (b c)", g=2)
                    ve.tensor_scalar(gate_z, z[:, 0], LIMIT, None, ALU.min).then_inc(z_gate, 1)
                    ve.tensor_scalar(lin_z, z[:, 1], LIMIT, -LIMIT, ALU.min, ALU.max).then_inc(z_lin, 1)
                    ve.wait_ge(z_lin, j + 1)
                    ve.scalar_tensor_tensor(act, lin_z, 1.0, gate_z, ALU.add, ALU.mult).then_inc(z_prod, 1)
                    ve.wait_ge(z_prod, j + 1)
                    ve.wait_ge(sig_ok, j + 1)
                    tt(act, act, sig, ALU.mult).then_inc(act_ok, 1)
                    weigh(j, e)
                    if not tail:
                        pick_bias(e + 1)
                        take(j + 1)
                    ve.wait_ge(gated_trans, j + 1)
                    for q in range(2):
                        r = slice(64 * q, 64 * q + SLOTS)
                        ins = ve.tensor_copy(gated_t[r, q, :], ps[r, 1, 0:T])
                    ins.then_inc(gated_t_ok, 1)

                if isinstance(c, int):
                    ve.wait_ge(zeroed, 9)
                choose(0)
                pick_bias(0)
                if isinstance(c, int):
                    gate_weights()
                take(first)
                if isinstance(c, int):
                    gates_out()
                body(first, 0)
                with ve.Fori(1, NE - 1) as e:
                    body(e + first, e)
                body(first + NE - 1, NE - 1, tail=True)
                ve.wait_ge(first_sum_ok, c + 1)
                ve.tensor_copy(stat[:, 62:63], stat[:, 60:61])
            passes(ve, one_pass)
            ve.tensor_copy(stat[:, 63:64], stat[:, 60:61]).then_inc(tile_ok, 1)

            ve.wait_ge(gfin_in, 16)
            for n, bank_free in ((1, None), (0, (squared, 1)), (3, (sum_ok, 1)), (2, (squared, 3))):
                if bank_free:
                    ve.wait_ge(*bank_free)
                q = n % 2
                tt(final[:, n // 2, 512 * q:512 * q + 512], ps[:, 4 + n, :], gfin[:, 512 * q:512 * q + 512],
                   ALU.mult).then_inc(under_gains, 1)
            ve.wait_ge(sum_sq, 5)
            link(ve.tensor_reduce(stat[:, 0:2], stat[:, 48:52].rearrange("p (t n) -> p t n", t=TT), AX.X, ALU.add))
            rstd(2, rstd_ok)
            ve.wait_ge(under_gains, 4)
            ve.tensor_scalar(final[:, 0, :], final[:, 0, :], stat[:, 6:7], None, ALU.mult).then_inc(out_ready[0], 1)

        @block.tensor
        def _(pe):
            def job(name):
                n = JOB[name]
                if n >= 2:
                    pe.wait_ge(rot_free, n - 1)
                return rot[n % 2]

            def keep_busy(n, bank):
                for _ in range(n):
                    pe.matmul(ps[:, bank, 0:T], idle_w, idle_x, start=True, stop=True)

            idle_w, idle_x = b_t[0][:, 0, :], b_t[0][:, 0:2, :].rearrange("p j c -> p (j c)")
            pe.wait_ge(zeroed, 5)
            keep_busy(4, 3)
            pe.wait_ge(ident_in, 16)
            pe.wait_ge(vec_in, 16 * 8)
            pe.wait_ge(small_free, 1)
            pe.transpose(ps[:, 7, 0:72], vec_rows[:, :], ident[0:72, 0:72])
            pe.transpose(ps[:, 7, 128:128 + NCH], dt_rows[:, :], ident[0:NCH, 0:NCH]).then_inc(small_t, 1)
            def norm_t(name, n, src):
                b = job(name)
                for k in (2 * n, 2 * n + 1):
                    for t in range(TT):
                        i = pe.transpose(b[:, (k % 2) * T + t * P:(k % 2) * T + t * P + P],
                                         src[:, t, k * P:k * P + P], ident)
                i.then_inc(rot_done, 1)

            keep_busy(1, 3)
            pe.wait_ge(x_norm, TT)
            for n in range(4):
                norm_t(f"X{n}", n, xs)

            def feature_job(name, src, kt, first_m, slot):
                b = job(name)
                for m in range(2):
                    for k in range(kt):
                        i = pe.matmul(b[:, m * T:m * T + T], slot[:, k, (first_m + m) * P:(first_m + m + 1) * P],
                                      src[:, k, :], start=(k == 0), stop=(k == kt - 1))
                i.then_inc(rot_done, 1)

            chunk_arrived(pe, "U0")
            pe.wait_ge(rot_free, JOB["X3"] + 1)
            feature_job("U0", x_t, KD, 0, chunk_view("U0")[0])
            pe.wait_ge(bnat_in, 16 * 4)
            for n in range(2):
                for a in range(4):
                    i = pe.transpose(ps[:, 4 + n, a * P:a * P + P], b_nat[n][:, a, :], ident)
            i.then_inc(small_t, 1)
            pe.wait_ge(cnat_in, 16 * 16)
            pe.wait_ge(small_free, 2)
            for n in range(2):
                for a in range(4):
                    i = pe.transpose(ps[:, 6 + n, a * P:a * P + P], c_nat[n][:, a, :], ident)
            i.then_inc(small_t, 1)
            chunk_arrived(pe, "U1")
            feature_job("U1", x_t, KD, 0, chunk_view("U1")[0])
            pe.wait_ge(tables_in, 32)

            def bu(i):
                if i == 0:
                    pe.wait_ge(b_ready, 1)
                    pe.wait_ge(c_ready, 1)
                    pe.wait_ge(rot_free, JOB["U1"] + 1)
                else:
                    pe.wait_ge(bu_used, i)
                for n in range(2):
                    for a in range(4):
                        ins = pe.matmul(ps[:, 4 + 2 * n + a // 2, (a % 2) * T:(a % 2) * T + T],
                                        b_t[n][:, 4 * i + a, :], u_in[:, i, :], start=True, stop=True)
                ins.then_inc(bu_done, 1)

            def y_out(i):
                pe.wait_ge(x_state, i + 1)
                for n, v in enumerate((xs_re, xs_im)):
                    for a in range(4):
                        ins = pe.matmul(ps[32 * a:32 * a + 32, 2 + i // 2, (i % 2) * T:(i % 2) * T + T],
                                        c_t[n][:, i, 32 * a:32 * a + 32], v[:, a, :], start=(n == 0), stop=(n == 1))
                ins.then_inc(y_done, 1)

            def token_job(n):
                w = TOK[n][1]
                chunk_arrived(pe, f"T{n}")
                slot = chunk_view(f"T{n}")[0]
                b = job(f"T{n}")
                for t in range(TT):
                    for k in range(KD):
                        i = pe.matmul(b[:, t * w:t * w + w], x_t[:, k, t * P:t * P + P], slot[:, k, :],
                                      start=(k == 0), stop=(k == KD - 1))
                i.then_inc(rot_done, 1)

            def gate_job(letter, n):
                chunk_arrived(pe, f"{letter}{n}")
                feature_job(f"{letter}{n}", x_t, KD, 0, chunk_view(f"{letter}{n}")[0])

            for n in range(4):
                token_job(n)
            bu(0)
            token_job(4)
            token_job(5)
            bu(1)
            token_job(6)
            y_out(0)
            token_job(7)
            bu(2)
            gate_job("S", 0)
            y_out(1)
            bu(3)
            gate_job("S", 1)
            gate_job("S", 2)
            y_out(2)
            gate_job("S", 3)
            y_out(3)

            def trans_job(name, cols_of):
                b = job(name)
                for n, c in enumerate(cols_of):
                    for t in range(TT):
                        i = pe.transpose(b[:, n * T + t * P:n * T + t * P + P], c(t), ident)
                i.then_inc(rot_done, 1)

            pe.wait_ge(roped, 4)
            q0 = C_QI - C_Q
            for n in range(4):
                trans_job(f"QI{n}", [lambda t, k=k: ptok[:, t, q0 + k * P:q0 + k * P + P] for k in (2 * n, 2 * n + 1)])
            b = job("KK")
            for t in range(TT):
                pe.transpose(b[:, t * P:t * P + P],
                             ki_two[:, t].rearrange("p n d -> p (n d)"), ident)
            for t in range(TT):
                i = pe.transpose(b[:, T + t * P:T + t * P + P], ptok[:, t, C_K - C_Q:C_K - C_Q + P], ident)
            i.then_inc(rot_done, 1)
            for n in range(2):
                trans_job(f"Q{n}", [lambda t, k=k: ptok[:, t, k * P:k * P + P] for k in (2 * n, 2 * n + 1)])

            pe.wait_ge(rot_free, JOB["KK"] + 1)
            for t in range(TT):
                w = P * (t + 1)
                per = 512 // w
                for n in range(4 * (t + 1)):
                    b = job(f"R{t}_{n}")
                    for m in range(per // 2):
                        i = pe.matmul(b[:, 2 * m * w:2 * m * w + 2 * w], qi_t[:, n * per // 2 + m, t * P:t * P + P],
                                      ki_t[:, :, 0:w], start=True, stop=True)
                    i.then_inc(rot_done, 1)

            pe.wait_ge(rot_free, JOB["Q1"] + 1)

            def logits(t):
                w = P * (t + 1)
                if t:
                    pe.wait_ge(row_max, t)
                for h in range(NH // 2):
                    i = pe.matmul(ps[:, 4 + h, :].rearrange("p (n s) -> p n s", n=2)[:, :, 0:w],
                                  q_t[:, h, t * P:t * P + P], k_t[:, :, 0:w], start=True, stop=True)
                i.then_inc(logit_done, 1)

            def attend(t):
                pe.wait_ge(prob_ok, t + 1)
                for n in range(2 * (t + 1)):
                    b = job(f"P{t}_{n}")
                    for m in range(4):
                        at = 4 * n + m
                        h, s = at // (t + 1), at % (t + 1)
                        i = pe.transpose(b[:, m * P:m * P + P], logit[:, h, s * P:s * P + P], ident)
                    i.then_inc(rot_done, 1)
                pe.wait_ge(rot_free, JOB[f"P{t}_{2 * t + 1}"] + 1)
                for h in range(NH):
                    for s in range(t + 1):
                        at = (2 * (h % 4) + h // 4) * (t + 1) + s
                        base = 64 * (h % 2)
                        i = pe.matmul(ps[base:base + 64, 2 + t, (h // 2) * P:(h // 2) * P + P],
                                      ptok[:, s, v0 + 64 * (h // 4):v0 + 64 * (h // 4) + 64],
                                      prob_t[:, at * P:at * P + P], start=(s == 0), stop=(s == t))
                i.then_inc(att_done, 1)

            v0 = C_V - C_Q
            logits(0)
            gate_job("A", 0)
            chunk_arrived(pe, "GLU")
            pe.wait_ge(gelu_ok, 1)
            for n in range(2):
                feature_job(f"GLU{n}", y_gelu, KS, 2 * n, chunk_view("GLU")[0])
            gate_job("A", 1)
            logits(1)
            attend(0)
            gate_job("A", 2)
            gate_job("A", 3)
            pe.wait_ge(y_ssm_ok, 1)
            for n in range(4):
                if n % 2 == 0:
                    chunk_arrived(pe, f"PS{n // 2}")
                feature_job(f"PS{n}", y_ssm, KS, 2 * (n % 2), chunk_view(f"PS{n // 2}")[0])
            attend(1)
            pe.wait_ge(att_out, 2)
            pe.wait_ge(row_max, 2)
            for n in range(4):
                if n % 2 == 0:
                    chunk_arrived(pe, f"PA{n // 2}")
                slot = chunk_view(f"PA{n // 2}")[0]
                for m in range(2):
                    for k in range(KS):
                        at = (2 * (n % 2) + m) * P
                        i = pe.matmul(ps[:, 4 + n, m * T:m * T + T], slot[:, k, at:at + P], y_att[:, k, :],
                                      start=(k == 0), stop=(k == KS - 1))
                i.then_inc(proj_done, 1)
            pe.wait_ge(mixed_ok, 4)
            for n in range(4):
                chunk_arrived(pe, f"W{n}")
                slot = chunk_view(f"W{n}")[0]
                for t in range(TT):
                    for k in range(KD):
                        i = pe.matmul(ps[:, 4 + n, t * T:t * T + 256], mixed[:, k, t * P:t * P + P], slot[:, k, :],
                                      start=(k == 0), stop=(k == KD - 1))
                i.then_inc(wout_done, 1)
                if n:
                    pe.wait_ge(x1_ok, n)
                    norm_t(f"HX{n - 1}", n - 1, x)
            pe.wait_ge(x1_ok, 4)
            norm_t("HX3", 3, x)

            for k in range(KD):
                c = k % 4
                if k == 0:
                    pe.wait_ge(rot_free, JOB["HX2"] + 1)
                    pe.wait_ge(misc_in, 32)
                if k == 6:
                    pe.wait_ge(rot_free, JOB["HX3"] + 1)
                i = pe.matmul(ps[32 * c:32 * c + 32, 2, 0:T], w_rout[:, k, :], x_t[:, k, :],
                              start=(k < 4), stop=(k >= 4))
            i.then_inc(rlogit, 1)
            pe.wait_ge(rlogit_sb, 1)
            for t in range(TT):
                i = pe.transpose(ps[:, 3, t * P:t * P + P], rsum[:, t * P:t * P + P], ident)
            i.then_inc(rlogit, 1)
            for n in range(2 * TT):
                i = pe.matmul(ps[:, 4 + n, :], ident, x[:, n // 2, 512 * (n % 2):512 * (n % 2) + 512], start=True,
                              stop=False, skip_group_check=True)
            i.then_inc(sum_open, 1)
            pe.wait_ge(picked_ok, 1)
            pe.matmul(ps[:, 3, 0:TT * NE], tri, picked[:, :, :].rearrange("p t e -> p (t e)"), start=True, stop=False)
            pe.matmul(ps[:, 3, NE:2 * NE], ones, picked[:, 0, :], start=False, stop=True).then_inc(placed, 1)

            def gates_turned():
                pe.wait_ge(route_ok, 1)
                for t in range(TT):
                    pe.transpose(ps[0:2 * NE, 2, t * P:t * P + P], gates_two[:, t].rearrange("p q e -> p (q e)"), ident)
                pe.matmul(ps[:, 2, T:T + NE], ones, picked[:, 0, :], start=True, stop=False)
                pe.matmul(ps[:, 2, T:T + NE], ones, picked[:, 1, :], start=False, stop=True).then_inc(gates_tr, 1)

            def one_pass(c, first):
                def gather(j):
                    pe.wait_ge(hot_ok, j + 1)
                    for t in range(TT):
                        for q in range(2):
                            i = pe.matmul(ps[64 * q:64 * q + SLOTS, 3, :], one_hot[:, t, :],
                                          xs[:, t, 512 * q:512 * q + 512], start=(t == 0), stop=(t == TT - 1))
                    i.then_inc(gathered, 1)

                def gather_t(j):
                    pe.wait_ge(h_tok_ok, j + 1)
                    for n in range(4):
                        i = pe.transpose(ps[:, 3, n * P:n * P + P], h_tok[:, n * P:n * P + P], ident)
                    i.then_inc(h_trans, 1)

                def scatter(j, done=None):
                    pe.wait_ge(y_tok_ok, j + 1)
                    for t in range(TT):
                        for q in range(2):
                            i = pe.matmul(ps[:, 4 + 2 * t + q, :], gated_t[:, q, t * P:t * P + P], y_tok,
                                          start=False, stop=False, skip_group_check=True)
                        if done is not None and t == 0:
                            i.then_inc(done, 1)

                def body(j, pair, odd, head=False, tail=False):
                    def weights(k):
                        if k >= NX:
                            pe.wait_ge(moe_in[k], 16 * j + 16)
                        elif odd:
                            pe.wait_ge(extra_in[k], 16 * pair + 16)
                        else:
                            pe.wait_ge(moe_in[k], 16 * pair + 16)
                        return extra[k] if odd and k < NX else ring[:, k * SW:(k + 1) * SW]

                    pe.wait_ge(h_sel_ok, j + 1)
                    if not head:
                        pe.wait_ge(gated_t_ok, j)
                    for k in range(KD):
                        w = weights(k)
                        for n in range(4):
                            r = slice(64 * (n % 2), 64 * (n % 2) + SLOTS)
                            i = pe.matmul(ps[r, n // 2, :], h_sel[:, k % 4, k // 4, :], w[:, 512 * n:512 * n + 512],
                                          start=(k == 0), stop=(k == KD - 1))
                        i.then_inc(chunk_used, 1)
                        if k == 0:
                            if head and isinstance(c, int):
                                pe.wait_ge(b_in_in, 16 * 4)
                            pe.wait_ge(chosen_ok, j + 1)
                            for n in range(4):
                                r = slice(64 * (n % 2), 64 * (n % 2) + SLOTS)
                                pe.matmul(ps[r, n // 2, :], chosen[:, n, :], b_in, start=False, stop=False)
                        if tail and isinstance(c, int) and k < 2 * TT:
                            if k == 0:
                                pe.wait_ge(gates_t_ok, 1)
                                pe.wait_ge(b_out_in, 16 * 2)
                            t, q = k // 2, k % 2
                            r = slice(NE * q, NE * q + NE)
                            pe.matmul(ps[:, 4 + k, :], gates_t[r, t * P:t * P + P], b_out[r, :], start=False,
                                      stop=False, skip_group_check=True)
                    if not head:
                        scatter(j - 1)
                    if not tail:
                        gather(j + 1)
                    pe.wait_ge(act_ok, j + 1)
                    for n in range(4):
                        i = pe.transpose(ps[:, 0, n * P:n * P + P], act[:, n * P:n * P + P], ident)
                    i.then_inc(act_trans, 1)
                    pe.wait_ge(gated_ok, j + 1)
                    for t in range(TT):
                        i = pe.transpose(ps[:, 1, t * P:t * P + P], gated[:, t].rearrange("p q s -> p (q s)"), ident)
                    i.then_inc(gated_trans, 1)
                    if not tail:
                        gather_t(j + 1)
                    pe.wait_ge(act_t_ok, j + 1)
                    for k in range(KF):
                        c_ = NW_IN + k // 2
                        if k % 2 == 0:
                            two = weights(c_)
                        w = two[:, (k % 2) * D:(k % 2) * D + D]
                        for q in range(2):
                            i = pe.matmul(ps[64 * q:64 * q + SLOTS, 2, :], act_tile(k), w[:, 512 * q:512 * q + 512],
                                          start=(k == 0), stop=(k == KF - 1))
                        if k % 2:
                            i.then_inc(chunk_used, 1)

                if isinstance(c, int):
                    pe.wait_ge(x_norm, 2 * TT)
                gather(first)
                gather_t(first)
                if isinstance(c, int):
                    gates_turned()
                    pe.wait_ge(zeroed, 9)
                pairs = c * (NE // 2)
                body(first, pairs, 0, head=True)
                body(first + 1, pairs, 1)
                with pe.Fori(1, NE // 2 - 1) as m:
                    for odd in range(2):
                        body(2 * m + (first + odd), m + pairs, odd)
                body(first + NE - 2, pairs + NE // 2 - 1, 0)
                body(first + NE - 1, pairs + NE // 2 - 1, 1, tail=True)
                pe.wait_ge(gated_t_ok, first + NE)
                scatter(first + NE - 1, first_sum_ok)
            passes(pe, one_pass)
            pe.matmul(ps[0:1, 3, 0:1], ones[0:1, 0:1], ones[0:1, 0:1], start=True, stop=True).then_inc(sum_ok, 1)


_INS = ["x", "norm1_g", "w_in", "b_gate", "ssm_lam_re", "ssm_lam_im", "ssm_log_dt", "ssm_b_re", "ssm_b_im",
        "ssm_c_re", "ssm_c_im", "ssm_d", "w_glu", "b_glu", "w_proj_ssm", "w_proj_attn", "w_out", "norm2_g",
        "w_router", "b_router", "w_moe_in", "b_moe_in", "w_moe_out", "b_moe_out", "norm_f_g"]
_FLAT = {"norm1_g", "b_gate", "ssm_lam_re", "ssm_lam_im", "ssm_log_dt", "ssm_d", "b_glu", "norm2_g", "b_router",
         "norm_f_g"}


def kernel(**inputs):
    import concourse.bacc as _bacc
    from concourse.bass_utils import run_bass_kernel_spmd as _run

    nc = _bacc.Bacc("TRN2", target_bir_lowering=False, num_devices=1)
    arrays, io = {}, {}
    for name in _INS + ["tables"]:
        if name == "tables":
            a = constant_tables()
        else:
            a = np.ascontiguousarray(inputs[name])
            if name in _FLAT:
                a = a.reshape(-1)
            elif name != "norm_f_g":
                a = a.reshape(a.shape[1:])
        arrays[f"in_{name}"] = a
        io[name] = nc.dram_tensor(f"in_{name}", a.shape, mybir.dt.from_np(a.dtype), kind="ExternalInput").ap()
    out = nc.dram_tensor("out_0", (T, D), mybir.dt.float32, kind="ExternalOutput").ap()
    build(nc, io, out)
    r = _run(nc, [arrays], core_ids=[0])
    return r.results[0]["out_0"].reshape(1, T, D)
```
